# Optimizing a Trainium2 kernel written in Bass

```python
import jax, jax.numpy as jnp
from jax import lax
import numpy as np

D_MODEL = 1024
BATCH = 1
SEQ = 512
DEPTH = 2

D_MIX = 2 * D_MODEL
D_CONV = D_MIX // 2
CONV_GROUPS = 16
SHORT_CONV = 3
D_SSM = D_MIX - D_CONV
SSM_HEADDIM = 64
SSM_HEADS = D_SSM // SSM_HEADDIM
SSM_GROUPS = 2
SSM_STATE = 128
SSM_CONV = 4
SSM_CHUNK = 128
D_XBC = D_SSM + 2 * SSM_GROUPS * SSM_STATE
D_IN = 3 * D_CONV + D_SSM + D_XBC + SSM_HEADS
SPLITS = [D_CONV, 2 * D_CONV, 3 * D_CONV, 3 * D_CONV + D_SSM, 3 * D_CONV + D_SSM + D_XBC]
PEER_HEADS = 8
PEER_KEYS = 128
PEER_EXPERTS = PEER_KEYS * PEER_KEYS
PEER_TOPK = 16
PEER_DHALF = 128
PEER_BLOCK = 128
PLE_DIM = 256
EPS = 1e-6

kernel_name = "hymba_conv_ssd_peer_trunk"

def rmsnorm(x, w):
    xf = x.astype(jnp.float32)
    y = xf * lax.rsqrt(jnp.mean(xf * xf, axis=-1, keepdims=True) + EPS)
    return (y * w.astype(jnp.float32)).astype(x.dtype)

def causal_dwconv(x, w):
    k = w.shape[0]
    return lax.conv_general_dilated(
        x, w[:, None, :].astype(x.dtype), window_strides=(1,), padding=[(k - 1, 0)],
        dimension_numbers=("NWC", "WIO", "NWC"), feature_group_count=x.shape[-1])

def ssd_scan(x, dt, A, Bm, Cm, D):
    b, s, h, pdim = x.shape
    g, n = Bm.shape[2], Bm.shape[3]
    hg = h // g
    c, l = s // SSM_CHUNK, SSM_CHUNK
    f32 = jnp.float32
    xf = x.astype(f32).reshape(b, c, l, g, hg, pdim)
    dtf = dt.astype(f32).reshape(b, c, l, g, hg)
    Bf = Bm.astype(f32).reshape(b, c, l, g, n)
    Cf = Cm.astype(f32).reshape(b, c, l, g, n)
    xdt = xf * dtf[..., None]
    a = (dtf * A.astype(f32).reshape(g, hg)).transpose(0, 3, 4, 1, 2)
    a_cum = jnp.cumsum(a, axis=-1)
    causal = jnp.tril(jnp.ones((l, l), dtype=bool))
    L = jnp.exp(jnp.where(causal, a_cum[..., :, None] - a_cum[..., None, :], -jnp.inf))
    cb = jnp.einsum('bclgn,bcsgn->bgcls', Cf, Bf)
    y_diag = jnp.einsum('bghcls,bcsghp->bclghp', cb[:, :, None] * L, xdt)
    decay_in = jnp.exp(a_cum[..., -1:] - a_cum).transpose(0, 3, 4, 1, 2)
    states = jnp.einsum('bclgn,bclghp->bcghpn', Bf, xdt * decay_in[..., None])
    chunk_decay = jnp.exp(a_cum[..., -1]).transpose(3, 0, 1, 2)

    def step(carry, inp):
        st, dec = inp
        return carry * dec[..., None, None] + st, carry

    _, s_in = lax.scan(step, jnp.zeros_like(states[:, 0]),
                       (states.transpose(1, 0, 2, 3, 4, 5), chunk_decay))
    s_in = s_in.transpose(1, 0, 2, 3, 4, 5)
    decay_out = jnp.exp(a_cum).transpose(0, 3, 4, 1, 2)
    y_off = jnp.einsum('bclgn,bcghpn->bclghp', Cf, s_in) * decay_out[..., None]
    y = y_diag + y_off + xf * D.astype(f32).reshape(g, hg)[..., None]
    return y.reshape(b, s, h * pdim).astype(x.dtype)

def hybrid_mixer(xn, w_in, conv_w, mconv_w, mconv_b, dt_bias, a_log, d_skip,
                 conv_norm_w, ssd_norm_w, w_out):
    b, s, _ = xn.shape
    proj = xn @ w_in
    gb, gc, hc, z, xbc, dt = jnp.split(proj, SPLITS, axis=-1)
    y_conv = rmsnorm(gb * causal_dwconv(gc * hc, conv_w), conv_norm_w)
    xbc = jax.nn.silu(causal_dwconv(xbc, mconv_w) + mconv_b)
    xs, Bm, Cm = jnp.split(xbc, [D_SSM, D_SSM + SSM_GROUPS * SSM_STATE], axis=-1)
    dt = jax.nn.softplus(dt.astype(jnp.float32) + dt_bias.astype(jnp.float32))
    A = -jnp.exp(a_log.astype(jnp.float32))
    y_ssd = ssd_scan(xs.reshape(b, s, SSM_HEADS, SSM_HEADDIM), dt, A,
                     Bm.reshape(b, s, SSM_GROUPS, SSM_STATE),
                     Cm.reshape(b, s, SSM_GROUPS, SSM_STATE), d_skip)
    y_ssd = rmsnorm(y_ssd * jax.nn.silu(z), ssd_norm_w)
    return jnp.concatenate([y_conv, y_ssd], axis=-1) @ w_out

def peer_ffn(xn, wq, keys, u, v):
    b, s, d = xn.shape
    xt = xn.reshape(-1, PEER_BLOCK, d)
    keys_f = keys.astype(jnp.float32)

    def block(xb):
        t = xb.shape[0]
        q = (xb @ wq).reshape(t, PEER_HEADS, 2, PEER_DHALF).astype(jnp.float32)
        sc = jnp.einsum('thkd,hknd->thkn', q, keys_f)
        sv, si = lax.top_k(sc, PEER_TOPK)
        cand = (sv[:, :, 0, :, None] + sv[:, :, 1, None, :]).reshape(t, PEER_HEADS, PEER_TOPK * PEER_TOPK)
        tv, ti = lax.top_k(cand, PEER_TOPK)
        i1 = jnp.take_along_axis(si[:, :, 0], ti // PEER_TOPK, axis=-1)
        i2 = jnp.take_along_axis(si[:, :, 1], ti % PEER_TOPK, axis=-1)
        eidx = (i1 * PEER_KEYS + i2).reshape(t, PEER_HEADS * PEER_TOPK)
        gate = jax.nn.softmax(tv, axis=-1).reshape(t, PEER_HEADS * PEER_TOPK)
        ue = jnp.take(u, eidx, axis=0)
        ve = jnp.take(v, eidx, axis=0)
        act = jax.nn.gelu(jnp.einsum('tkd,td->tk', ue, xb))
        return jnp.einsum('tk,tkd->td', (gate * act).astype(xb.dtype), ve)

    return lax.map(block, xt).reshape(b, s, d)

def setup_inputs(seed: int = 0) -> dict:
    key = jax.random.key(seed)
    ks = jax.random.split(key, 24)
    f32 = jnp.float32
    nrm = lambda k, shape, scale: (jax.random.normal(k, shape, f32) * scale).astype(f32)
    gain = lambda k, shape: 1.0 + 0.05 * jax.random.normal(k, shape, f32)
    dt0 = jnp.exp(jax.random.uniform(ks[7], (DEPTH, SSM_HEADS), f32) * (jnp.log(0.1) - jnp.log(0.001)) + jnp.log(0.001))
    return {
        "x": nrm(ks[0], (BATCH, SEQ, D_MODEL), 1.0),
        "p": nrm(ks[1], (DEPTH, BATCH, SEQ, PLE_DIM), 1.0),
        "norm_mix_w": gain(ks[2], (DEPTH, D_MODEL)),
        "w_in": nrm(ks[3], (DEPTH, D_MODEL, D_IN), D_MODEL ** -0.5),
        "conv_w": nrm(ks[4], (DEPTH, SHORT_CONV, D_CONV), SHORT_CONV ** -0.5),
        "mconv_w": nrm(ks[5], (DEPTH, SSM_CONV, D_XBC), SSM_CONV ** -0.5),
        "mconv_b": nrm(ks[6], (DEPTH, D_XBC), 0.01),
        "dt_bias": dt0 + jnp.log(-jnp.expm1(-dt0)),
        "a_log": jnp.log(jax.random.uniform(ks[8], (DEPTH, SSM_HEADS), f32, 1.0, 16.0)),
        "d_skip": gain(ks[9], (DEPTH, SSM_HEADS)),
        "conv_norm_w": gain(ks[10], (DEPTH, D_CONV)),
        "ssd_norm_w": gain(ks[11], (DEPTH, D_SSM)),
        "w_out": nrm(ks[12], (DEPTH, D_MIX, D_MODEL), D_MIX ** -0.5),
        "norm_ffn_w": gain(ks[13], (DEPTH, D_MODEL)),
        "peer_wq": nrm(ks[14], (DEPTH, D_MODEL, PEER_HEADS * 2 * PEER_DHALF), D_MODEL ** -0.5),
        "peer_keys": nrm(ks[15], (DEPTH, PEER_HEADS, 2, PEER_KEYS, PEER_DHALF), PEER_DHALF ** -0.5),
        "peer_u": nrm(ks[16], (DEPTH, PEER_EXPERTS, D_MODEL), D_MODEL ** -0.5),
        "peer_v": nrm(ks[17], (DEPTH, PEER_EXPERTS, D_MODEL), PEER_HEADS ** -0.5),
        "norm_ple_w": gain(ks[18], (DEPTH, D_MODEL)),
        "w_ple_gate": nrm(ks[19], (DEPTH, D_MODEL, D_MODEL), D_MODEL ** -0.5),
        "w_ple": nrm(ks[20], (DEPTH, PLE_DIM, D_MODEL), PLE_DIM ** -0.5),
        "final_norm_w": gain(ks[21], (D_MODEL,)),
    }

def reference(x, p, norm_mix_w, w_in, conv_w, mconv_w, mconv_b, dt_bias, a_log, d_skip,
              conv_norm_w, ssd_norm_w, w_out, norm_ffn_w, peer_wq, peer_keys, peer_u, peer_v,
              norm_ple_w, w_ple_gate, w_ple, final_norm_w):
    h = x
    for i in range(DEPTH):
        h = h + hybrid_mixer(rmsnorm(h, norm_mix_w[i]), w_in[i], conv_w[i], mconv_w[i], mconv_b[i],
                             dt_bias[i], a_log[i], d_skip[i], conv_norm_w[i], ssd_norm_w[i], w_out[i])
        h = h + peer_ffn(rmsnorm(h, norm_ffn_w[i]), peer_wq[i], peer_keys[i], peer_u[i], peer_v[i])
        gate = jax.nn.sigmoid(rmsnorm(h, norm_ple_w[i]) @ w_ple_gate[i])
        h = h + gate * (p[i] @ w_ple[i])
    return rmsnorm(h, final_norm_w)


_drawn_inputs = setup_inputs


def setup_inputs(seed=0):
    import zlib

    import numpy as np

    out = dict(_drawn_inputs(seed))
    spreads = {}
    factors = {'mconv_b': 2.74, 'norm_ple_w': 4.253}
    for name, (base, spread) in spreads.items():
        noise = np.random.default_rng([zlib.crc32(name.encode()), seed]).standard_normal(out[name].shape)
        drawn = base * np.exp(spread * noise) if base else spread * noise
        out[name] = __import__('jax').numpy.asarray(drawn.astype(out[name].dtype))
    for name, factor in factors.items():
        out[name] = (out[name] * factor).astype(out[name].dtype)
    return out
```

```python
from contextlib import ExitStack

import concourse.bass as bass
from concourse import mybir

F32 = mybir.dt.float32
I32 = mybir.dt.int32
U32 = mybir.dt.uint32
ALU = mybir.AluOpType
ACT = mybir.ActivationFunctionType
AX = mybir.AxisListType

P = 128
EPS = 1e-6
NEG = -3.0e38
GELU_C = 0.7978845608028654
GELU_A = 0.044715
VEC_PER_TURN = 392
VEC_PER_LAYER = 4
SCA_PER_TURN = 8


class Signal:

    def __init__(self, sem, per_turn, head=0):
        self.sem, self.per_turn, self.head = sem, per_turn, head

    def at(self, turn, n):
        return turn * self.per_turn + (n + self.head)


class Steps:

    def __init__(self, per_turn, per_layer, turn, layer, start):
        self.n, self.per_turn, self.per_layer, self.turn, self.layer = start, per_turn, per_layer, turn, layer

    def one(self):
        self.n += 1
        return 1

    def so_far(self):
        return self.turn * self.per_turn + self.layer * self.per_layer + self.n


def over(ap, axis, n):
    a = ap.unsqueeze(axis)
    shape = list(a.shape)
    shape[axis] = n
    return a.to_broadcast(shape)


def trunk(nc, x, p, norm_mix_w, w_in, conv_w, mconv_w, mconv_b, dt_bias, a_log, d_skip, conv_norm_w,
          ssd_norm_w, w_out, norm_ffn_w, peer_wq, peer_keys, peer_u, peer_v, norm_ple_w, w_ple_gate,
          w_ple, final_norm_w, out):
    D = x.shape[2]
    SEQ = x.shape[1]
    DEPTH = p.shape[0]
    KT = D // P
    NBLK = SEQ // P
    HB = 2
    HALVES = NBLK // HB
    T = HB * P
    D_IN = w_in.shape[2]
    HEADS = dt_bias.shape[1]
    HD = D // HEADS
    HG = HEADS // 2
    CONV_K, MCONV_K = conv_w.shape[1], mconv_w.shape[1]
    XT = mconv_b.shape[1] // P
    PH, KEYS, EXPERTS = peer_keys.shape[1], peer_keys.shape[3], peer_u.shape[1]
    TOPK = 16
    J = 2 * PH
    SLOTS = PH * TOPK
    PLE = p.shape[3]
    PT = PLE // P
    NW = 512
    TPU = NW // P

    IN_COLS = [D, D + NW, 2 * D, 2 * D + NW, 0, NW, 3 * D, 3 * D + NW] + [4 * D + NW * i for i in range(XT // TPU)]
    U_IN = 0
    U_OUT = len(IN_COLS)
    U_Q = U_OUT + 4
    U_PLE = U_Q + 4
    UNITS = U_PLE + 4
    EVEN = (UNITS + 1) // 2
    ODD = UNITS // 2

    R_CONV = 0
    R_MCONV = R_CONV + CONV_K * KT
    R_MB = R_MCONV + MCONV_K * XT
    R_CN = R_MB + XT
    R_SN = R_CN + KT
    ROWS = R_SN + KT

    SMALL = 16 * 9

    RING = 8
    SUMS = 448
    BODY = 2 * RING

    with ExitStack() as c:
        def sb(name, shape, dt=F32):
            return c.enter_context(nc.sbuf_tensor(name, shape, dt))

        def ps(name, shape):
            return c.enter_context(nc.psum_tensor(name, shape, F32))

        def sem(name):
            return c.enter_context(nc.semaphore(name))

        h = sb("h", [P, NBLK, D])
        wbuf = sb("wbuf", [P, 2, KT, NW])
        wdt = sb("wdt", [P, KT, HEADS])
        xn = sb("xn", [P, HB, D])
        xnT = sb("xnT", [P, KT, T])
        conv_in = sb("conv_in", [P, KT, CONV_K - 1 + T])
        xbc_in = sb("xbc_in", [P, XT, MCONV_K - 1 + T])
        gain = sb("gain", [P, D])
        params = sb("params", [P, P])
        paramsT = sb("paramsT", [P, P])
        dskip = sb("dskip", [P, KT])
        etmp = sb("etmp", [P, TPU, T])
        state = sb("state", [P, HEADS, HD])
        ring = sb("ring", [P, RING, D])
        junk = sb("junk", [P, 2, D])
        arena = sb("arena", [P, 12 * D])

        def region(k0, shape):
            n = 1
            for s in shape:
                n *= s
            flat = arena[:, k0 * D:k0 * D + n]
            if len(shape) == 1:
                return flat
            names = "abc"[:len(shape)]
            sizes = {names[i]: shape[i] for i in range(1, len(shape))}
            return flat.rearrange(f"p ({' '.join(names)}) -> p {' '.join(names)}", **sizes)

        yc = region(0, [KT, T])
        zs = region(2, [KT, T])
        ys = region(4, [KT, T])
        xc = region(6, [XT, T])
        decay = region(9, [HG, P])
        c_dec = region(10, [HG, P])
        xdt = region(11, [HG, HD])
        xdtd = arena[:, 11 * D + NW:12 * D].rearrange("p (a b) -> p a b", b=HD)
        qT = region(0, [J, T])
        cand = region(0, [PH * TOPK, TOPK]).rearrange("p (h a) b -> p h a b", a=TOPK)
        keys = region(4, [J, P])
        keysT = region(6, [J, P])
        sc = region(8, [J, KEYS])
        sc2 = region(10, [J, KEYS])
        cand2 = region(4, [PH, TOPK * TOPK])
        hot = region(10, [SLOTS, TOPK])

        ident = sb("ident", [P, P])
        causalT = sb("causalT", [P, P])
        ones = sb("ones", [P, P])
        iota_i = sb("iota_i", [P, TOPK], I32)
        iota_f = sb("iota_f", [P, TOPK])
        expert0 = sb("expert0", [P, 1])
        ss = sb("ss", [P, HB])
        rstd = sb("rstd", [P, HB])
        ss2 = sb("ss2", [P, HB, 2])
        sums = sb("sums", [P, 3 * HB])
        fin = sb("fin", [P, 2, NBLK])
        rstd2 = sb("rstd2", [P, HB, 2])
        dall = sb("dall", [P, HEADS])
        dtb = sb("dtb", [P, HEADS])
        alog = sb("alog", [P, HEADS])
        expa = sb("expa", [P, HEADS])
        dts = sb("dts", [P, 6, HB, HEADS])
        dt = sb("dt", [P, HB, HEADS])
        a_ = sb("a_", [P, HB, HEADS])
        acum = sb("acum", [P, HB, 2, HEADS])
        d_in = sb("d_in", [P, HB, HEADS])
        d_chunk = sb("d_chunk", [P, HB, HEADS])
        cbm = sb("cbm", [P, P])
        b_tok = sb("b_tok", [P, P])
        sv = sb("sv", [P, J, TOPK])
        si = sb("si", [P, J, TOPK], U32)
        sif = sb("sif", [P, J, TOPK])
        tv = sb("tv", [P, PH, TOPK])
        ti = sb("ti", [P, PH, TOPK], U32)
        tq = sb("tq", [P, 2, SLOTS], U32)
        tqf = sb("tqf", [P, 2, SLOTS])
        ei = sb("ei", [P, 2, SLOTS])
        eidx = sb("eidx", [P, SLOTS])
        idx_u = sb("idx_u", [P, HB, SLOTS], I32)
        idx_v = sb("idx_v", [P, HB, P], I32)
        stage = sb("stage", [P, 2, RING], I32)
        gsum = sb("gsum", [P, PH])
        gate = sb("gate", [P, HB, SLOTS])
        act = sb("act", [P, HB, SLOTS])
        gl = sb("gl", [P, HB, SLOTS])
        wT = sb("wT", [P, HB, P])
        ptok = sb("ptok", [P, HB, PLE])
        pT = region(0, [HB * PT, P])

        pp = ps("pp", [P, 2, 2, NW])
        px = ps("px", [P, NW])
        pm = ps("pm", [P, NW])
        pv = ps("pv", [P, KT, P])
        ppt = pp[:, :, :, :].rearrange("p a b (c t) -> p a (b c) t", t=T)
        ppf = pp[:, :, :, :].rearrange("p a b n -> p (a b n)")
        pxt = px[:, :].rearrange("p (a b) -> p a b", b=P)

        s_const = sem("s_const")
        s_hload = sem("s_hload")
        s_w = [sem("s_w_even"), sem("s_w_odd")]
        small = Signal(sem("s_small"), SMALL)
        gains = Signal(sem("s_gain"), 16 * 3)
        keys_in = Signal(sem("s_keys"), 16)
        p_in = Signal(sem("s_p"), 16)
        sumsq = Signal(sem("s_sumsq"), 3)
        meansq = Signal(sem("s_meansq"), 3)
        rstds = Signal(sem("s_rstd"), 3)
        xns = Signal(sem("s_xn"), 6)
        tr_done = Signal(sem("s_transposed"), 6)
        xnT_done = Signal(sem("s_xnT"), 6)
        par_T = Signal(sem("s_params_transposed"), 1)
        par_done = Signal(sem("s_params"), 1)
        proj = Signal(sem("s_proj"), UNITS, 1)
        hc_done = Signal(sem("s_hc"), 2)
        out_used = Signal(sem("s_out_used"), 4)
        expa_done = Signal(sem("s_expa"), 1)
        gc_in = Signal(sem("s_gc"), 2)
        z_exp = Signal(sem("s_z_exp"), 2)
        z_done = Signal(sem("s_z_done"), 2)
        xbc_cp = Signal(sem("s_xbc_copied"), XT // TPU)
        conv_done = Signal(sem("s_xbc_conv"), XT // TPU)
        silu_exp = Signal(sem("s_silu_exp"), XT // TPU)
        silu_done = Signal(sem("s_silu_done"), XT // TPU)
        yc_done = Signal(sem("s_yc"), 2)
        sq_done = Signal(sem("s_square"), 4)
        sq_used = Signal(sem("s_square_used"), 4)
        y_scaled = Signal(sem("s_y_scaled"), 2)
        dt_proj = Signal(sem("s_dt_proj"), 1)
        dt_raw = Signal(sem("s_dt_raw"), 1)
        dt_exp = Signal(sem("s_dt_exp"), 1)
        dt_ln = Signal(sem("s_dt_ln"), 1)
        dt_u = Signal(sem("s_dt_u"), 1)
        a_done = Signal(sem("s_a"), 1)
        acum_mm = Signal(sem("s_acum_mm"), 1)
        acum_cp = Signal(sem("s_acum"), 1)
        d_raw = Signal(sem("s_decay_raw"), 1)
        d_exp = Signal(sem("s_decay_exp"), 1)
        g_mm = Signal(sem("s_ssd_inputs"), 4)
        g_cbm = Signal(sem("s_cb_masked"), 4)
        g_x = Signal(sem("s_xdt"), 4)
        g_cdec = Signal(sem("s_decay_out"), 4)
        g_dif = Signal(sem("s_decay_diff"), 4)
        g_act = Signal(sem("s_decay_mats"), 4)
        g_mats = Signal(sem("s_ssd_mats"), 4)
        g_y = Signal(sem("s_ssd_y"), 4)
        g_used = Signal(sem("s_ssd_used"), 4)
        ys_done = Signal(sem("s_ys"), 2)
        ss2_ms = Signal(sem("s_ss2_ms"), 1)
        rstd2s = Signal(sem("s_rstd2"), 1)
        keysT_tr = Signal(sem("s_keysT_tr"), 4)
        keysT_cp = Signal(sem("s_keysT"), 4)
        qT_cp = Signal(sem("s_qT"), 4)
        score_mm = Signal(sem("s_scores_mm"), 2)
        score_cp = Signal(sem("s_scores"), 2)
        tv_sub = Signal(sem("s_gate_raw"), 2)
        tv_exp = Signal(sem("s_gate_exp"), 2)
        eidx_done = Signal(sem("s_eidx"), 2)
        eidxT_tr = Signal(sem("s_eidxT_tr"), 2)
        idx_done = Signal(sem("s_idx"), 2)
        staged = Signal(sem("s_staged"), 2 * T // RING)
        s_row = [sem(f"s_row{r}") for r in range(RING)]
        ROWS_PER_TURN = 2 * T // RING
        u_used = Signal(sem("s_u_used"), T)
        v_used = Signal(sem("s_v_used"), T)
        held = sem("s_held")
        gelu_raw = Signal(sem("s_gelu_raw"), 1)
        gelu_exp = Signal(sem("s_gelu_exp"), 1)
        w_done = Signal(sem("s_w_gate"), 1)
        wT_tr = Signal(sem("s_wT_tr"), 1)
        wT_cp = Signal(sem("s_wT"), 1)
        oT_cp = Signal(sem("s_oT"), 2)
        o_tr = Signal(sem("s_o_tr"), 2)
        h_blk = Signal(sem("s_h_block"), 2)
        pT_tr = Signal(sem("s_pT_tr"), 1)
        pT_cp = Signal(sem("s_pT"), 1)
        pg_exp = Signal(sem("s_ple_exp"), 2)
        pg_used = Signal(sem("s_ple_exp_used"), 2)
        turn_end = sem("s_turn_end")
        s_vec = sem("s_vector_step")
        s_sca = sem("s_scalar_step")
        s_fin = sem("s_final")
        s_finsq = sem("s_final_sumsq")
        s_out = sem("s_out")

        def turn_barrier(eng, turn):
            eng.drain()
            eng.sem_inc(turn_end, 1)
            eng.wait_ge(turn_end, (turn + 1) * 5)
            eng.sem_inc(held, 1)

        x_v = x.rearrange("o (b p) d -> p (o b) d", p=P)
        out_v = out.rearrange("o (b p) d -> p (o b) d", p=P)
        p_v = p.rearrange("l o (b p) k -> p (l o b) k", p=P)
        win_v = w_in.rearrange("l (k p) n -> p (l k) n", p=P)
        wout_v = w_out.rearrange("l (k p) n -> p (l k) n", p=P)
        wq_v = peer_wq.rearrange("l (k p) n -> p (l k) n", p=P)
        wg_v = w_ple_gate.rearrange("l (k p) n -> p (l k) n", p=P)
        wp_v = w_ple.rearrange("l (k p) n -> p (l k) n", p=P)
        keys_v = peer_keys.rearrange("l h s (a q) d -> (l h s a) (q d)", q=J)
        rows = [(R_CONV, CONV_K * KT, conv_w.rearrange("l j (c p) -> (l j c) p", p=P)),
                (R_MCONV, MCONV_K * XT, mconv_w.rearrange("l j (c p) -> (l j c) p", p=P)),
                (R_MB, XT, mconv_b.rearrange("l (c p) -> (l c) p", p=P)),
                (R_CN, KT, conv_norm_w.rearrange("l (c p) -> (l c) p", p=P)),
                (R_SN, KT, ssd_norm_w.rearrange("l (c p) -> (l c) p", p=P))]
        u_rows = peer_u.rearrange("l e d -> (l e) d")
        v_rows = peer_v.rearrange("l e d -> (l e) d")

        block = c.enter_context(nc.Block())

        @block.sync
        def _(sp):
            sp.dma_start(h[:, :, :], x_v).then_inc(s_hload, 16)
            with sp.Fori(0, DEPTH) as layer:
                with sp.Fori(0, HALVES) as half:
                    turn = layer * HALVES + half

                    def load_unit(u):
                        sp.wait_ge(proj.sem, proj.at(turn, u - 1 if u >= 2 else 0))
                        sp.sem_inc(held, 1)
                        if u < U_OUT:
                            src = win_v[:, bass.ds(layer * KT, KT), IN_COLS[u]:IN_COLS[u] + NW]
                        elif u < U_Q:
                            n, g = divmod(u - U_OUT, 2)
                            src = wout_v[:, bass.ds(layer * 2 * KT + g * KT, KT), n * NW:(n + 1) * NW]
                        elif u < U_PLE:
                            n = u - U_Q
                            src = wq_v[:, bass.ds(layer * KT, KT), n * NW:(n + 1) * NW]
                        else:
                            n, g = divmod(u - U_PLE, 2)
                            if g == 0:
                                src = wg_v[:, bass.ds(layer * KT, KT), n * NW:(n + 1) * NW]
                            else:
                                src = wp_v[:, bass.ds(layer * PT, PT), n * NW:(n + 1) * NW]
                        sp.dma_start(wbuf[:, u % 2, 0:src.shape[1], :], src).then_inc(s_w[u % 2], 16)

                    def load_gain(w):
                        sp.dma_start(gain[:, :], w[bass.ds(layer, 1), :].to_broadcast([P, D])).then_inc(gains.sem, 16)

                    load_gain(norm_mix_w)
                    load_unit(0)
                    for r0, n, v in rows:
                        sp.dma_start(params[r0:r0 + n, :], v[bass.ds(layer * n, n), :]).then_inc(small.sem, 16)
                    sp.dma_start(wdt[:, :, :], win_v[:, bass.ds(layer * KT, KT), D_IN - HEADS:D_IN]).then_inc(small.sem, 16)
                    sp.dma_start(dtb[:, :], dt_bias[bass.ds(layer, 1), :].to_broadcast([P, HEADS])).then_inc(small.sem, 16)
                    sp.dma_start(alog[:, :], a_log[bass.ds(layer, 1), :].to_broadcast([P, HEADS])).then_inc(small.sem, 16)
                    sp.dma_start(dall[:, :], d_skip[bass.ds(layer, 1), :].to_broadcast([P, HEADS])).then_inc(small.sem, 16)
                    sp.dma_start(ptok[:, :, :], p_v[:, bass.ds(turn * HB, HB), :]).then_inc(p_in.sem, 16)
                    for u in range(1, U_OUT):
                        load_unit(u)
                    sp.wait_ge(xns.sem, xns.at(turn, 2))
                    load_gain(norm_ffn_w)
                    for u in range(U_OUT, U_Q):
                        load_unit(u)
                    sp.wait_ge(out_used.sem, out_used.at(turn, 4))
                    sp.dma_start(keys.rearrange("p q d -> p (q d)"), keys_v[bass.ds(layer * P, P), :]).then_inc(keys_in.sem, 16)
                    for u in range(U_Q, U_PLE):
                        load_unit(u)
                    sp.wait_ge(xns.sem, xns.at(turn, 4))
                    load_gain(norm_ple_w)
                    for u in range(U_PLE, UNITS):
                        load_unit(u)
                    turn_barrier(sp, turn)
            sp.dma_start(gain[:, :], final_norm_w.rearrange("(o d) -> o d", o=1).to_broadcast([P, D])).then_inc(gains.sem, 16)
            for b in range(NBLK):
                sp.wait_ge(s_fin, b + 1)
                sp.dma_start(out_v[:, b, :], ring[:, b, :]).then_inc(s_out, 16)
            sp.wait_ge(s_out, 16 * NBLK)

        @block.gpsimd
        def _(g):
            g.memset(ident[:, :], 0.0).then_inc(s_const, 1)
            g.memset(ones[:, :], 1.0).then_inc(s_const, 1)
            g.iota(iota_i[:, :], pattern=[[1, TOPK]], base=0, channel_multiplier=0).then_inc(s_const, 1)
            g.wait_ge(s_const, 3)
            g.affine_select(out=ident[:, :], in_=ident[:, :], compare_op=ALU.not_equal, fill=1.0, base=0,
                            pattern=[[-1, P]], channel_multiplier=1).then_inc(s_const, 1)
            g.affine_select(out=causalT[:, :], in_=ones[:, :], compare_op=ALU.is_ge, fill=0.0, base=0,
                            pattern=[[1, P]], channel_multiplier=-1).then_inc(s_const, 1)

            u_idx = idx_u[:, :, :].rearrange("p b k -> p (b k)")
            v_idx = idx_v[:, :, :].rearrange("p b k -> p (b k)")

            def gather(table, par, r):
                g.indirect_dma_start(
                    out=ring[:, r, :], out_offset=None, in_=table,
                    in_offset=bass.IndirectOffsetOnAxis(ap=stage[:, par, r:r + 1], axis=0),
                ).then_inc(s_row[r], 16)

            with g.Fori(0, DEPTH) as layer:
                with g.Fori(0, HALVES) as half:
                    turn = layer * HALVES + half
                    g.wait_ge(idx_done.sem, idx_done.at(turn, HB))
                    g.sem_inc(held, 1)
                    for par in range(2):
                        g.tensor_copy(stage[:, par, :], u_idx[:, par * RING:(par + 1) * RING]).then_inc(staged.sem, 1)
                        g.wait_ge(staged.sem, staged.at(turn, par + 1))
                        g.sem_inc(held, 1)
                        for r in range(RING):
                            if par:
                                g.wait_ge(u_used.sem, u_used.at(turn, r + 1))
                                g.sem_inc(held, 1)
                            gather(u_rows, par, r)
                    with g.Fori(1, T // BODY) as i:
                        for par in range(2):
                            m = i * 2 + par
                            g.tensor_copy(stage[:, par, :], u_idx[:, bass.ds(m * RING, RING)]).then_inc(staged.sem, 1)
                            g.wait_ge(staged.sem, staged.at(turn, m + 1))
                            g.sem_inc(held, 1)
                            for r in range(RING):
                                g.wait_ge(u_used.sem, u_used.at(turn, m * RING + (r + 1 - RING)))
                                g.sem_inc(held, 1)
                                gather(u_rows, par, r)
                    for par in range(2):
                        g.tensor_copy(stage[:, par, :], v_idx[:, par * RING:(par + 1) * RING]).then_inc(staged.sem, 1)
                        g.wait_ge(staged.sem, staged.at(turn, T // RING + par + 1))
                        g.sem_inc(held, 1)
                        for r in range(RING):
                            if par:
                                g.wait_ge(v_used.sem, v_used.at(turn, r + 1))
                            else:
                                g.wait_ge(u_used.sem, u_used.at(turn, T - RING + r + 1))
                            g.sem_inc(held, 1)
                            gather(v_rows, par, r)
                    with g.Fori(1, T // BODY) as i:
                        for par in range(2):
                            m = i * 2 + par
                            g.tensor_copy(stage[:, par, :], v_idx[:, bass.ds(m * RING, RING)]).then_inc(staged.sem, 1)
                            g.wait_ge(staged.sem, staged.at(turn, m + (T // RING + 1)))
                            g.sem_inc(held, 1)
                            for r in range(RING):
                                g.wait_ge(v_used.sem, v_used.at(turn, m * RING + (r + 1 - RING)))
                                g.sem_inc(held, 1)
                                gather(v_rows, par, r)
                    turn_barrier(g, turn)

        @block.scalar
        def _(s):
            s.wait_ge(s_const, 5)
            with s.Fori(0, DEPTH) as layer:
                with s.Fori(0, HALVES) as half:
                    turn = layer * HALVES + half
                    own = Steps(SCA_PER_TURN, 0, turn, 0, 0)
                    hb = lambda b: h[:, bass.ds(half * HB + b, 1), :].rearrange("p o d -> p (o d)")

                    def norm(n):
                        if n == 0:
                            s.wait_ge(s_hload, 16)
                        elif n == 1:
                            s.wait_ge(out_used.sem, out_used.at(turn, 4))
                            s.sem_inc(held, 1)
                        else:
                            s.wait_ge(h_blk.sem, h_blk.at(turn, 2))
                            s.sem_inc(held, 1)
                        for b in range(HB):
                            m = s.activation(etmp[:, 0:4, :].rearrange("p a b -> p (a b)"), hb(b), ACT.Square,
                                             accum_out=ss[:, b:b + 1])
                            if b == HB - 1:
                                m.then_inc(sumsq.sem, 1)
                            else:
                                m.then_inc(s_sca, own.one())
                                s.wait_ge(s_sca, own.so_far())
                                s.sem_inc(held, 1)
                        s.wait_ge(meansq.sem, meansq.at(turn, n + 1))
                        s.activation(rstd[:, :], ss[:, :], ACT.Ln).then_inc(s_sca, own.one())
                        s.wait_ge(s_sca, own.so_far())
                        s.activation(rstd[:, :], rstd[:, :], ACT.Exp, scale=-0.5).then_inc(rstds.sem, 1)
                        for b in range(HB):
                            s.wait_ge(tr_done.sem, tr_done.at(turn, n * HB + b + 1))
                            s.copy(xnT[:, :, b * P:(b + 1) * P],
                                   ppf[:, b * D:(b + 1) * D].rearrange("p (a b) -> p a b", b=P)
                                   ).then_inc(xnT_done.sem, 1)

                    norm(0)
                    s.wait_ge(par_T.sem, par_T.at(turn, 1))
                    s.copy(paramsT[:, 0:ROWS], px[:, 0:ROWS]).then_inc(par_done.sem, 1)
                    s.wait_ge(par_done.sem, par_done.at(turn, 1))
                    s.wait_ge(small.sem, small.at(turn, SMALL))
                    s.activation(expa[:, :], alog[:, :], ACT.Exp).then_inc(expa_done.sem, 1)
                    for i in range(2):
                        s.wait_ge(proj.sem, proj.at(turn, i + 1))
                        s.copy(conv_in[:, i * TPU:(i + 1) * TPU, CONV_K - 1:], ppt[:, i % 2]).then_inc(gc_in.sem, 1)
                    s.wait_ge(dt_raw.sem, dt_raw.at(turn, 1))
                    s.activation(dts[:, 2], dts[:, 1], ACT.Exp, scale=-1.0).then_inc(dt_exp.sem, 1)
                    s.wait_ge(dt_u.sem, dt_u.at(turn, 1))
                    s.activation(dts[:, 4], dts[:, 3], ACT.Ln).then_inc(dt_ln.sem, 1)
                    for i in range(2):
                        s.wait_ge(yc_done.sem, yc_done.at(turn, i + 1))
                        if i:
                            s.wait_ge(sq_used.sem, sq_used.at(turn, i))
                        s.activation(etmp[:, :, :], yc[:, i * TPU:(i + 1) * TPU, :], ACT.Square).then_inc(sq_done.sem, 1)
                    s.wait_ge(sq_done.sem, sq_done.at(turn, 2))
                    for t in range(KT):
                        m = s.activation(yc[:, t, :], yc[:, t, :], ACT.Copy, scale=paramsT[:, R_CN + t:R_CN + t + 1])
                    m.then_inc(y_scaled.sem, 1)
                    for i in range(2):
                        s.wait_ge(proj.sem, proj.at(turn, 7 + i))
                        s.activation(zs[:, i * TPU:(i + 1) * TPU, :], ppt[:, i % 2], ACT.Exp, scale=-1.0).then_inc(z_exp.sem, 1)
                    s.wait_ge(sq_used.sem, sq_used.at(turn, 2))
                    for i in range(XT // TPU):
                        s.wait_ge(proj.sem, proj.at(turn, 9 + i))
                        s.copy(xbc_in[:, i * TPU:(i + 1) * TPU, MCONV_K - 1:], ppt[:, i % 2]).then_inc(xbc_cp.sem, 1)
                    for i in range(XT // TPU):
                        s.wait_ge(conv_done.sem, conv_done.at(turn, i + 1))
                        if i:
                            s.wait_ge(silu_done.sem, silu_done.at(turn, i))
                        s.activation(etmp[:, :, :], xc[:, i * TPU:(i + 1) * TPU, :], ACT.Exp, scale=-1.0).then_inc(silu_exp.sem, 1)
                    s.wait_ge(d_raw.sem, d_raw.at(turn, 1))
                    s.activation(d_in[:, :, :], d_in[:, :, :], ACT.Exp).then_inc(s_sca, own.one())
                    s.activation(d_chunk[:, :, :], acum[:, :, 1, :], ACT.Exp).then_inc(d_exp.sem, 1)
                    for i in range(4):
                        b, g = divmod(i, 2)
                        s.wait_ge(g_mm.sem, g_mm.at(turn, i + 1))
                        if i:
                            s.wait_ge(g_y.sem, g_y.at(turn, i))
                        s.activation(c_dec, ppf[:, 0:HG * P].rearrange("p (a b) -> p a b", b=P), ACT.Exp).then_inc(g_cdec.sem, 1)
                        s.wait_ge(g_dif.sem, g_dif.at(turn, i + 1))
                        s.activation(decay, decay, ACT.Exp).then_inc(g_act.sem, 1)
                    for b in range(HB):
                        s.wait_ge(ys_done.sem, ys_done.at(turn, b + 1))
                        if b:
                            s.wait_ge(sq_used.sem, sq_used.at(turn, 2 + b))
                        s.activation(etmp[:, :, :].rearrange("p a (b t) -> p (a b) t", t=P), ys[:, :, b * P:(b + 1) * P],
                                     ACT.Square).then_inc(sq_done.sem, 1)
                    s.wait_ge(sq_done.sem, sq_done.at(turn, 4))
                    for t in range(KT):
                        m = s.activation(ys[:, t, :], ys[:, t, :], ACT.Copy, scale=paramsT[:, R_SN + t:R_SN + t + 1])
                    m.then_inc(y_scaled.sem, 1)
                    s.wait_ge(ss2_ms.sem, ss2_ms.at(turn, 1))
                    s.activation(rstd2[:, :, :], ss2[:, :, :], ACT.Ln).then_inc(s_sca, own.one())
                    s.wait_ge(s_sca, own.so_far())
                    s.activation(rstd2[:, :, :], rstd2[:, :, :], ACT.Exp, scale=-0.5).then_inc(rstd2s.sem, 1)
                    s.wait_ge(sq_used.sem, sq_used.at(turn, 4))
                    norm(1)
                    for i in range(4):
                        s.wait_ge(proj.sem, proj.at(turn, U_Q + i + 1))
                        s.copy(qT[:, i * TPU:(i + 1) * TPU, :], ppt[:, (U_Q + i) % 2]).then_inc(qT_cp.sem, 1)
                    for i in range(4):
                        s.wait_ge(keysT_tr.sem, keysT_tr.at(turn, i + 1))
                        s.copy(keysT.rearrange("d j n -> d (j n)").rearrange("d (r q) -> d q r", q=J)[:, i * 4:(i + 1) * 4, :],
                               pxt).then_inc(keysT_cp.sem, 1)
                    for b in range(HB):
                        s.wait_ge(score_mm.sem, score_mm.at(turn, b + 1))
                        if b:
                            s.wait_ge(idx_done.sem, idx_done.at(turn, b))
                        s.copy(sc, ppf.rearrange("p (a b) -> p a b", b=P)).then_inc(score_cp.sem, 1)
                        s.wait_ge(tv_sub.sem, tv_sub.at(turn, b + 1))
                        s.activation(gate[:, b, :], gate[:, b, :], ACT.Exp).then_inc(tv_exp.sem, 1)
                    s.wait_ge(gelu_raw.sem, gelu_raw.at(turn, 1))
                    s.activation(gl[:, :, :], gl[:, :, :], ACT.Exp, scale=-2.0 * GELU_C).then_inc(gelu_exp.sem, 1)
                    for b in range(HB):
                        s.wait_ge(v_used.sem, v_used.at(turn, (b + 1) * P))
                        if b:
                            s.wait_ge(o_tr.sem, o_tr.at(turn, b))
                        s.copy(etmp[:, :, :].rearrange("p a (b t) -> p (a b) t", t=P), pv[:, :, :]).then_inc(oT_cp.sem, 1)
                    s.wait_ge(o_tr.sem, o_tr.at(turn, 2))
                    norm(2)
                    s.wait_ge(pT_tr.sem, pT_tr.at(turn, 1))
                    s.copy(pT, pxt).then_inc(pT_cp.sem, 1)
                    for n in range(2):
                        s.wait_ge(proj.sem, proj.at(turn, U_PLE + 2 * n + 1))
                        if n:
                            s.wait_ge(pg_used.sem, pg_used.at(turn, n))
                        else:
                            s.wait_ge(xnT_done.sem, xnT_done.at(turn, 6))
                        s.activation(etmp[:, :, :].rearrange("p a b -> p (a b)"),
                                     pp[:, (U_PLE + 2 * n) % 2].rearrange("p a b -> p (a b)"), ACT.Exp,
                                     scale=-1.0).then_inc(pg_exp.sem, 1)
                    assert own.n == SCA_PER_TURN, f"sca_turn={own.n}"
                    turn_barrier(s, turn)
            for b in range(NBLK):
                s.activation(junk[:, b % 2, :], h[:, b, :], ACT.Square, accum_out=fin[:, 0, b:b + 1]).then_inc(s_finsq, 1)
                s.wait_ge(s_finsq, b + 1)
            s.wait_ge(s_finsq, NBLK + 1)
            s.activation(fin[:, 1, :], fin[:, 1, :], ACT.Ln).then_inc(s_finsq, 1)
            s.wait_ge(s_finsq, NBLK + 2)
            s.activation(fin[:, 1, :], fin[:, 1, :], ACT.Exp, scale=-0.5).then_inc(s_finsq, 1)

        @block.vector
        def _(v):
            v.wait_ge(s_const, 5)
            pre = Steps(0, 0, 0, 0, 0)
            v.tensor_copy(iota_f[:, :], iota_i[:, :]).then_inc(s_vec, pre.one())
            v.memset(expert0[:, :], -float(EXPERTS)).then_inc(s_vec, pre.one())
            v.wait_ge(s_vec, pre.so_far())
            with v.Fori(0, DEPTH) as layer:
                lay = Steps(HALVES * VEC_PER_TURN, VEC_PER_LAYER, layer, layer, pre.n)
                v.memset(conv_in[:, :, 0:CONV_K - 1], 0.0).then_inc(s_vec, lay.one())
                v.memset(xbc_in[:, :, 0:MCONV_K - 1], 0.0).then_inc(s_vec, lay.one())
                v.memset(state[:, :, :], 0.0).then_inc(s_vec, lay.one())
                v.tensor_scalar_add(expert0[:, :], expert0[:, :], float(EXPERTS)).then_inc(s_vec, lay.one())
                v.wait_ge(s_vec, lay.so_far())
                v.sem_inc(held, 1)
                assert lay.n - pre.n == VEC_PER_LAYER, f"vec_layer={lay.n - pre.n}"
                with v.Fori(0, HALVES) as half:
                    turn = layer * HALVES + half
                    own = Steps(VEC_PER_TURN, VEC_PER_LAYER, turn, layer, lay.n)
                    hb = lambda b: h[:, bass.ds(half * HB + b, 1), :].rearrange("p o d -> p (o d)")
                    hbc = lambda b, c0, n: h[:, bass.ds(half * HB + b, 1), c0:c0 + n].rearrange("p o d -> p (o d)")

                    def norm(n):
                        v.wait_ge(sumsq.sem, sumsq.at(turn, n + 1))
                        v.tensor_scalar(ss[:, :], ss[:, :], 1.0 / D, EPS, ALU.mult, ALU.add).then_inc(meansq.sem, 1)
                        v.wait_ge(gains.sem, gains.at(turn, 16 * (n + 1)))
                        v.wait_ge(rstds.sem, rstds.at(turn, n + 1))
                        for b in range(HB):
                            v.scalar_tensor_tensor(out=xn[:, b, :], in0=hb(b), scalar=rstd[:, b:b + 1], in1=gain[:, :],
                                                   op0=ALU.mult, op1=ALU.mult).then_inc(xns.sem, 1)

                    def silu_tail(out, e, arg, signal):
                        v.tensor_scalar_add(e, e, 1.0).then_inc(s_vec, own.one())
                        v.wait_ge(s_vec, own.so_far())
                        v.reciprocal(e, e).then_inc(s_vec, own.one())
                        v.wait_ge(s_vec, own.so_far())
                        v.tensor_tensor(out, e, arg, ALU.mult).then_inc(signal.sem, 1)

                    v.wait_ge(s_hload, 16)
                    norm(0)
                    v.wait_ge(small.sem, small.at(turn, SMALL))
                    for s_ in range(2):
                        v.tensor_copy(dskip[s_ * HD:(s_ + 1) * HD, :],
                                              dall[s_ * HD:(s_ + 1) * HD, :].rearrange("p (c s) -> p s c", s=2)[:, s_, :]).then_inc(s_vec, own.one())
                    v.wait_ge(dt_proj.sem, dt_proj.at(turn, 1))
                    v.tensor_tensor(dts[:, 0], pm[:, 0:HB * HEADS].rearrange("p (a b) -> p a b", b=HEADS),
                                             over(dtb[:, :], 1, HB), ALU.add).then_inc(s_vec, own.one())
                    v.wait_ge(s_vec, own.so_far())
                    v.scalar_tensor_tensor(out=dts[:, 1], in0=dts[:, 0], scalar=-1.0, in1=dts[:, 0], op0=ALU.mult, op1=ALU.max).then_inc(dt_raw.sem, 1)
                    v.tensor_scalar_max(dts[:, 0], dts[:, 0], 0.0).then_inc(s_vec, own.one())
                    v.wait_ge(dt_exp.sem, dt_exp.at(turn, 1))
                    v.tensor_scalar_add(dts[:, 3], dts[:, 2], 1.0).then_inc(dt_u.sem, 1)
                    v.wait_ge(dt_u.sem, dt_u.at(turn, 1))
                    v.reciprocal(dts[:, 5], dts[:, 3]).then_inc(s_vec, own.one())
                    v.tensor_scalar_add(dt[:, :, :], dts[:, 3], -1.0).then_inc(s_vec, own.one())
                    v.wait_ge(s_vec, own.so_far())
                    v.tensor_tensor(dts[:, 2], dts[:, 2], dt[:, :, :], ALU.subtract).then_inc(s_vec, own.one())
                    v.wait_ge(s_vec, own.so_far())
                    v.tensor_tensor(dts[:, 2], dts[:, 2], dts[:, 5], ALU.mult).then_inc(s_vec, own.one())
                    v.wait_ge(s_vec, own.so_far())
                    v.tensor_tensor(dts[:, 2], dts[:, 2], dts[:, 0], ALU.add).then_inc(s_vec, own.one())
                    v.wait_ge(s_vec, own.so_far())
                    v.wait_ge(dt_ln.sem, dt_ln.at(turn, 1))
                    v.tensor_tensor(dt[:, :, :], dts[:, 2], dts[:, 4], ALU.add).then_inc(s_vec, own.one())
                    v.wait_ge(s_vec, own.so_far())
                    v.wait_ge(par_done.sem, par_done.at(turn, 1))
                    v.wait_ge(expa_done.sem, expa_done.at(turn, 1))
                    v.scalar_tensor_tensor(out=a_[:, :, :], in0=dt[:, :, :], scalar=-1.0, in1=over(expa[:, :], 1, HB),
                                           op0=ALU.mult, op1=ALU.mult).then_inc(a_done.sem, 1)
                    for i in range(2):
                        tiles = slice(i * TPU, (i + 1) * TPU)
                        v.wait_ge(proj.sem, proj.at(turn, 3 + i))
                        v.wait_ge(gc_in.sem, gc_in.at(turn, 2))
                        v.tensor_tensor(conv_in[:, tiles, CONV_K - 1:], conv_in[:, tiles, CONV_K - 1:], ppt[:, i % 2],
                                        ALU.mult).then_inc(hc_done.sem, 1)
                        v.wait_ge(hc_done.sem, hc_done.at(turn, i + 1))

                        def tap(j, t):
                            return paramsT[:, R_CONV + j * KT + t:R_CONV + j * KT + t + 1]

                        for j in range(CONV_K):
                            for t in range(i * TPU, (i + 1) * TPU):
                                if j == 0:
                                    m = v.tensor_scalar(yc[:, t, :], conv_in[:, t, 0:T], tap(0, t), None, ALU.mult)
                                else:
                                    m = v.scalar_tensor_tensor(out=yc[:, t, :], in0=conv_in[:, t, j:j + T], scalar=tap(j, t),
                                                               in1=yc[:, t, :], op0=ALU.mult, op1=ALU.add)
                                m.then_inc(s_vec, own.one())
                            v.wait_ge(s_vec, own.so_far())
                    v.tensor_copy(conv_in[:, :, 0:CONV_K - 1], conv_in[:, :, T:T + CONV_K - 1]).then_inc(s_vec, own.one())
                    for i in range(2):
                        tiles = slice(i * TPU, (i + 1) * TPU)
                        v.wait_ge(proj.sem, proj.at(turn, 5 + i))
                        v.tensor_tensor(yc[:, tiles, :], yc[:, tiles, :], ppt[:, i % 2], ALU.mult).then_inc(yc_done.sem, 1)
                    for i in range(2):
                        v.wait_ge(z_exp.sem, z_exp.at(turn, i + 1))
                        silu_tail(zs[:, i * TPU:(i + 1) * TPU, :], zs[:, i * TPU:(i + 1) * TPU, :], ppt[:, i % 2], z_done)
                    for i in range(XT // TPU):
                        v.wait_ge(xbc_cp.sem, xbc_cp.at(turn, i + 1))

                        def mtap(j, t):
                            return paramsT[:, R_MCONV + j * XT + t:R_MCONV + j * XT + t + 1]

                        for j in range(MCONV_K):
                            for t in range(i * TPU, (i + 1) * TPU):
                                if j == 0:
                                    m = v.tensor_scalar(xc[:, t, :], xbc_in[:, t, 0:T], mtap(0, t),
                                                        paramsT[:, R_MB + t:R_MB + t + 1], ALU.mult, ALU.add)
                                else:
                                    m = v.scalar_tensor_tensor(out=xc[:, t, :], in0=xbc_in[:, t, j:j + T], scalar=mtap(j, t),
                                                               in1=xc[:, t, :], op0=ALU.mult, op1=ALU.add)
                                if j == MCONV_K - 1 and t == (i + 1) * TPU - 1:
                                    m.then_inc(conv_done.sem, 1)
                                else:
                                    m.then_inc(s_vec, own.one())
                            if j < MCONV_K - 1:
                                v.wait_ge(s_vec, own.so_far())
                        v.wait_ge(silu_exp.sem, silu_exp.at(turn, i + 1))
                        silu_tail(xc[:, i * TPU:(i + 1) * TPU, :], etmp[:, :, :], xc[:, i * TPU:(i + 1) * TPU, :], silu_done)
                    v.tensor_copy(xbc_in[:, :, 0:MCONV_K - 1], xbc_in[:, :, T:T + MCONV_K - 1]).then_inc(s_vec, own.one())
                    v.wait_ge(acum_mm.sem, acum_mm.at(turn, 1))
                    v.tensor_copy(acum[:, :, :, :].rearrange("p a b c -> p (a b c)"), pm[:, 0:4 * HEADS]).then_inc(acum_cp.sem, 1)
                    v.wait_ge(acum_cp.sem, acum_cp.at(turn, 1))
                    v.tensor_tensor(d_in[:, :, :], acum[:, :, 1, :], acum[:, :, 0, :], ALU.subtract).then_inc(d_raw.sem, 1)
                    v.wait_ge(d_exp.sem, d_exp.at(turn, 1))
                    v.wait_ge(silu_done.sem, silu_done.at(turn, XT // TPU))
                    for i in range(4):
                        b, g = divmod(i, 2)
                        heads = slice(g * HG, (g + 1) * HG)
                        v.wait_ge(g_mm.sem, g_mm.at(turn, i + 1))
                        if i:
                            v.wait_ge(g_y.sem, g_y.at(turn, i))
                        v.tensor_tensor(cbm[:, :], pm[:, P:2 * P], causalT[:, :], ALU.mult)
                        v.tensor_copy(b_tok[:, :], pm[:, 2 * P:3 * P])
                        v.tensor_tensor(xdt, pxt.rearrange("p a (b c) -> p (a b) c", c=HD),
                                                 over(dt[:, b, heads], 2, HD), ALU.mult).then_inc(s_vec, own.one())
                        v.wait_ge(s_vec, own.so_far())
                        v.tensor_tensor(xdtd, xdt, over(d_in[:, b, heads], 2, HD), ALU.mult).then_inc(s_vec, own.one())
                        v.wait_ge(g_cdec.sem, g_cdec.at(turn, i + 1))
                        for k in range(HG):
                            m = v.tensor_scalar(decay[:, k, :], ppf[:, k * P:(k + 1) * P],
                                                acum[:, b, 0, g * HG + k:g * HG + k + 1], 0.0, ALU.subtract, ALU.min)
                        m.then_inc(g_dif.sem, 1)
                        v.wait_ge(g_act.sem, g_act.at(turn, i + 1))
                        v.tensor_tensor(c_dec, c_dec, over(xc[:, 10 + g, b * P:(b + 1) * P], 1, HG), ALU.mult)
                        v.tensor_tensor(decay, decay, over(cbm[:, :], 1, HG), ALU.mult).then_inc(g_mats.sem, 1)
                        v.wait_ge(g_y.sem, g_y.at(turn, i + 1))
                        v.tensor_tensor(state[:, heads, :], state[:, heads, :],
                                                 over(d_chunk[:, b, heads], 2, HD), ALU.mult).then_inc(s_vec, own.one())
                        v.wait_ge(s_vec, own.so_far())
                        v.tensor_tensor(state[:, heads, :], state[:, heads, :],
                                                ppf[:, 3 * NW:4 * NW].rearrange("p (a b) -> p a b", b=HD), ALU.add).then_inc(s_vec, own.one())
                        for t in range(4):
                            tt = g * 4 + t
                            m = v.scalar_tensor_tensor(out=ys[:, tt, b * P:(b + 1) * P], in0=xc[:, tt, b * P:(b + 1) * P],
                                                       scalar=dskip[:, tt:tt + 1],
                                                       in1=ppf[:, 2 * NW + t * P:2 * NW + (t + 1) * P],
                                                       op0=ALU.mult, op1=ALU.add)
                        m.then_inc(g_used.sem, 1)
                        if g == 1:
                            v.wait_ge(g_used.sem, g_used.at(turn, i + 1))
                            v.tensor_tensor(ys[:, :, b * P:(b + 1) * P], ys[:, :, b * P:(b + 1) * P],
                                            zs[:, :, b * P:(b + 1) * P], ALU.mult).then_inc(ys_done.sem, 1)
                    v.wait_ge(sq_used.sem, sq_used.at(turn, 4))
                    v.tensor_copy(sums[:, :], pm[:, SUMS:SUMS + 6]).then_inc(s_vec, own.one())
                    v.wait_ge(s_vec, own.so_far())
                    v.tensor_tensor(sums[:, 0:HB], sums[:, 0:HB], sums[:, HB:2 * HB], ALU.add).then_inc(s_vec, own.one())
                    v.wait_ge(s_vec, own.so_far())
                    v.tensor_scalar(ss2[:, :, 0], sums[:, 0:HB], 1.0 / D, EPS, ALU.mult, ALU.add)
                    v.tensor_scalar(ss2[:, :, 1], sums[:, 2 * HB:3 * HB], 1.0 / D, EPS, ALU.mult,
                                    ALU.add).then_inc(ss2_ms.sem, 1)
                    v.wait_ge(rstd2s.sem, rstd2s.at(turn, 1))
                    for i in range(4):
                        n, g = divmod(i, 2)
                        v.wait_ge(proj.sem, proj.at(turn, U_OUT + i + 1))
                        for b in range(HB):
                            hh = hbc(b, n * NW, NW)
                            m = v.scalar_tensor_tensor(out=hh, in0=pp[:, (U_OUT + i) % 2, b, :], scalar=rstd2[:, b, g:g + 1],
                                                       in1=hh, op0=ALU.mult, op1=ALU.add)
                            if b == HB - 1:
                                m.then_inc(out_used.sem, 1)
                        v.wait_ge(out_used.sem, out_used.at(turn, i + 1))
                    norm(1)
                    for b in range(HB):
                        v.wait_ge(score_cp.sem, score_cp.at(turn, b + 1))
                        v.sem_inc(held, 1)
                        for j in range(J):
                            v.max(out=sv[:, j, 0:8], in_=sc[:, j, :]).then_inc(s_vec, own.one())
                        v.wait_ge(s_vec, own.so_far())
                        v.sem_inc(held, 1)
                        for j in range(J):
                            v.max_index(out=si[:, j, 0:8], in_max=sv[:, j, 0:8], in_values=sc[:, j, :]).then_inc(s_vec, own.one())
                            v.match_replace(out=sc2[:, j, :], in_to_replace=sv[:, j, 0:8], in_values=sc[:, j, :],
                                                    imm_value=NEG).then_inc(s_vec, own.one())
                        v.wait_ge(s_vec, own.so_far())
                        v.sem_inc(held, 1)
                        for j in range(J):
                            v.max(out=sv[:, j, 8:16], in_=sc2[:, j, :]).then_inc(s_vec, own.one())
                        v.wait_ge(s_vec, own.so_far())
                        v.sem_inc(held, 1)
                        for j in range(J):
                            v.max_index(out=si[:, j, 8:16], in_max=sv[:, j, 8:16], in_values=sc2[:, j, :]).then_inc(s_vec, own.one())
                        v.wait_ge(s_vec, own.so_far())
                        v.sem_inc(held, 1)
                        svp = sv[:, :, :].rearrange("p (h s) k -> p h s k", s=2)
                        v.tensor_copy(sif[:, :, :], si[:, :, :]).then_inc(s_vec, own.one())
                        v.wait_ge(score_mm.sem, score_mm.at(turn, HB))
                        v.tensor_tensor(cand[:, :, :, :], over(svp[:, :, 0, :], 3, TOPK), over(svp[:, :, 1, :], 2, TOPK),
                                                 ALU.add).then_inc(s_vec, own.one())
                        v.wait_ge(s_vec, own.so_far())
                        v.sem_inc(held, 1)
                        cf = cand[:, :, :, :].rearrange("p h a b -> p h (a b)")
                        for j in range(PH):
                            v.max(out=tv[:, j, 0:8], in_=cf[:, j, :]).then_inc(s_vec, own.one())
                        v.wait_ge(s_vec, own.so_far())
                        v.sem_inc(held, 1)
                        for j in range(PH):
                            v.max_index(out=ti[:, j, 0:8], in_max=tv[:, j, 0:8], in_values=cf[:, j, :]).then_inc(s_vec, own.one())
                            v.match_replace(out=cand2[:, j, :], in_to_replace=tv[:, j, 0:8], in_values=cf[:, j, :],
                                                    imm_value=NEG).then_inc(s_vec, own.one())
                        v.wait_ge(s_vec, own.so_far())
                        v.sem_inc(held, 1)
                        for j in range(PH):
                            v.max(out=tv[:, j, 8:16], in_=cand2[:, j, :]).then_inc(s_vec, own.one())
                        v.wait_ge(s_vec, own.so_far())
                        v.sem_inc(held, 1)
                        for j in range(PH):
                            v.max_index(out=ti[:, j, 8:16], in_max=tv[:, j, 8:16], in_values=cand2[:, j, :]).then_inc(s_vec, own.one())
                        v.wait_ge(s_vec, own.so_far())
                        v.sem_inc(held, 1)
                        gb = gate[:, b, :].rearrange("p (h k) -> p h k", k=TOPK)
                        v.tensor_tensor(gb, tv[:, :, :], tv[:, :, 0:1].to_broadcast([P, PH, TOPK]),
                                        ALU.subtract).then_inc(tv_sub.sem, 1)
                        tif = ti[:, :, :].rearrange("p h k -> p (h k)")
                        v.tensor_single_scalar(tq[:, 0, :], tif, 4, ALU.logical_shift_right).then_inc(s_vec, own.one())
                        v.tensor_single_scalar(tq[:, 1, :], tif, 15, ALU.bitwise_and).then_inc(s_vec, own.one())
                        v.wait_ge(s_vec, own.so_far())
                        v.tensor_copy(tqf[:, :, :], tq[:, :, :]).then_inc(s_vec, own.one())
                        v.wait_ge(s_vec, own.so_far())
                        for s_ in range(2):
                            v.tensor_tensor(hot, over(tqf[:, s_, :], 2, TOPK), over(iota_f[:, :], 1, SLOTS), ALU.is_equal).then_inc(s_vec, own.one())
                            v.wait_ge(s_vec, own.so_far())
                            h4 = hot.rearrange("p (h k) j -> p h k j", k=TOPK)
                            sel = over(sif[:, :, :].rearrange("p (h s) k -> p h s k", s=2)[:, :, s_, :], 2, TOPK)
                            v.tensor_tensor(h4, h4, sel, ALU.mult).then_inc(s_vec, own.one())
                            v.wait_ge(s_vec, own.so_far())
                            v.tensor_reduce(out=ei[:, s_, :], in_=hot, axis=AX.X, op=ALU.add).then_inc(s_vec, own.one())
                            v.wait_ge(s_vec, own.so_far())
                        v.scalar_tensor_tensor(out=eidx[:, :], in0=ei[:, 0, :], scalar=float(KEYS), in1=ei[:, 1, :],
                                                        op0=ALU.mult, op1=ALU.add).then_inc(s_vec, own.one())
                        v.wait_ge(s_vec, own.so_far())
                        v.tensor_scalar(eidx[:, :], eidx[:, :], expert0[:, 0:1], None, ALU.add).then_inc(eidx_done.sem, 1)
                        v.wait_ge(eidx_done.sem, eidx_done.at(turn, b + 1))
                        v.tensor_copy(idx_u[:, b, :], eidx[:, :]).then_inc(s_vec, own.one())
                        v.wait_ge(eidxT_tr.sem, eidxT_tr.at(turn, b + 1))
                        v.tensor_copy(idx_v[:, b, :], px[:, 0:P]).then_inc(idx_done.sem, 1)
                        v.wait_ge(tv_exp.sem, tv_exp.at(turn, b + 1))
                        v.tensor_reduce(out=gsum[:, :], in_=gb, axis=AX.X, op=ALU.add).then_inc(s_vec, own.one())
                        v.wait_ge(s_vec, own.so_far())
                        v.reciprocal(gsum[:, :], gsum[:, :]).then_inc(s_vec, own.one())
                        v.wait_ge(s_vec, own.so_far())
                        v.tensor_tensor(gb, gb, over(gsum[:, :], 2, TOPK), ALU.mult).then_inc(s_vec, own.one())
                        v.wait_ge(s_vec, own.so_far())
                    for b in range(HB):
                        def dots(i, first):
                            for r in range(BODY):
                                k = i * BODY + (b * P + r)
                                v.wait_ge(s_row[r % RING], (turn * ROWS_PER_TURN + i * 2 + (b * P // RING + r // RING + 1)) * 16)
                                if not (first and r < 2):
                                    v.wait_ge(u_used.sem, u_used.at(turn, k - 1))
                                col = act[:, b, r:r + 1] if isinstance(i, int) else act[:, b, bass.ds(i * BODY + r, 1)]
                                v.scalar_tensor_tensor(out=junk[:, r % 2, :], in0=ring[:, r % RING, :], scalar=1.0,
                                                       in1=xn[:, b, :], op0=ALU.mult, op1=ALU.mult,
                                                       accum_out=col).then_inc(u_used.sem, 1)
                        dots(0, b == 0)
                        with v.Fori(1, P // BODY) as i:
                            dots(i, False)
                    v.wait_ge(u_used.sem, u_used.at(turn, T))
                    v.tensor_tensor(gl[:, :, :], act[:, :, :], act[:, :, :], ALU.mult).then_inc(s_vec, own.one())
                    v.wait_ge(s_vec, own.so_far())
                    v.tensor_scalar(gl[:, :, :], gl[:, :, :], GELU_A, 1.0, ALU.mult, ALU.add).then_inc(s_vec, own.one())
                    v.wait_ge(s_vec, own.so_far())
                    v.tensor_tensor(gl[:, :, :], gl[:, :, :], act[:, :, :], ALU.mult).then_inc(gelu_raw.sem, 1)
                    v.wait_ge(gelu_exp.sem, gelu_exp.at(turn, 1))
                    v.tensor_scalar_add(gl[:, :, :], gl[:, :, :], 1.0).then_inc(s_vec, own.one())
                    v.wait_ge(s_vec, own.so_far())
                    v.reciprocal(gl[:, :, :], gl[:, :, :]).then_inc(s_vec, own.one())
                    v.wait_ge(s_vec, own.so_far())
                    v.tensor_tensor(gl[:, :, :], gl[:, :, :], act[:, :, :], ALU.mult).then_inc(s_vec, own.one())
                    v.wait_ge(s_vec, own.so_far())
                    v.tensor_tensor(gl[:, :, :], gl[:, :, :], gate[:, :, :], ALU.mult).then_inc(w_done.sem, 1)
                    v.wait_ge(wT_tr.sem, wT_tr.at(turn, 1))
                    v.tensor_copy(wT[:, :, :].rearrange("p a b -> p (a b)"), px[:, 0:T]).then_inc(wT_cp.sem, 1)
                    for b in range(HB):
                        v.wait_ge(o_tr.sem, o_tr.at(turn, b + 1))
                        v.tensor_tensor(hb(b), hb(b), ppf[:, b * D:(b + 1) * D], ALU.add).then_inc(h_blk.sem, 1)
                    v.wait_ge(h_blk.sem, h_blk.at(turn, 2))
                    norm(2)
                    for n in range(2):
                        v.wait_ge(pg_exp.sem, pg_exp.at(turn, n + 1))
                        e2 = etmp[:, :, :].rearrange("p a b -> p (a b)")
                        v.tensor_scalar_add(e2, e2, 1.0).then_inc(s_vec, own.one())
                        v.wait_ge(s_vec, own.so_far())
                        v.reciprocal(e2, e2).then_inc(s_vec, own.one())
                        v.wait_ge(s_vec, own.so_far())
                        v.wait_ge(proj.sem, proj.at(turn, U_PLE + 2 * n + 2))
                        v.tensor_tensor(e2, e2, pp[:, (U_PLE + 2 * n + 1) % 2].rearrange("p a b -> p (a b)"), ALU.mult).then_inc(s_vec, own.one())
                        v.wait_ge(s_vec, own.so_far())
                        for b in range(HB):
                            hh = hbc(b, n * NW, NW)
                            m = v.tensor_tensor(hh, hh, e2[:, b * NW:(b + 1) * NW], ALU.add)
                        m.then_inc(pg_used.sem, 1)
                    assert own.n - lay.n == VEC_PER_TURN, f"vec_turn={own.n - lay.n}"
                    turn_barrier(v, turn)
            v.wait_ge(s_finsq, NBLK)
            v.tensor_scalar(fin[:, 1, :], fin[:, 0, :], 1.0 / D, EPS, ALU.mult, ALU.add).then_inc(s_finsq, 1)
            v.wait_ge(gains.sem, 16 * (3 * DEPTH * HALVES + 1))
            v.wait_ge(s_finsq, NBLK + 3)
            for b in range(NBLK):
                v.scalar_tensor_tensor(out=ring[:, b, :], in0=h[:, b, :], scalar=fin[:, 1, b:b + 1], in1=gain[:, :],
                                       op0=ALU.mult, op1=ALU.mult).then_inc(s_fin, 1)

        @block.tensor
        def _(t):
            t.wait_ge(s_const, 5)
            t.sem_inc(proj.sem, 1)
            with t.Fori(0, DEPTH) as layer:
                with t.Fori(0, HALVES) as half:
                    turn = layer * HALVES + half

                    def weights(u):
                        per = EVEN if u % 2 == 0 else ODD
                        t.wait_ge(s_w[u % 2], (turn * per + (u // 2 + 1)) * 16)

                    def tiles_unit(u):
                        weights(u)
                        for m in range(TPU):
                            for k in range(KT):
                                mm = t.matmul(ppt[:, u % 2, m, :], wbuf[:, u % 2, k, m * P:(m + 1) * P], xnT[:, k, :],
                                              start=(k == 0), stop=(k == KT - 1))
                        mm.then_inc(proj.sem, 1)

                    def rows_unit(u, lhs, nk):
                        weights(u)
                        for b in range(HB):
                            for k in range(nk):
                                mm = t.matmul(pp[:, u % 2, b, :], lhs(k, b), wbuf[:, u % 2, k, :], start=(k == 0),
                                              stop=(k == nk - 1))
                        mm.then_inc(proj.sem, 1)

                    def block_of(tile, k, b):
                        return tile[:, k, b * P:(b + 1) * P]

                    def norm_T(n):
                        for b in range(HB):
                            t.wait_ge(xns.sem, xns.at(turn, n * HB + b + 1))
                            for k in range(KT):
                                mm = t.transpose(ppf[:, b * D + k * P:b * D + (k + 1) * P], xn[:, b, k * P:(k + 1) * P],
                                                 ident[:, :])
                            mm.then_inc(tr_done.sem, 1)
                        t.wait_ge(xnT_done.sem, xnT_done.at(turn, n * HB + HB))

                    norm_T(0)
                    t.wait_ge(small.sem, small.at(turn, SMALL))
                    t.transpose(px[:, 0:ROWS], params[0:ROWS, :], ident[0:ROWS, 0:ROWS]).then_inc(par_T.sem, 1)
                    for b in range(HB):
                        for k in range(KT):
                            mm = t.matmul(pm[:, b * HEADS:(b + 1) * HEADS], block_of(xnT, k, b), wdt[:, k, :],
                                          start=(k == 0), stop=(k == KT - 1))
                    mm.then_inc(dt_proj.sem, 1)
                    for u in range(U_OUT):
                        if u >= 2:
                            reader = [gc_in, hc_done, yc_done, z_done, xbc_cp][(u - 2) // 2]
                            t.wait_ge(reader.sem, reader.at(turn, (u - 2) % 2 + 1))
                        tiles_unit(u)
                        if u in (6, 7):
                            i = u - 6
                            t.wait_ge(sq_done.sem, sq_done.at(turn, i + 1))
                            for b in range(HB):
                                for m in range(TPU):
                                    mm = t.matmul(pm[:, SUMS + i * HB + b:SUMS + i * HB + b + 1], block_of(etmp, m, b),
                                                  ones[:, 0:1], start=(m == 0), stop=(m == TPU - 1))
                            mm.then_inc(sq_used.sem, 1)
                    t.wait_ge(a_done.sem, a_done.at(turn, 1))
                    for b in range(HB):
                        t.matmul(pm[:, b * 2 * HEADS:(b * 2 + 1) * HEADS], causalT[:, :], a_[:, b, :], start=True, stop=True)
                        mm = t.matmul(pm[:, (b * 2 + 1) * HEADS:(b * 2 + 2) * HEADS], ones[:, :], a_[:, b, :], start=True, stop=True)
                    mm.then_inc(acum_mm.sem, 1)
                    t.wait_ge(acum_cp.sem, acum_cp.at(turn, 1))
                    t.wait_ge(silu_done.sem, silu_done.at(turn, XT // TPU))
                    etf = etmp[:, :, :].rearrange("p a b -> p (a b)")
                    for i in range(4):
                        b, g = divmod(i, 2)
                        if i:
                            t.wait_ge(g_act.sem, g_act.at(turn, i))
                        t.matmul(pm[:, P:2 * P], block_of(xc, KT + g, b), block_of(xc, KT + 2 + g, b), start=True, stop=True)
                        t.transpose(pm[:, 2 * P:3 * P], block_of(xc, KT + g, b), ident[:, :])
                        for m in range(TPU):
                            t.transpose(px[:, m * P:(m + 1) * P], block_of(xc, g * TPU + m, b), ident[:, :])
                        for k in range(HG):
                            col = a_[:, b, g * HG + k:g * HG + k + 1].to_broadcast([P, P])
                            mm = t.matmul(ppf[:, k * P:(k + 1) * P], col, causalT[:, :], start=True, stop=True)
                        mm.then_inc(g_mm.sem, 1)
                        t.wait_ge(g_mats.sem, g_mats.at(turn, i + 1))
                        if i:
                            t.wait_ge(g_used.sem, g_used.at(turn, i))
                        for k in range(HG):
                            y = ppf[(k % 2) * HD:(k % 2 + 1) * HD, 2 * NW + (k // 2) * P:2 * NW + (k // 2 + 1) * P]
                            t.matmul(y, xdt[:, k, :], decay[:, k, :], start=True, stop=False)
                            t.matmul(y, state[:, g * HG + k, :], c_dec[:, k, :], start=False, stop=True)
                        t.matmul(ppf[:, 3 * NW:4 * NW], b_tok[:, :], xdtd.rearrange("p a b -> p (a b)"), start=True,
                                 stop=True).then_inc(g_y.sem, 1)
                    for b in range(HB):
                        t.wait_ge(sq_done.sem, sq_done.at(turn, 2 + b + 1))
                        for m in range(KT):
                            mm = t.matmul(pm[:, SUMS + 2 * HB + b:SUMS + 2 * HB + b + 1], etf[:, m * P:(m + 1) * P],
                                          ones[:, 0:1], start=(m == 0), stop=(m == KT - 1))
                        mm.then_inc(sq_used.sem, 1)
                    t.wait_ge(y_scaled.sem, y_scaled.at(turn, 2))
                    for i in range(4):
                        n, g = divmod(i, 2)
                        if i >= 2:
                            t.wait_ge(out_used.sem, out_used.at(turn, i - 1))
                        rows_unit(U_OUT + i, lambda k, b: block_of((yc, ys)[g], k, b), KT)
                    norm_T(1)
                    for i in range(4):
                        if i >= 2:
                            t.wait_ge(qT_cp.sem, qT_cp.at(turn, i - 1))
                        tiles_unit(U_Q + i)
                    t.wait_ge(keys_in.sem, keys_in.at(turn, 16))
                    for i in range(J // 4):
                        if i:
                            t.wait_ge(keysT_cp.sem, keysT_cp.at(turn, i))
                        for m in range(4):
                            mm = t.transpose(px[:, m * P:(m + 1) * P], keys[:, i * 4 + m, :], ident[:, :])
                        mm.then_inc(keysT_tr.sem, 1)
                    t.wait_ge(qT_cp.sem, qT_cp.at(turn, 4))
                    t.wait_ge(keysT_cp.sem, keysT_cp.at(turn, 4))
                    for b in range(HB):
                        if b:
                            t.wait_ge(score_cp.sem, score_cp.at(turn, b))
                        for j in range(J):
                            mm = t.matmul(ppf[:, j * KEYS:(j + 1) * KEYS], block_of(qT, j, b), keysT[:, j, :], start=True, stop=True)
                        mm.then_inc(score_mm.sem, 1)
                    for b in range(HB):
                        t.wait_ge(eidx_done.sem, eidx_done.at(turn, b + 1))
                        t.transpose(px[:, 0:P], eidx[:, :], ident[:, :]).then_inc(eidxT_tr.sem, 1)
                    t.wait_ge(w_done.sem, w_done.at(turn, 1))
                    for b in range(HB):
                        mm = t.transpose(px[:, b * P:(b + 1) * P], gl[:, b, :], ident[:, :])
                    mm.then_inc(wT_tr.sem, 1)
                    t.wait_ge(wT_cp.sem, wT_cp.at(turn, 1))
                    t.sem_inc(held, 1)
                    for b in range(HB):
                        if b:
                            t.wait_ge(oT_cp.sem, oT_cp.at(turn, b))
                            t.sem_inc(held, 1)
                        with t.Fori(0, P // BODY) as i:
                            for r in range(BODY):
                                tok = i * BODY + r
                                t.wait_ge(s_row[r % RING],
                                          (turn * ROWS_PER_TURN + i * 2 + (T // RING + b * P // RING + r // RING + 1)) * 16)
                                for d in range(KT):
                                    mm = t.matmul(pv[:, d, bass.ds(tok, 1)], ring[:, r % RING, d * P:(d + 1) * P],
                                                  wT[:, b, bass.ds(tok, 1)], start=True, stop=True)
                                mm.then_inc(v_used.sem, 1)
                    for b in range(HB):
                        t.wait_ge(oT_cp.sem, oT_cp.at(turn, b + 1))
                        for m in range(KT):
                            mm = t.transpose(ppf[:, b * D + m * P:b * D + (m + 1) * P], etf[:, m * P:(m + 1) * P], ident[:, :])
                        mm.then_inc(o_tr.sem, 1)
                    t.wait_ge(p_in.sem, p_in.at(turn, 16))
                    for b in range(HB):
                        for k in range(PT):
                            m_ = b * PT + k
                            mm = t.transpose(px[:, m_ * P:(m_ + 1) * P], ptok[:, b, k * P:(k + 1) * P], ident[:, :])
                    mm.then_inc(pT_tr.sem, 1)
                    norm_T(2)
                    t.wait_ge(pT_cp.sem, pT_cp.at(turn, 1))
                    for n in range(2):
                        if n:
                            t.wait_ge(pg_exp.sem, pg_exp.at(turn, n))
                        rows_unit(U_PLE + 2 * n, lambda k, b: block_of(xnT, k, b), KT)
                        if n:
                            t.wait_ge(pg_used.sem, pg_used.at(turn, n))
                        rows_unit(U_PLE + 2 * n + 1, lambda k, b: pT[:, b * PT + k, :], PT)
                    turn_barrier(t, turn)


_INS = ['x', 'p', 'norm_mix_w', 'w_in', 'conv_w', 'mconv_w', 'mconv_b', 'dt_bias', 'a_log', 'd_skip', 'conv_norm_w',
        'ssd_norm_w', 'w_out', 'norm_ffn_w', 'peer_wq', 'peer_keys', 'peer_u', 'peer_v', 'norm_ple_w', 'w_ple_gate',
        'w_ple', 'final_norm_w']


def kernel(**inputs):
    import numpy as _np
    import concourse.bacc as _bacc
    from concourse import mybir as _mybir
    from concourse.bass_utils import run_bass_kernel_spmd as _run

    nc = _bacc.Bacc("TRN2", target_bir_lowering=False, num_devices=1)
    arrays, args = {}, []
    for name in _INS:
        a = _np.ascontiguousarray(inputs[name])
        arrays[f"in_{name}_dram"] = a
        args.append(nc.dram_tensor(f"in_{name}_dram", a.shape, _mybir.dt.from_np(a.dtype), kind="ExternalInput").ap())
    shape = inputs["x"].shape
    args.append(nc.dram_tensor("out_0_dram", shape, _mybir.dt.float32, kind="ExternalOutput").ap())
    trunk(nc, *args)
    r = _run(nc, [arrays], core_ids=[0])
    return r.results[0]["out_0_dram"]
```

```python
from contextlib import ExitStack

import concourse.bass as bass
from concourse import mybir

F32 = mybir.dt.float32
I32 = mybir.dt.int32
U32 = mybir.dt.uint32
ALU = mybir.AluOpType
ACT = mybir.ActivationFunctionType
AX = mybir.AxisListType

P = 128
EPS = 1e-6
NEG = -3.0e38
GELU_C = 0.7978845608028654
GELU_A = 0.044715
TOP_STAGES = 12
VEC_PER_ROUND = 399
SCA_PER_ROUND = 8


class Signal:

    def __init__(self, sem, per_turn, early=None, head=0):
        self.sem, self.per_turn, self.head = sem, per_turn, head
        self.early = per_turn if early is None else early

    def at(self, turn, n):
        if isinstance(turn, int):
            return min(turn, 2) * self.early + max(turn - 2, 0) * self.per_turn + n + self.head
        return turn * self.per_turn + (2 * self.early - 2 * self.per_turn + n + self.head)


class Steps:

    def __init__(self, per_round):
        self.n, self.per_round = 0, per_round

    def one(self):
        self.n += 1
        return 1

    def so_far(self, turn):
        if isinstance(turn, int):
            return self.n
        return turn * self.per_round + (self.n - 2 * self.per_round)


def expert_rows():
    out, slot = [], 0
    count = {"u": 0, "vector": 0, "tensor": 0}

    def row(kind, b, k):
        nonlocal slot
        who = "u" if kind == "u" else ("vector" if (k % 4 == 3 if b == 0 else k % 2 == 1) else "tensor")
        count[who] += 1
        out.append((who, b, k, slot, count[who]))
        slot += 1

    lead = 12
    for k in range(P):
        row("u", 0, k)
    out.append(("w1", 0, 0, 0, 0))
    for k in range(2):
        row("u", 1, k)
    out.append(("w2", 0, 0, 0, 0))
    for k in range(2, lead):
        row("u", 1, k)
    for k in range(lead, P):
        row("u", 1, k)
        row("v", 0, k - lead)
    out.append(("w1", 1, 0, 0, 0))
    for k in range(P - lead, P - lead + 2):
        row("v", 0, k)
    out.append(("w2", 1, 0, 0, 0))
    for k in range(P - lead + 2, P):
        row("v", 0, k)
    out.append(("add", 0, 0, 0, 0))
    for k in range(P):
        row("v", 1, k)
    out.append(("add", 1, 0, 0, 0))
    return out, count


def schedule(entries, stages):
    total = sum(w for _, w in stages)
    upto, done = {}, 0.0
    for name, w in stages:
        done += w
        upto[name] = round(entries * done / total)
    return upto


def over(ap, axis, n):
    a = ap.unsqueeze(axis)
    shape = list(a.shape)
    shape[axis] = n
    return a.to_broadcast(shape)


def trunk(nc, x, p, norm_mix_w, w_in, conv_w, mconv_w, mconv_b, dt_bias, a_log, d_skip, conv_norm_w,
          ssd_norm_w, w_out, norm_ffn_w, peer_wq, peer_keys, peer_u, peer_v, norm_ple_w, w_ple_gate,
          w_ple, final_norm_w, out):
    D = x.shape[2]
    SEQ = x.shape[1]
    DEPTH = p.shape[0]
    KT = D // P
    NBLK = SEQ // P
    HB = 2
    HALVES = NBLK // HB
    T = HB * P
    D_IN = w_in.shape[2]
    HEADS = dt_bias.shape[1]
    HD = D // HEADS
    HG = HEADS // 2
    CONV_K, MCONV_K = conv_w.shape[1], mconv_w.shape[1]
    XT = mconv_b.shape[1] // P
    PH, KEYS, EXPERTS = peer_keys.shape[1], peer_keys.shape[3], peer_u.shape[1]
    TOPK = 16
    J = 2 * PH
    assert SEQ == 2 * T and DEPTH == 2
    SLOTS = PH * TOPK
    PLE = p.shape[3]
    PT = PLE // P
    NW = 512
    TPU = NW // P

    IN_COLS = [D, D + NW, 2 * D, 2 * D + NW, 0, NW, 3 * D, 3 * D + NW] + [4 * D + NW * i for i in range(XT // TPU)]
    U_IN = 0
    U_OUT = len(IN_COLS)
    U_Q = U_OUT + 4
    U_PLE = U_Q + 4
    UNITS = U_PLE + 4
    EVEN = U_PLE - U_PLE // 2
    ODD = U_PLE // 2

    R_CONV = 0
    R_MCONV = R_CONV + CONV_K * KT
    R_MB = R_MCONV + MCONV_K * XT
    R_CN = R_MB + XT
    R_SN = R_CN + KT
    ROWS = R_SN + KT

    SMALL = 16 * 9

    RING = 8
    SUMS = 448
    BODY = 2 * RING

    entries, n_rows = expert_rows()
    tensor_rows = [sum(e[0] == "tensor" and e[1] <= b for e in entries) for b in range(HB)]
    vector_rows = [sum(e[0] == "vector" and e[1] <= b for e in entries) for b in range(HB)]
    diag_groups = [(0, 4 * q, 1, 3) for q in range(P // 4)] + [(1, 8 * q, 2, 4) for q in range(P // 8)]
    group_of, group_end, at = {}, [], 0
    for q, (gb_, k0, st, n) in enumerate(diag_groups):
        for j in range(n):
            group_of[gb_, k0 + st * j] = (q, j)
        at += n
        group_end.append(at)

    embed_stages = [("e_norm.a", 5), ("e_norm.b", 5), ("e_norm.c", 4), ("e0.0", 7), ("e0.1", 7), ("e1", 4), ("e2.0", 7), ("e2.1", 7), ("e3", 4), ("e4", 6)]
    mix_stages = [("norm0.a", 5), ("norm0.b", 5), ("norm0.c", 4), ("dt", 3)] + [(f"in{u}.{m}", 3.6) for u in range(U_OUT) for m in range(TPU)]
    mix_stages += [("cum0", 4), ("cum1", 4)] + [(f"ssd{i}{x}", w) for i in range(4) for x, w in (("a", 6), ("b", 6), ("c", 5))]
    mix_stages += [("post0", 4), ("post1", 4)] + [(f"out{i}.{b}", 7) for i in range(4) for b in range(HB)]
    mix_stages += [("norm1.a", 5), ("norm1.b", 5), ("norm1.c", 4)] + [(f"q{i}.{m}", 3.6) for i in range(4) for m in range(TPU)] + [("keys", 5), ("score", 5)]
    mix_stages += [(f"top{b}.{j}", 5) for b in range(HB) for j in range(TOP_STAGES)] + [("end", 1)]
    UPTO = {"mix": schedule(len(entries), mix_stages), "both": schedule(len(entries), embed_stages + mix_stages),
            "embed": schedule(len(entries), embed_stages + [("end", 300)])}

    with ExitStack() as c:
        def sb(name, shape, dt=F32):
            return c.enter_context(nc.sbuf_tensor(name, shape, dt))

        def ps(name, shape):
            return c.enter_context(nc.psum_tensor(name, shape, F32))

        def sem(name):
            return c.enter_context(nc.semaphore(name))

        h = sb("h", [P, NBLK, D])
        wbuf = sb("wbuf", [P, 2, KT, NW])
        wdt = sb("wdt", [P, KT, HEADS])
        xf = sb("xf", [P, HB, D])
        xnT = sb("xnT", [P, KT, T])
        conv_past = sb("conv_past", [P, KT, CONV_K - 1])
        xbc_past = sb("xbc_past", [P, XT, MCONV_K - 1])
        gain = sb("gain", [P, D])
        params = sb("params", [P, P])
        paramsT = sb("paramsT", [P, P])
        dskip = sb("dskip", [P, KT])
        etmp = sb("etmp", [P, TPU, T])
        state = sb("state", [P, HEADS, HD])
        ring = sb("ring", [P, RING, D])
        junk = sb("junk", [P, 2, D])
        CONV_IN = KT * (CONV_K - 1 + T)
        XBC_IN = XT * (MCONV_K - 1 + T)
        arena = sb("arena", [P, 12 * D + CONV_IN + XBC_IN])

        def region(k0, shape):
            n = 1
            for s in shape:
                n *= s
            flat = arena[:, k0 * D:k0 * D + n]
            if len(shape) == 1:
                return flat
            names = "abc"[:len(shape)]
            sizes = {names[i]: shape[i] for i in range(1, len(shape))}
            return flat.rearrange(f"p ({' '.join(names)}) -> p {' '.join(names)}", **sizes)

        xtmp = region(2, [HB, D])
        conv_in = arena[:, 12 * D:12 * D + CONV_IN].rearrange("p (a b) -> p a b", a=KT)
        xbc_in = arena[:, 12 * D + CONV_IN:12 * D + CONV_IN + XBC_IN].rearrange("p (a b) -> p a b", a=XT)
        yc = region(0, [KT, T])
        zs = region(2, [KT, T])
        ys = region(4, [KT, T])
        xc = region(6, [XT, T])
        decay = region(9, [HG, P])
        c_dec = region(10, [HG, P])
        xdt = region(11, [HG, HD])
        xdtd = arena[:, 11 * D + NW:12 * D].rearrange("p (a b) -> p a b", b=HD)
        qT = region(0, [J, T])
        xfn = region(12, [HB, D])
        cand = region(0, [PH * TOPK, TOPK]).rearrange("p (h a) b -> p h a b", a=TOPK)
        keys = region(4, [J, P])
        keysT = region(6, [J, P])
        sc = region(8, [J, KEYS])
        sc2 = region(10, [J, KEYS])
        cand2 = region(4, [PH, TOPK * TOPK])
        hot = region(10, [SLOTS, TOPK])

        ident = sb("ident", [P, P])
        causalT = sb("causalT", [P, P])
        ones = sb("ones", [P, P])
        iota_i = sb("iota_i", [P, TOPK], I32)
        iota_f = sb("iota_f", [P, TOPK])
        ss = sb("ss", [P, HB])
        rstd = sb("rstd", [P, HB])
        ss2 = sb("ss2", [P, HB, 2])
        sums = sb("sums", [P, 3 * HB])
        fin = sb("fin", [P, 2, NBLK])
        rstd2 = sb("rstd2", [P, HB, 2])
        dall = sb("dall", [P, HEADS])
        dtb = sb("dtb", [P, HEADS])
        alog = sb("alog", [P, HEADS])
        expa = sb("expa", [P, HEADS])
        dts = sb("dts", [P, 6, HB, HEADS])
        dt = sb("dt", [P, HB, HEADS])
        a_ = sb("a_", [P, HB, HEADS])
        acum = sb("acum", [P, HB, 2, HEADS])
        d_in = sb("d_in", [P, HB, HEADS])
        d_chunk = sb("d_chunk", [P, HB, HEADS])
        cbm = sb("cbm", [P, P])
        b_tok = sb("b_tok", [P, P])
        sv = sb("sv", [P, J, TOPK])
        si = sb("si", [P, J, TOPK], U32)
        sif = sb("sif", [P, J, TOPK])
        tv = sb("tv", [P, PH, TOPK])
        ti = sb("ti", [P, PH, TOPK], U32)
        tq = sb("tq", [P, 2, SLOTS], U32)
        tqf = region(8, [2, SLOTS])
        ei = region(9, [2, SLOTS])
        eidx = sb("eidx", [P, SLOTS])
        idx_u = sb("idx_u", [P, HB, SLOTS], I32)
        gsum = sb("gsum", [P, PH])
        gate = sb("gate", [P, HB, SLOTS])
        act = sb("act", [P, HB, SLOTS])
        gl = sb("gl", [P, HB, SLOTS])
        idx_c = sb("idx_c", [P, HB, SLOTS], I32)
        gate_c = sb("gate_c", [P, HB, SLOTS])
        diag = sb("diag", [P, 2, 4, P])
        pT = region(0, [HB * PT, P])
        ptok = region(1, [HB, PLE])

        pp = ps("pp", [P, 2, 2, NW])
        px = ps("px", [P, NW])
        pm = ps("pm", [P, NW])
        pv = ps("pv", [P, D])
        ppt = pp[:, :, :, :].rearrange("p a b (c t) -> p a (b c) t", t=T)
        ppf = pp[:, :, :, :].rearrange("p a b n -> p (a b n)")
        pxt = px[:, :].rearrange("p (a b) -> p a b", b=P)

        s_const = sem("s_const")
        s_hload = sem("s_hload")
        w_in_sem = [Signal(sem("s_w_even"), 16 * (EVEN + 2), 16 * EVEN), Signal(sem("s_w_odd"), 16 * (ODD + 2), 16 * ODD)]
        small = Signal(sem("s_small"), SMALL)
        gains = Signal(sem("s_gain"), 16 * 3, early=16 * 2)
        keys_in = Signal(sem("s_keys"), 16)
        p_in = Signal(sem("s_p"), 16, early=0)
        sumsq = Signal(sem("s_sumsq"), 3, early=2)
        meansq = Signal(sem("s_meansq"), 3, early=2)
        rstds = Signal(sem("s_rstd"), 3, early=2)
        xns = Signal(sem("s_xn"), 6, early=4)
        tr_done = Signal(sem("s_transposed"), 6, early=4)
        xnT_done = Signal(sem("s_xnT"), 6, early=4)
        par_T = Signal(sem("s_params_transposed"), 1)
        par_done = Signal(sem("s_params"), 1)
        proj = Signal(sem("s_proj"), UNITS, early=UNITS - 4, head=1)
        hc_done = Signal(sem("s_hc"), 2)
        out_used = Signal(sem("s_out_used"), 4)
        expa_done = Signal(sem("s_expa"), 1)
        gc_in = Signal(sem("s_gc"), 2)
        z_exp = Signal(sem("s_z_exp"), 2)
        z_done = Signal(sem("s_z_done"), 2)
        xbc_cp = Signal(sem("s_xbc_copied"), XT // TPU)
        conv_done = Signal(sem("s_xbc_conv"), XT // TPU)
        silu_exp = Signal(sem("s_silu_exp"), XT // TPU)
        silu_done = Signal(sem("s_silu_done"), XT // TPU)
        yc_done = Signal(sem("s_yc"), 2)
        sq_done = Signal(sem("s_square"), 4)
        sq_used = Signal(sem("s_square_used"), 4)
        y_scaled = Signal(sem("s_y_scaled"), 2)
        dt_proj = Signal(sem("s_dt_proj"), 1)
        dt_raw = Signal(sem("s_dt_raw"), 1)
        dt_exp = Signal(sem("s_dt_exp"), 1)
        dt_ln = Signal(sem("s_dt_ln"), 1)
        dt_u = Signal(sem("s_dt_u"), 1)
        a_done = Signal(sem("s_a"), 1)
        acum_mm = Signal(sem("s_acum_mm"), 1)
        acum_cp = Signal(sem("s_acum"), 1)
        d_raw = Signal(sem("s_decay_raw"), 1)
        d_exp = Signal(sem("s_decay_exp"), 1)
        g_mm = Signal(sem("s_ssd_inputs"), 4)
        g_cbm = Signal(sem("s_cb_masked"), 4)
        g_x = Signal(sem("s_xdt"), 4)
        g_cdec = Signal(sem("s_decay_out"), 4)
        g_dif = Signal(sem("s_decay_diff"), 4)
        g_act = Signal(sem("s_decay_mats"), 4)
        g_mats = Signal(sem("s_ssd_mats"), 4)
        g_y = Signal(sem("s_ssd_y"), 4)
        g_used = Signal(sem("s_ssd_used"), 4)
        ys_done = Signal(sem("s_ys"), 2)
        ss2_ms = Signal(sem("s_ss2_ms"), 1)
        rstd2s = Signal(sem("s_rstd2"), 1)
        keysT_tr = Signal(sem("s_keysT_tr"), 4)
        keysT_cp = Signal(sem("s_keysT"), 4)
        qT_cp = Signal(sem("s_qT"), 4)
        score_mm = Signal(sem("s_scores_mm"), 2)
        score_cp = Signal(sem("s_scores"), 2)
        tv_sub = Signal(sem("s_gate_raw"), 2)
        tv_exp = Signal(sem("s_gate_exp"), 2)
        eidx_done = Signal(sem("s_eidx"), 2)
        idx_done = Signal(sem("s_idx"), 2)
        s_row = [sem(f"s_row{r}") for r in range(RING)]
        ROWS_PER_TURN = 2 * T // RING
        handed = Signal(sem("s_handed"), 1)
        used = {"u": Signal(sem("s_u_used"), n_rows["u"]), "vector": Signal(sem("s_v_added"), n_rows["vector"]),
                "tensor": Signal(sem("s_v_multiplied"), n_rows["tensor"])}
        gelu_raw = Signal(sem("s_gelu_raw"), 2)
        gelu_exp = Signal(sem("s_gelu_exp"), 2)
        w_done = Signal(sem("s_weights"), 2)
        diag_done = Signal(sem("s_diag"), len(diag_groups))
        added = Signal(sem("s_block_added"), 2)
        held = sem("s_held")
        pT_tr = Signal(sem("s_pT_tr"), 1, early=0)
        pT_cp = Signal(sem("s_pT"), 1, early=0)
        pg_exp = Signal(sem("s_ple_exp"), 2, early=0)
        pg_used = Signal(sem("s_ple_exp_used"), 2, early=0)
        turn_end = sem("s_turn_end")
        s_vec = sem("s_vector_step")
        s_sca = sem("s_scalar_step")
        s_fin = sem("s_final")
        s_finsq = sem("s_final_sumsq")
        s_out = sem("s_out")

        def turn_barrier(eng, turn):
            eng.drain()
            eng.sem_inc(turn_end, 1)
            eng.wait_ge(turn_end, (turn + 1) * 5)
            eng.sem_inc(held, 1)

        x_v = x.rearrange("o (b p) d -> p (o b) d", p=P)
        out_v = out.rearrange("o (b p) d -> p (o b) d", p=P)
        p_v = p.rearrange("l o (b p) k -> p (l o b) k", p=P)
        win_v = w_in.rearrange("l (k p) n -> p (l k) n", p=P)
        wout_v = w_out.rearrange("l (k p) n -> p (l k) n", p=P)
        wq_v = peer_wq.rearrange("l (k p) n -> p (l k) n", p=P)
        wg_v = w_ple_gate.rearrange("l (k p) n -> p (l k) n", p=P)
        wp_v = w_ple.rearrange("l (k p) n -> p (l k) n", p=P)
        keys_v = peer_keys.rearrange("l h s (a q) d -> (l h s a) (q d)", q=J)
        rows = [(R_CONV, CONV_K * KT, conv_w.rearrange("l j (c p) -> (l j c) p", p=P)),
                (R_MCONV, MCONV_K * XT, mconv_w.rearrange("l j (c p) -> (l j c) p", p=P)),
                (R_MB, XT, mconv_b.rearrange("l (c p) -> (l c) p", p=P)),
                (R_CN, KT, conv_norm_w.rearrange("l (c p) -> (l c) p", p=P)),
                (R_SN, KT, ssd_norm_w.rearrange("l (c p) -> (l c) p", p=P))]
        u_rows = peer_u.rearrange("l e d -> (l e) d")
        v_rows = peer_v.rearrange("l e d -> (l e) d")

        block = c.enter_context(nc.Block())

        @block.sync
        def _(sp):
            def stream(src, par, turn, pos):
                if pos >= 2:
                    sp.wait_ge(proj.sem, proj.at(turn, pos - 1))
                    sp.sem_inc(held, 1)
                sp.dma_start(wbuf[:, par, 0:src.shape[1], :], src).then_inc(w_in_sem[par].sem, 16)

            def load_gain(row):
                sp.dma_start(gain[:, :], row.to_broadcast([P, D])).then_inc(gains.sem, 16)

            def embed(turn, half, layer, pos0):
                load_gain(norm_ple_w[layer:layer + 1, :])
                sp.dma_start(ptok[:, :, :], p_v[:, bass.ds(half * HB + layer * NBLK, HB), :]).then_inc(p_in.sem, 16)
                for i in range(4):
                    n, g = divmod(i, 2)
                    view, kt = ((wg_v, KT), (wp_v, PT))[g]
                    stream(view[:, layer * kt:(layer + 1) * kt, n * NW:(n + 1) * NW], i % 2, turn, pos0 + i)

            def mix(turn, half, layer, early):
                pos0 = 0 if early else 4
                norms = 0 if early else 1

                def load_unit(u):
                    if u < U_OUT:
                        src = win_v[:, layer * KT:(layer + 1) * KT, IN_COLS[u]:IN_COLS[u] + NW]
                    elif u < U_Q:
                        n, g = divmod(u - U_OUT, 2)
                        src = wout_v[:, (2 * layer + g) * KT:(2 * layer + g + 1) * KT, n * NW:(n + 1) * NW]
                    else:
                        n = u - U_Q
                        src = wq_v[:, layer * KT:(layer + 1) * KT, n * NW:(n + 1) * NW]
                    stream(src, u % 2, turn, pos0 + u)

                if not early:
                    sp.wait_ge(xns.sem, xns.at(turn, 2))
                    sp.sem_inc(held, 1)
                load_gain(norm_mix_w[layer:layer + 1, :])
                load_unit(0)
                for r0, n, view in rows:
                    sp.dma_start(params[r0:r0 + n, :], view[layer * n:(layer + 1) * n, :]).then_inc(small.sem, 16)
                sp.dma_start(wdt[:, :, :], win_v[:, layer * KT:(layer + 1) * KT, D_IN - HEADS:D_IN]).then_inc(small.sem, 16)
                sp.dma_start(dtb[:, :], dt_bias[layer:layer + 1, :].to_broadcast([P, HEADS])).then_inc(small.sem, 16)
                sp.dma_start(alog[:, :], a_log[layer:layer + 1, :].to_broadcast([P, HEADS])).then_inc(small.sem, 16)
                sp.dma_start(dall[:, :], d_skip[layer:layer + 1, :].to_broadcast([P, HEADS])).then_inc(small.sem, 16)
                for u in range(1, U_OUT):
                    load_unit(u)
                sp.wait_ge(xns.sem, xns.at(turn, norms * HB + 2))
                sp.sem_inc(held, 1)
                load_gain(norm_ffn_w[layer:layer + 1, :])
                for u in range(U_OUT, U_Q):
                    load_unit(u)
                sp.wait_ge(out_used.sem, out_used.at(turn, 4))
                sp.sem_inc(held, 1)
                sp.dma_start(keys.rearrange("p q d -> p (q d)"), keys_v[layer * P:(layer + 1) * P, :]).then_inc(keys_in.sem, 16)
                for u in range(U_Q, U_PLE):
                    load_unit(u)

            sp.dma_start(h[:, :, :], x_v).then_inc(s_hload, 16)
            for turn in range(HALVES):
                mix(turn, turn, 0, True)
                turn_barrier(sp, turn)
            with sp.Fori(0, HALVES) as half:
                turn = half + HALVES
                embed(turn, half, 0, 0)
                mix(turn, half, 1, False)
                turn_barrier(sp, turn)
            turn = 2 * HALVES
            embed(turn, 0, 1, 0)
            turn_barrier(sp, turn)
            embed(turn, 1, 1, 4)
            sp.wait_ge(xns.sem, xns.at(turn, 4))
            load_gain(final_norm_w.rearrange("(o d) -> o d", o=1))
            for b in range(NBLK):
                sp.wait_ge(s_fin, b + 1)
                sp.dma_start(out_v[:, b, :], ring[:, b, :]).then_inc(s_out, 16)
            sp.wait_ge(s_out, 16 * NBLK)

        @block.gpsimd
        def _(g):
            g.memset(ident[:, :], 0.0).then_inc(s_const, 1)
            g.memset(ones[:, :], 1.0).then_inc(s_const, 1)
            g.iota(iota_i[:, :], pattern=[[1, TOPK]], base=0, channel_multiplier=0).then_inc(s_const, 1)
            g.wait_ge(s_const, 3)
            g.affine_select(out=ident[:, :], in_=ident[:, :], compare_op=ALU.not_equal, fill=1.0, base=0,
                            pattern=[[-1, P]], channel_multiplier=1).then_inc(s_const, 1)
            g.affine_select(out=causalT[:, :], in_=ones[:, :], compare_op=ALU.is_ge, fill=0.0, base=0,
                            pattern=[[1, P]], channel_multiplier=-1).then_inc(s_const, 1)

            g.wait_ge(s_const, 5)
            turn_barrier(g, 0)
            with g.Fori(0, 2 * HALVES) as bgt:
                g.wait_ge(handed.sem, handed.at(bgt, 1))
                g.sem_inc(held, 1)
                consumer = {}
                for who, b, k, slot, nth in entries:
                    if who not in used:
                        continue
                    if who == "tensor" and group_of[b, k][1] == 0:
                        q = group_of[b, k][0]
                        _, k0, st, n = diag_groups[q]
                        if q in (0, P // 4):
                            g.wait_ge(w_done.sem, w_done.at(bgt, b + 1))
                        if q >= 2:
                            g.wait_ge(used["tensor"].sem, used["tensor"].at(bgt, group_end[q - 2]))
                        g.sem_inc(held, 1)
                        g.tensor_tensor(diag[:, q % 2, 0:n, :], over(ident[:, :], 1, n),
                                        over(gl[:, b, k0:k0 + st * (n - 1) + 1:st], 2, P), ALU.mult).then_inc(diag_done.sem, 1)
                    if slot >= RING:
                        last, count = consumer[slot - RING]
                        g.wait_ge(used[last].sem, used[last].at(bgt, count))
                        g.sem_inc(held, 1)
                    consumer[slot] = (who, nth)
                    g.indirect_dma_start(
                        out=ring[:, slot % RING, :], out_offset=None, in_=u_rows if who == "u" else v_rows,
                        in_offset=bass.IndirectOffsetOnAxis(ap=idx_c[:, b, k:k + 1], axis=0),
                    ).then_inc(s_row[slot % RING], 16)
                turn_barrier(g, bgt + 1)

        @block.scalar
        def _(s):
            own = Steps(SCA_PER_ROUND)

            def idle(stage):
                pass

            def follow(kind, bgt):
                done = [0]

                def background(stage):
                    for who, b, k, slot, nth in entries[done[0]:UPTO[kind][stage]]:
                        if who == "w1":
                            s.wait_ge(gelu_raw.sem, gelu_raw.at(bgt, b + 1))
                            s.activation(gl[:, b, :], gl[:, b, :], ACT.Exp, scale=-2.0 * GELU_C).then_inc(gelu_exp.sem, 1)
                    done[0] = UPTO[kind][stage]

                return background

            def norm(turn, half, n, name, background):
                for b in range(HB):
                    hb = h[:, bass.ds(half * HB + b, 1), :].rearrange("p o d -> p (o d)")
                    m = s.activation(etmp[:, 0:4, :].rearrange("p a b -> p (a b)"), hb, ACT.Square,
                                     accum_out=ss[:, b:b + 1])
                    if b == HB - 1:
                        m.then_inc(sumsq.sem, 1)
                    else:
                        m.then_inc(s_sca, own.one())
                        s.wait_ge(s_sca, own.so_far(turn))
                        s.sem_inc(held, 1)
                background(name + ".b")
                s.wait_ge(meansq.sem, meansq.at(turn, n + 1))
                s.activation(rstd[:, :], ss[:, :], ACT.Ln).then_inc(s_sca, own.one())
                s.wait_ge(s_sca, own.so_far(turn))
                s.activation(rstd[:, :], rstd[:, :], ACT.Exp, scale=-0.5).then_inc(rstds.sem, 1)
                background(name + ".c")
                for b in range(HB):
                    s.wait_ge(tr_done.sem, tr_done.at(turn, n * HB + b + 1))
                    s.copy(xnT[:, :, b * P:(b + 1) * P],
                           ppf[:, b * D:(b + 1) * D].rearrange("p (a b) -> p a b", b=P)).then_inc(xnT_done.sem, 1)

            def embed(turn, half, n0, pos0, background):
                background("e_norm.a")
                if n0:
                    s.wait_ge(pg_used.sem, pg_used.at(turn, 2 * n0))
                    s.sem_inc(held, 1)
                norm(turn, half, n0, "e_norm", background)
                s.wait_ge(pT_tr.sem, pT_tr.at(turn, n0 + 1))
                s.copy(pT, pxt).then_inc(pT_cp.sem, 1)
                for n in range(2):
                    background(f"e{2 * n}.1")
                    s.wait_ge(proj.sem, proj.at(turn, pos0 + 2 * n + 1))
                    if n:
                        s.wait_ge(pg_used.sem, pg_used.at(turn, 2 * n0 + n))
                    else:
                        s.wait_ge(xnT_done.sem, xnT_done.at(turn, 2 * n0 + 2))
                    s.activation(etmp[:, :, :].rearrange("p a b -> p (a b)"), pp[:, 0].rearrange("p a b -> p (a b)"),
                                 ACT.Exp, scale=-1.0).then_inc(pg_exp.sem, 1)

            def mix(turn, half, early, background):
                pos0 = 0 if early else 4
                n0 = 0 if early else 1
                background("norm0.a")
                if not early:
                    s.wait_ge(pg_used.sem, pg_used.at(turn, 2))
                    s.sem_inc(held, 1)
                norm(turn, half, n0, "norm0", background)
                background("dt")
                s.wait_ge(par_T.sem, par_T.at(turn, 1))
                s.copy(paramsT[:, 0:ROWS], px[:, 0:ROWS]).then_inc(par_done.sem, 1)
                s.wait_ge(par_done.sem, par_done.at(turn, 1))
                s.wait_ge(small.sem, small.at(turn, SMALL))
                s.activation(expa[:, :], alog[:, :], ACT.Exp).then_inc(expa_done.sem, 1)
                s.wait_ge(dt_raw.sem, dt_raw.at(turn, 1))
                s.activation(dts[:, 2], dts[:, 1], ACT.Exp, scale=-1.0).then_inc(dt_exp.sem, 1)
                s.wait_ge(dt_u.sem, dt_u.at(turn, 1))
                s.activation(dts[:, 4], dts[:, 3], ACT.Ln).then_inc(dt_ln.sem, 1)
                for i in range(2):
                    background(f"in{i}.3")
                    s.wait_ge(proj.sem, proj.at(turn, pos0 + i + 1))
                    s.copy(conv_in[:, i * TPU:(i + 1) * TPU, CONV_K - 1:], ppt[:, i % 2]).then_inc(gc_in.sem, 1)
                for i in range(2):
                    background(f"in{i + 5}.3")
                    s.wait_ge(yc_done.sem, yc_done.at(turn, i + 1))
                    if i:
                        s.wait_ge(sq_used.sem, sq_used.at(turn, i))
                    s.activation(etmp[:, :, :], yc[:, i * TPU:(i + 1) * TPU, :], ACT.Square).then_inc(sq_done.sem, 1)
                s.wait_ge(sq_done.sem, sq_done.at(turn, 2))
                for t in range(KT):
                    m = s.activation(yc[:, t, :], yc[:, t, :], ACT.Copy, scale=paramsT[:, R_CN + t:R_CN + t + 1])
                m.then_inc(y_scaled.sem, 1)
                for i in range(2):
                    background(f"in{i + 6}.3")
                    s.wait_ge(proj.sem, proj.at(turn, pos0 + 7 + i))
                    s.activation(zs[:, i * TPU:(i + 1) * TPU, :], ppt[:, i % 2], ACT.Exp, scale=-1.0).then_inc(z_exp.sem, 1)
                for i in range(XT // TPU):
                    background(f"in{i + 8}.3")
                    s.wait_ge(proj.sem, proj.at(turn, pos0 + 9 + i))
                    s.copy(xbc_in[:, i * TPU:(i + 1) * TPU, MCONV_K - 1:], ppt[:, i % 2]).then_inc(xbc_cp.sem, 1)
                    if i:
                        s.wait_ge(silu_done.sem, silu_done.at(turn, i))
                    else:
                        s.wait_ge(sq_used.sem, sq_used.at(turn, 2))
                    s.wait_ge(conv_done.sem, conv_done.at(turn, i + 1))
                    s.activation(etmp[:, :, :], xc[:, i * TPU:(i + 1) * TPU, :], ACT.Exp, scale=-1.0).then_inc(silu_exp.sem, 1)
                background("cum0")
                s.wait_ge(d_raw.sem, d_raw.at(turn, 1))
                s.activation(d_in[:, :, :], d_in[:, :, :], ACT.Exp).then_inc(s_sca, own.one())
                s.activation(d_chunk[:, :, :], acum[:, :, 1, :], ACT.Exp).then_inc(d_exp.sem, 1)
                for i in range(4):
                    background(f"ssd{i}a")
                    s.wait_ge(g_mm.sem, g_mm.at(turn, i + 1))
                    if i:
                        s.wait_ge(g_y.sem, g_y.at(turn, i))
                    s.activation(c_dec, ppf[:, 0:HG * P].rearrange("p (a b) -> p a b", b=P), ACT.Exp).then_inc(g_cdec.sem, 1)
                    background(f"ssd{i}b")
                    s.wait_ge(g_dif.sem, g_dif.at(turn, i + 1))
                    s.activation(decay, decay, ACT.Exp).then_inc(g_act.sem, 1)
                for b in range(HB):
                    background(f"post{b}")
                    s.wait_ge(ys_done.sem, ys_done.at(turn, b + 1))
                    if b:
                        s.wait_ge(sq_used.sem, sq_used.at(turn, 2 + b))
                    s.activation(etmp[:, :, :].rearrange("p a (b t) -> p (a b) t", t=P), ys[:, :, b * P:(b + 1) * P],
                                 ACT.Square).then_inc(sq_done.sem, 1)
                s.wait_ge(sq_done.sem, sq_done.at(turn, 4))
                for t in range(KT):
                    m = s.activation(ys[:, t, :], ys[:, t, :], ACT.Copy, scale=paramsT[:, R_SN + t:R_SN + t + 1])
                m.then_inc(y_scaled.sem, 1)
                s.wait_ge(ss2_ms.sem, ss2_ms.at(turn, 1))
                s.activation(rstd2[:, :, :], ss2[:, :, :], ACT.Ln).then_inc(s_sca, own.one())
                s.wait_ge(s_sca, own.so_far(turn))
                s.activation(rstd2[:, :, :], rstd2[:, :, :], ACT.Exp, scale=-0.5).then_inc(rstd2s.sem, 1)
                background("norm1.a")
                s.wait_ge(sq_used.sem, sq_used.at(turn, 4))
                s.wait_ge(out_used.sem, out_used.at(turn, 4))
                s.sem_inc(held, 1)
                norm(turn, half, n0 + 1, "norm1", background)
                for i in range(4):
                    background(f"q{i}.3")
                    s.wait_ge(proj.sem, proj.at(turn, pos0 + U_Q + i + 1))
                    s.copy(qT[:, i * TPU:(i + 1) * TPU, :], ppt[:, (U_Q + i) % 2]).then_inc(qT_cp.sem, 1)
                background("keys")
                for i in range(4):
                    s.wait_ge(keysT_tr.sem, keysT_tr.at(turn, i + 1))
                    s.copy(keysT.rearrange("d j n -> d (j n)").rearrange("d (r q) -> d q r", q=J)[:, i * 4:(i + 1) * 4, :],
                           pxt).then_inc(keysT_cp.sem, 1)
                for b in range(HB):
                    if b:
                        background(f"top{b}.0")
                        s.wait_ge(idx_done.sem, idx_done.at(turn, b))
                    else:
                        background("score")
                    s.wait_ge(score_mm.sem, score_mm.at(turn, b + 1))
                    s.copy(sc, ppf.rearrange("p (a b) -> p a b", b=P)).then_inc(score_cp.sem, 1)
                    background(f"top{b}.10")
                    s.wait_ge(tv_sub.sem, tv_sub.at(turn, b + 1))
                    s.activation(gate[:, b, :], gate[:, b, :], ACT.Exp).then_inc(tv_exp.sem, 1)
                background("end")

            s.wait_ge(s_const, 5)
            s.wait_ge(s_hload, 16)
            mix(0, 0, True, idle)
            turn_barrier(s, 0)
            s.wait_ge(handed.sem, handed.at(0, 1))
            mix(1, 1, True, follow("mix", 0))
            turn_barrier(s, 1)
            before = own.n
            with s.Fori(0, HALVES) as half:
                turn = half + HALVES
                s.wait_ge(handed.sem, handed.at(turn - 1, 1))
                s.sem_inc(held, 1)
                background = follow("both", turn - 1)
                embed(turn, half, 0, 0, background)
                mix(turn, half, False, background)
                turn_barrier(s, turn)
            assert own.n - before == SCA_PER_ROUND, f"sca_turn={own.n - before}"
            own.n += SCA_PER_ROUND
            turn = 2 * HALVES
            background = follow("embed", turn - 1)
            embed(turn, 0, 0, 0, background)
            background("end")
            turn_barrier(s, turn)
            embed(turn, 1, 1, 4, idle)
            s.wait_ge(pg_used.sem, pg_used.at(turn, 4))
            for b in range(NBLK):
                s.activation(junk[:, b % 2, :], h[:, b, :], ACT.Square, accum_out=fin[:, 0, b:b + 1]).then_inc(s_finsq, 1)
                s.wait_ge(s_finsq, b + 1)
            s.wait_ge(s_finsq, NBLK + 1)
            s.activation(fin[:, 1, :], fin[:, 1, :], ACT.Ln).then_inc(s_finsq, 1)
            s.wait_ge(s_finsq, NBLK + 2)
            s.activation(fin[:, 1, :], fin[:, 1, :], ACT.Exp, scale=-0.5).then_inc(s_finsq, 1)

        @block.vector
        def _(v):
            own = Steps(VEC_PER_ROUND)

            def h_of(half, b):
                return h[:, bass.ds(half * HB + b, 1), :].rearrange("p o d -> p (o d)")

            def h_cols(half, b, c0, n):
                return h[:, bass.ds(half * HB + b, 1), c0:c0 + n].rearrange("p o d -> p (o d)")

            def idle(stage):
                pass

            def follow(kind, bgt, bg_half, turn):
                done = [0]

                def row_in(slot):
                    v.wait_ge(s_row[slot % RING], (bgt * ROWS_PER_TURN + (slot // RING + 1)) * 16)

                def background(stage):
                    for who, b, k, slot, nth in entries[done[0]:UPTO[kind][stage]]:
                        if who == "u":
                            row_in(slot)
                            if nth > 2:
                                v.wait_ge(used["u"].sem, used["u"].at(bgt, nth - 2))
                            v.scalar_tensor_tensor(out=junk[:, (nth - 1) % 2, :], in0=ring[:, slot % RING, :], scalar=1.0,
                                                   in1=xf[:, b, :], op0=ALU.mult, op1=ALU.mult,
                                                   accum_out=act[:, b, k:k + 1]).then_inc(used["u"].sem, 1)
                        elif who == "vector":
                            row_in(slot)
                            if nth > 1:
                                v.wait_ge(used["vector"].sem, used["vector"].at(bgt, nth - 1))
                            v.sem_inc(held, 1)
                            v.scalar_tensor_tensor(out=h_of(bg_half, b), in0=ring[:, slot % RING, :],
                                                   scalar=gl[:, b, k:k + 1], in1=h_of(bg_half, b), op0=ALU.mult,
                                                   op1=ALU.add).then_inc(used["vector"].sem, 1)
                        elif who == "w1":
                            v.wait_ge(used["u"].sem, used["u"].at(bgt, (b + 1) * P))
                            v.tensor_tensor(gl[:, b, :], act[:, b, :], act[:, b, :], ALU.mult).then_inc(s_vec, own.one())
                            v.wait_ge(s_vec, own.so_far(turn))
                            v.tensor_scalar(gl[:, b, :], gl[:, b, :], GELU_A, 1.0, ALU.mult, ALU.add).then_inc(s_vec, own.one())
                            v.wait_ge(s_vec, own.so_far(turn))
                            v.tensor_tensor(gl[:, b, :], gl[:, b, :], act[:, b, :], ALU.mult).then_inc(gelu_raw.sem, 1)
                        elif who == "w2":
                            v.wait_ge(gelu_exp.sem, gelu_exp.at(bgt, b + 1))
                            v.tensor_scalar_add(gl[:, b, :], gl[:, b, :], 1.0).then_inc(s_vec, own.one())
                            v.wait_ge(s_vec, own.so_far(turn))
                            v.reciprocal(gl[:, b, :], gl[:, b, :]).then_inc(s_vec, own.one())
                            v.wait_ge(s_vec, own.so_far(turn))
                            v.tensor_tensor(gl[:, b, :], gl[:, b, :], act[:, b, :], ALU.mult).then_inc(s_vec, own.one())
                            v.wait_ge(s_vec, own.so_far(turn))
                            v.tensor_tensor(gl[:, b, :], gl[:, b, :], gate_c[:, b, :], ALU.mult).then_inc(w_done.sem, 1)
                            v.wait_ge(w_done.sem, w_done.at(bgt, b + 1))
                        elif who == "add":
                            v.wait_ge(used["tensor"].sem, used["tensor"].at(bgt, tensor_rows[b]))
                            v.wait_ge(used["vector"].sem, used["vector"].at(bgt, vector_rows[b]))
                            v.sem_inc(held, 1)
                            v.tensor_tensor(h_of(bg_half, b), h_of(bg_half, b), pv[:, :], ALU.add).then_inc(added.sem, 1)
                    done[0] = UPTO[kind][stage]

                return background

            def hand_over(turn):
                v.tensor_copy(xf[:, :, :], xfn)
                v.tensor_copy(gate_c[:, :, :], gate[:, :, :])
                v.tensor_copy(idx_c[:, :, :], idx_u[:, :, :]).then_inc(handed.sem, 1)
                v.wait_ge(handed.sem, handed.at(turn - 1, 1))
                v.sem_inc(held, 1)

            def norm(turn, half, n, out_rows, name, background):
                background(name + ".b")
                v.wait_ge(sumsq.sem, sumsq.at(turn, n + 1))
                v.tensor_scalar(ss[:, :], ss[:, :], 1.0 / D, EPS, ALU.mult, ALU.add).then_inc(meansq.sem, 1)
                v.wait_ge(gains.sem, gains.at(turn, 16 * (n + 1)))
                v.wait_ge(rstds.sem, rstds.at(turn, n + 1))
                for b in range(HB):
                    v.scalar_tensor_tensor(out=out_rows[:, b, :], in0=h_of(half, b), scalar=rstd[:, b:b + 1], in1=gain[:, :],
                                           op0=ALU.mult, op1=ALU.mult).then_inc(xns.sem, 1)

            def silu_tail(turn, out, e, arg, signal):
                v.tensor_scalar_add(e, e, 1.0).then_inc(s_vec, own.one())
                v.wait_ge(s_vec, own.so_far(turn))
                v.reciprocal(e, e).then_inc(s_vec, own.one())
                v.wait_ge(s_vec, own.so_far(turn))
                v.tensor_tensor(out, e, arg, ALU.mult).then_inc(signal.sem, 1)

            def embed(turn, half, n0, pos0, background):
                norm(turn, half, n0, xtmp, "e_norm", background)
                e2 = etmp[:, :, :].rearrange("p a b -> p (a b)")
                for n in range(2):
                    background(f"e{2 * n + 1}")
                    v.wait_ge(pg_exp.sem, pg_exp.at(turn, 2 * n0 + n + 1))
                    v.tensor_scalar_add(e2, e2, 1.0).then_inc(s_vec, own.one())
                    v.wait_ge(s_vec, own.so_far(turn))
                    v.reciprocal(e2, e2).then_inc(s_vec, own.one())
                    v.wait_ge(s_vec, own.so_far(turn))
                    v.wait_ge(proj.sem, proj.at(turn, pos0 + 2 * n + 2))
                    v.tensor_tensor(e2, e2, pp[:, 1].rearrange("p a b -> p (a b)"), ALU.mult).then_inc(s_vec, own.one())
                    v.wait_ge(s_vec, own.so_far(turn))
                    for b in range(HB):
                        hh = h_cols(half, b, n * NW, NW)
                        m = v.tensor_tensor(hh, hh, e2[:, b * NW:(b + 1) * NW], ALU.add)
                    m.then_inc(pg_used.sem, 1)

            def clear():
                v.memset(conv_past[:, :, :], 0.0)
                v.memset(xbc_past[:, :, :], 0.0)
                v.memset(state[:, :, :], 0.0).then_inc(s_vec, own.one())
                v.wait_ge(s_vec, own.n)

            def mix(turn, half, early, background):
                pos0 = 0 if early else 4
                n0 = 0 if early else 1
                v.tensor_copy(conv_in[:, :, 0:CONV_K - 1], conv_past[:, :, :]).then_inc(s_vec, own.one())
                v.tensor_copy(xbc_in[:, :, 0:MCONV_K - 1], xbc_past[:, :, :]).then_inc(s_vec, own.one())
                norm(turn, half, n0, xtmp, "norm0", background)
                background("dt")
                v.wait_ge(small.sem, small.at(turn, SMALL))
                for s_ in range(2):
                    v.tensor_copy(dskip[s_ * HD:(s_ + 1) * HD, :],
                                          dall[s_ * HD:(s_ + 1) * HD, :].rearrange("p (c s) -> p s c", s=2)[:, s_, :]).then_inc(s_vec, own.one())
                v.wait_ge(dt_proj.sem, dt_proj.at(turn, 1))
                v.tensor_tensor(dts[:, 0], pm[:, 0:HB * HEADS].rearrange("p (a b) -> p a b", b=HEADS),
                                         over(dtb[:, :], 1, HB), ALU.add).then_inc(s_vec, own.one())
                v.wait_ge(s_vec, own.so_far(turn))
                v.scalar_tensor_tensor(out=dts[:, 1], in0=dts[:, 0], scalar=-1.0, in1=dts[:, 0], op0=ALU.mult, op1=ALU.max).then_inc(dt_raw.sem, 1)
                v.tensor_scalar_max(dts[:, 0], dts[:, 0], 0.0).then_inc(s_vec, own.one())
                v.wait_ge(dt_exp.sem, dt_exp.at(turn, 1))
                v.tensor_scalar_add(dts[:, 3], dts[:, 2], 1.0).then_inc(dt_u.sem, 1)
                v.wait_ge(dt_u.sem, dt_u.at(turn, 1))
                v.reciprocal(dts[:, 5], dts[:, 3]).then_inc(s_vec, own.one())
                v.tensor_scalar_add(dt[:, :, :], dts[:, 3], -1.0).then_inc(s_vec, own.one())
                v.wait_ge(s_vec, own.so_far(turn))
                v.tensor_tensor(dts[:, 2], dts[:, 2], dt[:, :, :], ALU.subtract).then_inc(s_vec, own.one())
                v.wait_ge(s_vec, own.so_far(turn))
                v.tensor_tensor(dts[:, 2], dts[:, 2], dts[:, 5], ALU.mult).then_inc(s_vec, own.one())
                v.wait_ge(s_vec, own.so_far(turn))
                v.tensor_tensor(dts[:, 2], dts[:, 2], dts[:, 0], ALU.add).then_inc(s_vec, own.one())
                v.wait_ge(s_vec, own.so_far(turn))
                v.wait_ge(dt_ln.sem, dt_ln.at(turn, 1))
                v.tensor_tensor(dt[:, :, :], dts[:, 2], dts[:, 4], ALU.add).then_inc(s_vec, own.one())
                v.wait_ge(s_vec, own.so_far(turn))
                v.wait_ge(par_done.sem, par_done.at(turn, 1))
                v.wait_ge(expa_done.sem, expa_done.at(turn, 1))
                v.scalar_tensor_tensor(out=a_[:, :, :], in0=dt[:, :, :], scalar=-1.0, in1=over(expa[:, :], 1, HB),
                                       op0=ALU.mult, op1=ALU.mult).then_inc(a_done.sem, 1)
                for i in range(2):
                    tiles = slice(i * TPU, (i + 1) * TPU)
                    background(f"in{i + 2}.3")
                    v.wait_ge(proj.sem, proj.at(turn, pos0 + 3 + i))
                    v.wait_ge(gc_in.sem, gc_in.at(turn, 2))
                    v.tensor_tensor(conv_in[:, tiles, CONV_K - 1:], conv_in[:, tiles, CONV_K - 1:], ppt[:, i % 2],
                                    ALU.mult).then_inc(hc_done.sem, 1)
                    v.wait_ge(hc_done.sem, hc_done.at(turn, i + 1))

                    def tap(j, t):
                        return paramsT[:, R_CONV + j * KT + t:R_CONV + j * KT + t + 1]

                    for j in range(CONV_K):
                        for t in range(i * TPU, (i + 1) * TPU):
                            if j == 0:
                                m = v.tensor_scalar(yc[:, t, :], conv_in[:, t, 0:T], tap(0, t), None, ALU.mult)
                            else:
                                m = v.scalar_tensor_tensor(out=yc[:, t, :], in0=conv_in[:, t, j:j + T], scalar=tap(j, t),
                                                           in1=yc[:, t, :], op0=ALU.mult, op1=ALU.add)
                            m.then_inc(s_vec, own.one())
                        v.wait_ge(s_vec, own.so_far(turn))
                v.tensor_copy(conv_past[:, :, :], conv_in[:, :, T:T + CONV_K - 1]).then_inc(s_vec, own.one())
                for i in range(2):
                    tiles = slice(i * TPU, (i + 1) * TPU)
                    background(f"in{i + 4}.3")
                    v.wait_ge(proj.sem, proj.at(turn, pos0 + 5 + i))
                    v.tensor_tensor(yc[:, tiles, :], yc[:, tiles, :], ppt[:, i % 2], ALU.mult).then_inc(yc_done.sem, 1)
                for i in range(2):
                    background(f"in{i + 6}.3")
                    v.wait_ge(z_exp.sem, z_exp.at(turn, i + 1))
                    silu_tail(turn, zs[:, i * TPU:(i + 1) * TPU, :], zs[:, i * TPU:(i + 1) * TPU, :], ppt[:, i % 2], z_done)
                for i in range(XT // TPU):
                    background(f"in{i + 8}.3")
                    v.wait_ge(xbc_cp.sem, xbc_cp.at(turn, i + 1))

                    def mtap(j, t):
                        return paramsT[:, R_MCONV + j * XT + t:R_MCONV + j * XT + t + 1]

                    for j in range(MCONV_K):
                        for t in range(i * TPU, (i + 1) * TPU):
                            if j == 0:
                                m = v.tensor_scalar(xc[:, t, :], xbc_in[:, t, 0:T], mtap(0, t),
                                                    paramsT[:, R_MB + t:R_MB + t + 1], ALU.mult, ALU.add)
                            else:
                                m = v.scalar_tensor_tensor(out=xc[:, t, :], in0=xbc_in[:, t, j:j + T], scalar=mtap(j, t),
                                                           in1=xc[:, t, :], op0=ALU.mult, op1=ALU.add)
                            if j == MCONV_K - 1 and t == (i + 1) * TPU - 1:
                                m.then_inc(conv_done.sem, 1)
                            else:
                                m.then_inc(s_vec, own.one())
                        if j < MCONV_K - 1:
                            v.wait_ge(s_vec, own.so_far(turn))
                    v.wait_ge(silu_exp.sem, silu_exp.at(turn, i + 1))
                    silu_tail(turn, xc[:, i * TPU:(i + 1) * TPU, :], etmp[:, :, :], xc[:, i * TPU:(i + 1) * TPU, :], silu_done)
                v.tensor_copy(xbc_past[:, :, :], xbc_in[:, :, T:T + MCONV_K - 1]).then_inc(s_vec, own.one())
                background("cum0")
                v.wait_ge(acum_mm.sem, acum_mm.at(turn, 1))
                v.tensor_copy(acum[:, :, :, :].rearrange("p a b c -> p (a b c)"), pm[:, 0:4 * HEADS]).then_inc(acum_cp.sem, 1)
                v.wait_ge(acum_cp.sem, acum_cp.at(turn, 1))
                v.tensor_tensor(d_in[:, :, :], acum[:, :, 1, :], acum[:, :, 0, :], ALU.subtract).then_inc(d_raw.sem, 1)
                background("cum1")
                v.wait_ge(d_exp.sem, d_exp.at(turn, 1))
                v.wait_ge(silu_done.sem, silu_done.at(turn, XT // TPU))
                for i in range(4):
                    b, g = divmod(i, 2)
                    heads = slice(g * HG, (g + 1) * HG)
                    background(f"ssd{i}a")
                    v.wait_ge(g_mm.sem, g_mm.at(turn, i + 1))
                    if i:
                        v.wait_ge(g_y.sem, g_y.at(turn, i))
                    v.tensor_tensor(cbm[:, :], pm[:, P:2 * P], causalT[:, :], ALU.mult)
                    v.tensor_copy(b_tok[:, :], pm[:, 2 * P:3 * P])
                    v.tensor_tensor(xdt, pxt.rearrange("p a (b c) -> p (a b) c", c=HD),
                                             over(dt[:, b, heads], 2, HD), ALU.mult).then_inc(s_vec, own.one())
                    v.wait_ge(s_vec, own.so_far(turn))
                    v.tensor_tensor(xdtd, xdt, over(d_in[:, b, heads], 2, HD), ALU.mult).then_inc(s_vec, own.one())
                    v.wait_ge(g_cdec.sem, g_cdec.at(turn, i + 1))
                    for k in range(HG):
                        m = v.tensor_scalar(decay[:, k, :], ppf[:, k * P:(k + 1) * P],
                                            acum[:, b, 0, g * HG + k:g * HG + k + 1], 0.0, ALU.subtract, ALU.min)
                    m.then_inc(g_dif.sem, 1)
                    background(f"ssd{i}b")
                    v.wait_ge(g_act.sem, g_act.at(turn, i + 1))
                    v.tensor_tensor(c_dec, c_dec, over(xc[:, 10 + g, b * P:(b + 1) * P], 1, HG), ALU.mult)
                    v.tensor_tensor(decay, decay, over(cbm[:, :], 1, HG), ALU.mult).then_inc(g_mats.sem, 1)
                    background(f"ssd{i}c")
                    v.wait_ge(g_y.sem, g_y.at(turn, i + 1))
                    v.tensor_tensor(state[:, heads, :], state[:, heads, :],
                                             over(d_chunk[:, b, heads], 2, HD), ALU.mult).then_inc(s_vec, own.one())
                    v.wait_ge(s_vec, own.so_far(turn))
                    v.tensor_tensor(state[:, heads, :], state[:, heads, :],
                                            ppf[:, 3 * NW:4 * NW].rearrange("p (a b) -> p a b", b=HD), ALU.add).then_inc(s_vec, own.one())
                    for t in range(4):
                        tt = g * 4 + t
                        m = v.scalar_tensor_tensor(out=ys[:, tt, b * P:(b + 1) * P], in0=xc[:, tt, b * P:(b + 1) * P],
                                                   scalar=dskip[:, tt:tt + 1],
                                                   in1=ppf[:, 2 * NW + t * P:2 * NW + (t + 1) * P],
                                                   op0=ALU.mult, op1=ALU.add)
                    m.then_inc(g_used.sem, 1)
                    if g == 1:
                        v.wait_ge(g_used.sem, g_used.at(turn, i + 1))
                        v.tensor_tensor(ys[:, :, b * P:(b + 1) * P], ys[:, :, b * P:(b + 1) * P],
                                        zs[:, :, b * P:(b + 1) * P], ALU.mult).then_inc(ys_done.sem, 1)
                background("post1")
                v.wait_ge(sq_used.sem, sq_used.at(turn, 4))
                v.tensor_copy(sums[:, :], pm[:, SUMS:SUMS + 6]).then_inc(s_vec, own.one())
                v.wait_ge(s_vec, own.so_far(turn))
                v.tensor_tensor(sums[:, 0:HB], sums[:, 0:HB], sums[:, HB:2 * HB], ALU.add).then_inc(s_vec, own.one())
                v.wait_ge(s_vec, own.so_far(turn))
                v.tensor_scalar(ss2[:, :, 0], sums[:, 0:HB], 1.0 / D, EPS, ALU.mult, ALU.add)
                v.tensor_scalar(ss2[:, :, 1], sums[:, 2 * HB:3 * HB], 1.0 / D, EPS, ALU.mult,
                                ALU.add).then_inc(ss2_ms.sem, 1)
                v.wait_ge(rstd2s.sem, rstd2s.at(turn, 1))
                for i in range(4):
                    n, g = divmod(i, 2)
                    background(f"out{i}.1")
                    v.wait_ge(proj.sem, proj.at(turn, pos0 + U_OUT + i + 1))
                    for b in range(HB):
                        hh = h_cols(half, b, n * NW, NW)
                        m = v.scalar_tensor_tensor(out=hh, in0=pp[:, (U_OUT + i) % 2, b, :], scalar=rstd2[:, b, g:g + 1],
                                                   in1=hh, op0=ALU.mult, op1=ALU.add)
                        if b == HB - 1:
                            m.then_inc(out_used.sem, 1)
                    v.wait_ge(out_used.sem, out_used.at(turn, i + 1))
                background("norm1.a")
                norm(turn, half, n0 + 1, xfn, "norm1", background)
                for b in range(HB):
                    background(f"top{b}.0")
                    v.wait_ge(score_cp.sem, score_cp.at(turn, b + 1))
                    v.sem_inc(held, 1)
                    for j in range(J):
                        v.max(out=sv[:, j, 0:8], in_=sc[:, j, :]).then_inc(s_vec, own.one())
                    background(f"top{b}.1")
                    v.wait_ge(s_vec, own.so_far(turn))
                    v.sem_inc(held, 1)
                    for j in range(J):
                        v.max_index(out=si[:, j, 0:8], in_max=sv[:, j, 0:8], in_values=sc[:, j, :]).then_inc(s_vec, own.one())
                        v.match_replace(out=sc2[:, j, :], in_to_replace=sv[:, j, 0:8], in_values=sc[:, j, :],
                                                imm_value=NEG).then_inc(s_vec, own.one())
                    background(f"top{b}.2")
                    v.wait_ge(s_vec, own.so_far(turn))
                    v.sem_inc(held, 1)
                    for j in range(J):
                        v.max(out=sv[:, j, 8:16], in_=sc2[:, j, :]).then_inc(s_vec, own.one())
                    background(f"top{b}.3")
                    v.wait_ge(s_vec, own.so_far(turn))
                    v.sem_inc(held, 1)
                    for j in range(J):
                        v.max_index(out=si[:, j, 8:16], in_max=sv[:, j, 8:16], in_values=sc2[:, j, :]).then_inc(s_vec, own.one())
                    v.wait_ge(s_vec, own.so_far(turn))
                    v.sem_inc(held, 1)
                    background(f"top{b}.4")
                    svp = sv[:, :, :].rearrange("p (h s) k -> p h s k", s=2)
                    v.tensor_copy(sif[:, :, :], si[:, :, :]).then_inc(s_vec, own.one())
                    v.wait_ge(score_mm.sem, score_mm.at(turn, HB))
                    v.tensor_tensor(cand[:, :, :, :], over(svp[:, :, 0, :], 3, TOPK), over(svp[:, :, 1, :], 2, TOPK),
                                             ALU.add).then_inc(s_vec, own.one())
                    background(f"top{b}.5")
                    v.wait_ge(s_vec, own.so_far(turn))
                    v.sem_inc(held, 1)
                    cf = cand[:, :, :, :].rearrange("p h a b -> p h (a b)")
                    for j in range(PH):
                        v.max(out=tv[:, j, 0:8], in_=cf[:, j, :]).then_inc(s_vec, own.one())
                    background(f"top{b}.6")
                    v.wait_ge(s_vec, own.so_far(turn))
                    v.sem_inc(held, 1)
                    for j in range(PH):
                        v.max_index(out=ti[:, j, 0:8], in_max=tv[:, j, 0:8], in_values=cf[:, j, :]).then_inc(s_vec, own.one())
                        v.match_replace(out=cand2[:, j, :], in_to_replace=tv[:, j, 0:8], in_values=cf[:, j, :],
                                                imm_value=NEG).then_inc(s_vec, own.one())
                    background(f"top{b}.7")
                    v.wait_ge(s_vec, own.so_far(turn))
                    v.sem_inc(held, 1)
                    for j in range(PH):
                        v.max(out=tv[:, j, 8:16], in_=cand2[:, j, :]).then_inc(s_vec, own.one())
                    background(f"top{b}.8")
                    v.wait_ge(s_vec, own.so_far(turn))
                    v.sem_inc(held, 1)
                    for j in range(PH):
                        v.max_index(out=ti[:, j, 8:16], in_max=tv[:, j, 8:16], in_values=cand2[:, j, :]).then_inc(s_vec, own.one())
                    background(f"top{b}.9")
                    v.wait_ge(s_vec, own.so_far(turn))
                    v.sem_inc(held, 1)
                    gb = gate[:, b, :].rearrange("p (h k) -> p h k", k=TOPK)
                    v.tensor_tensor(gb, tv[:, :, :], tv[:, :, 0:1].to_broadcast([P, PH, TOPK]),
                                    ALU.subtract).then_inc(tv_sub.sem, 1)
                    tif = ti[:, :, :].rearrange("p h k -> p (h k)")
                    v.tensor_single_scalar(tq[:, 0, :], tif, 4, ALU.logical_shift_right).then_inc(s_vec, own.one())
                    v.tensor_single_scalar(tq[:, 1, :], tif, 15, ALU.bitwise_and).then_inc(s_vec, own.one())
                    v.wait_ge(s_vec, own.so_far(turn))
                    v.tensor_copy(tqf[:, :, :], tq[:, :, :]).then_inc(s_vec, own.one())
                    v.wait_ge(s_vec, own.so_far(turn))
                    background(f"top{b}.10")
                    for s_ in range(2):
                        v.tensor_tensor(hot, over(tqf[:, s_, :], 2, TOPK), over(iota_f[:, :], 1, SLOTS), ALU.is_equal).then_inc(s_vec, own.one())
                        v.wait_ge(s_vec, own.so_far(turn))
                        h4 = hot.rearrange("p (h k) j -> p h k j", k=TOPK)
                        sel = over(sif[:, :, :].rearrange("p (h s) k -> p h s k", s=2)[:, :, s_, :], 2, TOPK)
                        v.tensor_tensor(h4, h4, sel, ALU.mult).then_inc(s_vec, own.one())
                        v.wait_ge(s_vec, own.so_far(turn))
                        v.tensor_reduce(out=ei[:, s_, :], in_=hot, axis=AX.X, op=ALU.add).then_inc(s_vec, own.one())
                        v.wait_ge(s_vec, own.so_far(turn))
                    v.scalar_tensor_tensor(out=eidx[:, :], in0=ei[:, 0, :], scalar=float(KEYS), in1=ei[:, 1, :],
                                                    op0=ALU.mult, op1=ALU.add).then_inc(s_vec, own.one())
                    v.wait_ge(s_vec, own.so_far(turn))
                    if not early:
                        v.tensor_scalar_add(eidx[:, :], eidx[:, :], float(EXPERTS)).then_inc(s_vec, own.one())
                        v.wait_ge(s_vec, own.so_far(turn))
                    v.tensor_copy(idx_u[:, b, :], eidx[:, :]).then_inc(idx_done.sem, 1)
                    background(f"top{b}.11")
                    v.wait_ge(tv_exp.sem, tv_exp.at(turn, b + 1))
                    v.tensor_reduce(out=gsum[:, :], in_=gb, axis=AX.X, op=ALU.add).then_inc(s_vec, own.one())
                    v.wait_ge(s_vec, own.so_far(turn))
                    v.reciprocal(gsum[:, :], gsum[:, :]).then_inc(s_vec, own.one())
                    v.wait_ge(s_vec, own.so_far(turn))
                    v.tensor_tensor(gb, gb, over(gsum[:, :], 2, TOPK), ALU.mult).then_inc(s_vec, own.one())
                    v.wait_ge(s_vec, own.so_far(turn))
                background("end")

            v.wait_ge(s_const, 5)
            v.tensor_copy(iota_f[:, :], iota_i[:, :]).then_inc(s_vec, own.one())
            clear()
            v.wait_ge(s_hload, 16)
            mix(0, 0, True, idle)
            turn_barrier(v, 0)
            hand_over(1)
            mix(1, 1, True, follow("mix", 0, 0, 1))
            clear()
            turn_barrier(v, 1)
            before = own.n
            with v.Fori(0, HALVES) as half:
                turn = half + HALVES
                hand_over(turn)
                background = follow("both", turn - 1, 1 - half, turn)
                embed(turn, half, 0, 0, background)
                mix(turn, half, False, background)
                turn_barrier(v, turn)
            assert own.n - before == VEC_PER_ROUND, f"vec_turn={own.n - before}"
            own.n += VEC_PER_ROUND
            turn = 2 * HALVES
            hand_over(turn)
            background = follow("embed", turn - 1, 1, turn)
            embed(turn, 0, 0, 0, background)
            background("end")
            turn_barrier(v, turn)
            embed(turn, 1, 1, 4, idle)
            v.wait_ge(s_finsq, NBLK)
            v.tensor_scalar(fin[:, 1, :], fin[:, 0, :], 1.0 / D, EPS, ALU.mult, ALU.add).then_inc(s_finsq, 1)
            v.wait_ge(gains.sem, gains.at(turn, 16 * 3))
            v.wait_ge(s_finsq, NBLK + 3)
            for b in range(NBLK):
                v.scalar_tensor_tensor(out=ring[:, b, :], in0=h[:, b, :], scalar=fin[:, 1, b:b + 1], in1=gain[:, :],
                                       op0=ALU.mult, op1=ALU.mult).then_inc(s_fin, 1)

        @block.tensor
        def _(t):
            etf = etmp[:, :, :].rearrange("p a b -> p (a b)")

            def idle(stage):
                pass

            def follow(kind, bgt):
                done = [0]

                def background(stage):
                    for who, b, k, slot, nth in entries[done[0]:UPTO[kind][stage]]:
                        if who != "tensor":
                            continue
                        q, j = group_of[b, k]
                        first = k == 0
                        last = (b == 0 and k == P - 2) or (b == 1 and k == P - 2)
                        if j == 0:
                            t.wait_ge(diag_done.sem, diag_done.at(bgt, q + 1))
                        if first and b:
                            t.wait_ge(added.sem, added.at(bgt, b))
                        t.wait_ge(s_row[slot % RING], (bgt * ROWS_PER_TURN + (slot // RING + 1)) * 16)
                        for n in range(D // NW):
                            mm = t.matmul(pv[:, n * NW:(n + 1) * NW], diag[:, q % 2, j, :],
                                          ring[:, slot % RING, n * NW:(n + 1) * NW], start=first, stop=last)
                        mm.then_inc(used["tensor"].sem, 1)
                    done[0] = UPTO[kind][stage]

                return background

            def block_of(tile, k, b):
                return tile[:, k, b * P:(b + 1) * P]

            def norm_T(turn, n, rows_in, name, background):
                background(name + ".c")
                for b in range(HB):
                    t.wait_ge(xns.sem, xns.at(turn, n * HB + b + 1))
                    for k in range(KT):
                        mm = t.transpose(ppf[:, b * D + k * P:b * D + (k + 1) * P], rows_in[:, b, k * P:(k + 1) * P],
                                         ident[:, :])
                    mm.then_inc(tr_done.sem, 1)

            def embed(turn, n0, pos0, background):
                background("e_norm.a")
                t.wait_ge(p_in.sem, p_in.at(turn, 16 * (n0 + 1)))
                for b in range(HB):
                    for k in range(PT):
                        m_ = b * PT + k
                        mm = t.transpose(px[:, m_ * P:(m_ + 1) * P], ptok[:, b, k * P:(k + 1) * P], ident[:, :])
                mm.then_inc(pT_tr.sem, 1)
                norm_T(turn, n0, xtmp, "e_norm", background)
                for i in range(4):
                    n, g = divmod(i, 2)
                    if g == 0:
                        background(f"e{i}.0")
                        if i == 0:
                            t.wait_ge(xnT_done.sem, xnT_done.at(turn, n0 * HB + HB))
                        else:
                            t.wait_ge(pg_exp.sem, pg_exp.at(turn, 2 * n0 + n))
                    else:
                        background(f"e{i}")
                        if i == 1:
                            t.wait_ge(pT_cp.sem, pT_cp.at(turn, n0 + 1))
                        else:
                            t.wait_ge(pg_used.sem, pg_used.at(turn, 2 * n0 + n))
                    t.wait_ge(w_in_sem[g].sem, w_in_sem[g].at(turn, 16 * (2 * n0 + n + 1)))
                    nk = (KT, PT)[g]
                    for b in range(HB):
                        if g == 0 and b:
                            background(f"e{i}.1")
                        for k in range(nk):
                            lhs = pT[:, b * PT + k, :] if g else block_of(xnT, k, b)
                            mm = t.matmul(pp[:, g, b, :], lhs, wbuf[:, g, k, :], start=(k == 0), stop=(k == nk - 1))
                    mm.then_inc(proj.sem, 1)

            def mix(turn, early, background):
                n0 = 0 if early else 1

                def weights(u):
                    t.wait_ge(w_in_sem[u % 2].sem, w_in_sem[u % 2].at(turn, 16 * (u // 2 + 1 + 2 * n0)))

                def tiles_unit(u, name):
                    weights(u)
                    for m in range(TPU):
                        if m:
                            background(f"{name}.{m}")
                        for k in range(KT):
                            mm = t.matmul(ppt[:, u % 2, m, :], wbuf[:, u % 2, k, m * P:(m + 1) * P], xnT[:, k, :],
                                          start=(k == 0), stop=(k == KT - 1))
                    mm.then_inc(proj.sem, 1)

                norm_T(turn, n0, xtmp, "norm0", background)
                background("dt")
                t.wait_ge(xnT_done.sem, xnT_done.at(turn, n0 * HB + HB))
                t.wait_ge(small.sem, small.at(turn, SMALL))
                t.transpose(px[:, 0:ROWS], params[0:ROWS, :], ident[0:ROWS, 0:ROWS]).then_inc(par_T.sem, 1)
                for b in range(HB):
                    for k in range(KT):
                        mm = t.matmul(pm[:, b * HEADS:(b + 1) * HEADS], block_of(xnT, k, b), wdt[:, k, :],
                                      start=(k == 0), stop=(k == KT - 1))
                mm.then_inc(dt_proj.sem, 1)
                for u in range(U_OUT):
                    background(f"in{u}.0")
                    if u >= 2:
                        reader = [gc_in, hc_done, yc_done, z_done, xbc_cp][(u - 2) // 2]
                        t.wait_ge(reader.sem, reader.at(turn, (u - 2) % 2 + 1))
                    tiles_unit(u, f"in{u}")
                    if u in (6, 7):
                        i = u - 6
                        t.wait_ge(sq_done.sem, sq_done.at(turn, i + 1))
                        for b in range(HB):
                            for m in range(TPU):
                                mm = t.matmul(pm[:, SUMS + i * HB + b:SUMS + i * HB + b + 1], block_of(etmp, m, b),
                                              ones[:, 0:1], start=(m == 0), stop=(m == TPU - 1))
                        mm.then_inc(sq_used.sem, 1)
                background("cum0")
                t.wait_ge(a_done.sem, a_done.at(turn, 1))
                for b in range(HB):
                    t.matmul(pm[:, b * 2 * HEADS:(b * 2 + 1) * HEADS], causalT[:, :], a_[:, b, :], start=True, stop=True)
                    mm = t.matmul(pm[:, (b * 2 + 1) * HEADS:(b * 2 + 2) * HEADS], ones[:, :], a_[:, b, :], start=True, stop=True)
                mm.then_inc(acum_mm.sem, 1)
                background("cum1")
                t.wait_ge(acum_cp.sem, acum_cp.at(turn, 1))
                t.wait_ge(silu_done.sem, silu_done.at(turn, XT // TPU))
                for i in range(4):
                    b, g = divmod(i, 2)
                    background(f"ssd{i}a")
                    if i:
                        t.wait_ge(g_act.sem, g_act.at(turn, i))
                    t.matmul(pm[:, P:2 * P], block_of(xc, KT + g, b), block_of(xc, KT + 2 + g, b), start=True, stop=True)
                    t.transpose(pm[:, 2 * P:3 * P], block_of(xc, KT + g, b), ident[:, :])
                    for m in range(TPU):
                        t.transpose(px[:, m * P:(m + 1) * P], block_of(xc, g * TPU + m, b), ident[:, :])
                    for k in range(HG):
                        col = a_[:, b, g * HG + k:g * HG + k + 1].to_broadcast([P, P])
                        mm = t.matmul(ppf[:, k * P:(k + 1) * P], col, causalT[:, :], start=True, stop=True)
                    mm.then_inc(g_mm.sem, 1)
                    background(f"ssd{i}c")
                    t.wait_ge(g_mats.sem, g_mats.at(turn, i + 1))
                    if i:
                        t.wait_ge(g_used.sem, g_used.at(turn, i))
                    for k in range(HG):
                        y = ppf[(k % 2) * HD:(k % 2 + 1) * HD, 2 * NW + (k // 2) * P:2 * NW + (k // 2 + 1) * P]
                        t.matmul(y, xdt[:, k, :], decay[:, k, :], start=True, stop=False)
                        t.matmul(y, state[:, g * HG + k, :], c_dec[:, k, :], start=False, stop=True)
                    t.matmul(ppf[:, 3 * NW:4 * NW], b_tok[:, :], xdtd.rearrange("p a b -> p (a b)"), start=True,
                             stop=True).then_inc(g_y.sem, 1)
                for b in range(HB):
                    background(f"post{b}")
                    t.wait_ge(sq_done.sem, sq_done.at(turn, 2 + b + 1))
                    for m in range(KT):
                        mm = t.matmul(pm[:, SUMS + 2 * HB + b:SUMS + 2 * HB + b + 1], etf[:, m * P:(m + 1) * P],
                                      ones[:, 0:1], start=(m == 0), stop=(m == KT - 1))
                    mm.then_inc(sq_used.sem, 1)
                for i in range(4):
                    n, g = divmod(i, 2)
                    for b in range(HB):
                        background(f"out{i}.{b}")
                        if b == 0:
                            if i == 0:
                                t.wait_ge(y_scaled.sem, y_scaled.at(turn, 2))
                            if i >= 2:
                                t.wait_ge(out_used.sem, out_used.at(turn, i - 1))
                            weights(U_OUT + i)
                        for k in range(KT):
                            mm = t.matmul(pp[:, (U_OUT + i) % 2, b, :], block_of((yc, ys)[g], k, b),
                                          wbuf[:, (U_OUT + i) % 2, k, :], start=(k == 0), stop=(k == KT - 1))
                    mm.then_inc(proj.sem, 1)
                norm_T(turn, n0 + 1, xfn, "norm1", background)
                for i in range(4):
                    background(f"q{i}.0")
                    if i == 0:
                        t.wait_ge(xnT_done.sem, xnT_done.at(turn, (n0 + 1) * HB + HB))
                    if i >= 2:
                        t.wait_ge(qT_cp.sem, qT_cp.at(turn, i - 1))
                    tiles_unit(U_Q + i, f"q{i}")
                background("keys")
                t.wait_ge(keys_in.sem, keys_in.at(turn, 16))
                for i in range(J // 4):
                    if i:
                        t.wait_ge(keysT_cp.sem, keysT_cp.at(turn, i))
                    for m in range(4):
                        mm = t.transpose(px[:, m * P:(m + 1) * P], keys[:, i * 4 + m, :], ident[:, :])
                    mm.then_inc(keysT_tr.sem, 1)
                background("score")
                t.wait_ge(qT_cp.sem, qT_cp.at(turn, 4))
                t.wait_ge(keysT_cp.sem, keysT_cp.at(turn, 4))
                for b in range(HB):
                    if b:
                        t.wait_ge(score_cp.sem, score_cp.at(turn, b))
                    for j in range(J):
                        mm = t.matmul(ppf[:, j * KEYS:(j + 1) * KEYS], block_of(qT, j, b), keysT[:, j, :], start=True, stop=True)
                    mm.then_inc(score_mm.sem, 1)
                background("end")

            t.wait_ge(s_const, 5)
            t.sem_inc(proj.sem, 1)
            mix(0, True, idle)
            turn_barrier(t, 0)
            mix(1, True, follow("mix", 0))
            turn_barrier(t, 1)
            with t.Fori(0, HALVES) as half:
                turn = half + HALVES
                background = follow("both", turn - 1)
                embed(turn, 0, 0, background)
                mix(turn, False, background)
                turn_barrier(t, turn)
            turn = 2 * HALVES
            background = follow("embed", turn - 1)
            embed(turn, 0, 0, background)
            background("end")
            turn_barrier(t, turn)
            embed(turn, 1, 4, idle)


_INS = ['x', 'p', 'norm_mix_w', 'w_in', 'conv_w', 'mconv_w', 'mconv_b', 'dt_bias', 'a_log', 'd_skip', 'conv_norm_w',
        'ssd_norm_w', 'w_out', 'norm_ffn_w', 'peer_wq', 'peer_keys', 'peer_u', 'peer_v', 'norm_ple_w', 'w_ple_gate',
        'w_ple', 'final_norm_w']


def kernel(**inputs):
    import numpy as _np
    import concourse.bacc as _bacc
    from concourse import mybir as _mybir
    from concourse.bass_utils import run_bass_kernel_spmd as _run

    nc = _bacc.Bacc("TRN2", target_bir_lowering=False, num_devices=1)
    arrays, args = {}, []
    for name in _INS:
        a = _np.ascontiguousarray(inputs[name])
        arrays[f"in_{name}_dram"] = a
        args.append(nc.dram_tensor(f"in_{name}_dram", a.shape, _mybir.dt.from_np(a.dtype), kind="ExternalInput").ap())
    shape = inputs["x"].shape
    args.append(nc.dram_tensor("out_0_dram", shape, _mybir.dt.float32, kind="ExternalOutput").ap())
    trunk(nc, *args)
    r = _run(nc, [arrays], core_ids=[0])
    return r.results[0]["out_0_dram"]
```

```python
from contextlib import ExitStack

import concourse.bass as bass
from concourse import mybir

F32 = mybir.dt.float32
I32 = mybir.dt.int32
U32 = mybir.dt.uint32
ALU = mybir.AluOpType
ACT = mybir.ActivationFunctionType
AX = mybir.AxisListType

P = 128
EPS = 1e-6
NEG = -3.0e38
GELU_C = 0.7978845608028654
GELU_A = 0.044715
TOP_STAGES = 8
LEAD = 116
VEC_PER_ROUND = 401
SCA_PER_ROUND = 8


class Signal:

    def __init__(self, sem, per_turn, early=None, head=0):
        self.sem, self.per_turn, self.head = sem, per_turn, head
        self.early = per_turn if early is None else early

    def at(self, turn, n):
        if isinstance(turn, int):
            return min(turn, 2) * self.early + max(turn - 2, 0) * self.per_turn + n + self.head
        return turn * self.per_turn + (2 * self.early - 2 * self.per_turn + n + self.head)


class Steps:

    def __init__(self, per_round):
        self.n, self.per_round = 0, per_round

    def one(self):
        self.n += 1
        return 1

    def so_far(self, turn):
        if isinstance(turn, int):
            return self.n
        return turn * self.per_round + (self.n - 2 * self.per_round)


SHARES = [(0, 0, 64, 8, 2, 4), (0, 64, 128, 16, 4, 4), (1, 0, 128, 8, 2, 4)]


def on_tensor(b, k):
    return any(b == b_ and k0 <= k < k1 and (k - k0) % period % step == 0 and (k - k0) % period // step < n
               for b_, k0, k1, period, step, n in SHARES)


def expert_rows():
    out, slot = [], 0
    count = {"u": 0, "vector": 0, "tensor": 0}

    def row(kind, b, k):
        nonlocal slot
        who = "u" if kind == "u" else ("tensor" if on_tensor(b, k) else "vector")
        count[who] += 1
        out.append((who, b, k, slot, count[who]))
        slot += 1

    lead = 12
    for k in range(P):
        row("u", 0, k)
    out.append(("w1", 0, 0, 0, 0))
    for k in range(2):
        row("u", 1, k)
    out.append(("w2", 0, 0, 0, 0))
    for k in range(2, lead):
        row("u", 1, k)
    for k in range(lead, P):
        row("u", 1, k)
        row("v", 0, k - lead)
    out.append(("w1", 1, 0, 0, 0))
    for k in range(P - lead, P - lead + 2):
        row("v", 0, k)
    out.append(("w2", 1, 0, 0, 0))
    for k in range(P - lead + 2, P):
        row("v", 0, k)
    out.append(("add", 0, 0, 0, 0))
    for k in range(P):
        row("v", 1, k)
    out.append(("add", 1, 0, 0, 0))
    return out, count


def schedule(first, last, stages):
    total = sum(w for _, w in stages)
    upto, done = {"start": first}, 0.0
    for name, w in stages:
        done += w
        upto[name] = first + round((last - first) * done / total)
    return upto


def over(ap, axis, n):
    a = ap.unsqueeze(axis)
    shape = list(a.shape)
    shape[axis] = n
    return a.to_broadcast(shape)


def trunk(nc, x, p, norm_mix_w, w_in, conv_w, mconv_w, mconv_b, dt_bias, a_log, d_skip, conv_norm_w,
          ssd_norm_w, w_out, norm_ffn_w, peer_wq, peer_keys, peer_u, peer_v, norm_ple_w, w_ple_gate,
          w_ple, final_norm_w, out):
    D = x.shape[2]
    SEQ = x.shape[1]
    DEPTH = p.shape[0]
    KT = D // P
    NBLK = SEQ // P
    HB = 2
    HALVES = NBLK // HB
    T = HB * P
    D_IN = w_in.shape[2]
    HEADS = dt_bias.shape[1]
    HD = D // HEADS
    HG = HEADS // 2
    CONV_K, MCONV_K = conv_w.shape[1], mconv_w.shape[1]
    XT = mconv_b.shape[1] // P
    PH, KEYS, EXPERTS = peer_keys.shape[1], peer_keys.shape[3], peer_u.shape[1]
    TOPK = 16
    J = 2 * PH
    assert SEQ == 2 * T and DEPTH == 2
    SLOTS = PH * TOPK
    PLE = p.shape[3]
    PT = PLE // P
    NW = 512
    TPU = NW // P

    U_XBC = 0
    U_GC = U_XBC + XT // TPU
    U_HC, U_Z, U_GB = U_GC + 2, U_GC + 4, U_GC + 6
    IN_COLS = [4 * D + NW * i for i in range(XT // TPU)] + [D, D + NW, 2 * D, 2 * D + NW, 3 * D, 3 * D + NW, 0, NW]
    U_IN = 0
    U_OUT = len(IN_COLS)
    U_Q = U_OUT + 4
    U_PLE = U_Q + 4
    UNITS = U_PLE + 4
    EVEN = U_PLE - U_PLE // 2
    ODD = U_PLE // 2

    R_CONV = 0
    R_MCONV = R_CONV + CONV_K * KT
    R_MB = R_MCONV + MCONV_K * XT
    R_CN = R_MB + XT
    R_SN = R_CN + KT
    ROWS = R_SN + KT

    SMALL = 16 * 9

    RING = 10
    SUMS = 448

    entries, n_rows = expert_rows()
    tensor_rows = [sum(e[0] == "tensor" and e[1] <= b for e in entries) for b in range(HB)]
    vector_rows = [sum(e[0] == "vector" and e[1] <= b for e in entries) for b in range(HB)]
    diag_groups = [(b, k, step, n) for b, k0, k1, period, step, n in SHARES for k in range(k0, k1, period)]
    group_of, group_end, at = {}, [], 0
    for q, (gb_, k0, st, n) in enumerate(diag_groups):
        for j in range(n):
            group_of[gb_, k0 + st * j] = (q, j)
        at += n
        group_end.append(at)

    embed_stages = [("e_norm.a", 5), ("e_norm.b", 5), ("e_norm.c", 4), ("e0.0", 4), ("e0.1", 4), ("e1", 5), ("e2.0", 4),
                    ("e2.1", 4), ("e3", 5), ("e4", 3)]
    mix_stages = [("norm0.a", 5), ("norm0.b", 5), ("norm0.c", 4), ("dt", 4)]
    mix_stages += [(f"in{u}.{m}", 2) for u in range(U_GB) for m in range(TPU)]
    mix_stages += [("cum0", 2), ("cum1", 2)]
    mix_stages += [(f"in{u}.{m}", 2) for u in range(U_GB, U_OUT) for m in range(TPU)]
    mix_stages += [(f"ssd{i}{x}", 8) for i in range(4) for x in "abc"]
    mix_stages += [("post0", 5), ("post1", 5)] + [(f"out{i}.{b}", 4) for i in range(4) for b in range(HB)]
    mix_stages += [("norm1.a", 5), ("norm1.b", 5), ("keys", 3), ("norm1.c", 4)]
    mix_stages += [(f"q{i}.{m}", 3.0) for i in range(4) for m in range(TPU)] + [("score", 3), ("best", 8)]
    mix_stages += [(f"top{b}.{j}", 5) for b in range(HB) for j in range(TOP_STAGES)] + [("end", 1)]
    last_stages = [(f"last{b}.{x}", 12) for b in range(HB) for x in "abcdef"] + [("wait", 420)]
    last_stages += [(f"last{HB}.{x}", 15) for x in "abcdef"] + [("end", 60)]
    lead_stages = [(name, w if name.startswith("top1") else 0) for name, w in mix_stages]
    UPTO = {"lead": schedule(0, LEAD, lead_stages), "mix": schedule(LEAD, len(entries), mix_stages),
            "both": schedule(0, len(entries), embed_stages + mix_stages),
            "last": schedule(0, len(entries), last_stages)}
    first_done = entries.index(("add", 0, 0, 0, 0)) + 1
    assert first_done <= UPTO["mix"]["top0.7"] and first_done <= UPTO["both"]["top0.7"]
    assert first_done <= UPTO["last"]["wait"]
    assert LEAD <= P

    with ExitStack() as c:
        def sb(name, shape, dt=F32):
            return c.enter_context(nc.sbuf_tensor(name, shape, dt))

        def ps(name, shape):
            return c.enter_context(nc.psum_tensor(name, shape, F32))

        def sem(name):
            return c.enter_context(nc.semaphore(name))

        h = sb("h", [P, NBLK, D])
        wbuf = sb("wbuf", [P, 2, KT, NW])
        wdt = sb("wdt", [P, KT, HEADS])
        xf = sb("xf", [P, HB, D])
        xnT = sb("xnT", [P, KT, T])
        conv_past = sb("conv_past", [P, KT, CONV_K - 1])
        xbc_past = sb("xbc_past", [P, XT, MCONV_K - 1])
        gain = sb("gain", [P, D])
        params = sb("params", [P, P])
        paramsT = sb("paramsT", [P, P])
        dskip = sb("dskip", [P, KT])
        etmp = sb("etmp", [P, TPU, T])
        state = sb("state", [P, HEADS, HD])
        ring = sb("ring", [P, RING, D])
        CONV_IN = KT * (CONV_K - 1 + T)
        XBC_IN = XT * (MCONV_K - 1 + T)
        arena = sb("arena", [P, 12 * D + CONV_IN + XBC_IN])

        def region(k0, shape):
            n = 1
            for s in shape:
                n *= s
            flat = arena[:, k0 * D:k0 * D + n]
            if len(shape) == 1:
                return flat
            names = "abc"[:len(shape)]
            sizes = {names[i]: shape[i] for i in range(1, len(shape))}
            return flat.rearrange(f"p ({' '.join(names)}) -> p {' '.join(names)}", **sizes)

        xtmp = region(2, [HB, D])
        conv_in = arena[:, 12 * D:12 * D + CONV_IN].rearrange("p (a b) -> p a b", a=KT)
        xbc_in = arena[:, 12 * D + CONV_IN:12 * D + CONV_IN + XBC_IN].rearrange("p (a b) -> p a b", a=XT)
        yc = region(0, [KT, T])
        zs = region(2, [KT, T])
        ys = region(4, [KT, T])
        xc = region(6, [XT, T])
        decay = region(9, [HG, P])
        c_dec = region(10, [HG, P])
        xdt = region(11, [HG, HD])
        xdtd = arena[:, 11 * D + NW:12 * D].rearrange("p (a b) -> p a b", b=HD)
        qT = region(0, [J, T])
        xfn = region(12, [HB, D])
        cand = region(0, [PH * TOPK, TOPK]).rearrange("p (h a) b -> p h a b", a=TOPK)
        keys = region(4, [J, P])
        keysT = region(6, [J, P])
        sc = [region(8, [J, KEYS]), region(14, [J, KEYS])]
        sc2 = region(10, [HB * 4, KEYS])
        cand2 = region(4, [PH, TOPK * TOPK])
        hot = region(10, [SLOTS, TOPK])

        ident = sb("ident", [P, P])
        causalT = sb("causalT", [P, P])
        ones = sb("ones", [P, P])
        iota_i = sb("iota_i", [P, TOPK], I32)
        iota_f = sb("iota_f", [P, TOPK])
        ss = sb("ss", [P, HB])
        rstd = sb("rstd", [P, HB])
        ss2 = sb("ss2", [P, HB, 2])
        sums = sb("sums", [P, 3 * HB])
        fin = sb("fin", [P, 4, NBLK])
        rstd2 = sb("rstd2", [P, HB, 2])
        dall = sb("dall", [P, HEADS])
        dtb = sb("dtb", [P, HEADS])
        alog = sb("alog", [P, HEADS])
        expa = sb("expa", [P, HEADS])
        dts = sb("dts", [P, 6, HB, HEADS])
        dt = sb("dt", [P, HB, HEADS])
        a_ = sb("a_", [P, HB, HEADS])
        acum = sb("acum", [P, HB, 2, HEADS])
        d_in = sb("d_in", [P, HB, HEADS])
        d_chunk = sb("d_chunk", [P, HB, HEADS])
        cbm = sb("cbm", [P, P])
        b_tok = sb("b_tok", [P, P])
        sv = sb("sv", [P, HB, J, TOPK])
        si = sb("si", [P, HB, J, TOPK], U32)
        sif = sb("sif", [P, J, TOPK])
        tv = sb("tv", [P, PH, TOPK])
        ti = sb("ti", [P, PH, TOPK], U32)
        tq = sb("tq", [P, 2, SLOTS], U32)
        tqf = region(8, [2, SLOTS])
        ei = region(9, [2, SLOTS])
        eidx = arena[:, 8 * D + 2 * SLOTS:8 * D + 3 * SLOTS]
        idx_u = sb("idx_u", [P, HB, SLOTS], I32)
        gsum = sb("gsum", [P, PH])
        gate = sb("gate", [P, HB, SLOTS])
        act = sb("act", [P, HB, SLOTS])
        gl = sb("gl", [P, HB, SLOTS])
        idx_c = sb("idx_c", [P, HB, SLOTS], I32)
        gate_c = sb("gate_c", [P, HB, SLOTS])
        diag = sb("diag", [P, 2, 4, P])
        pT = region(0, [HB * PT, P])
        ptok = region(1, [HB, PLE])
        pT_all = region(0, [NBLK * PT, P])
        ptok_all = region(1, [NBLK, PLE])
        w_ple_all = region(10, [PT, D])
        out_rows = region(4, [NBLK, D])
        final_gain = region(8, [D])
        final_squares = region(9, [D])

        pp = ps("pp", [P, 2, 2, NW])
        px = ps("px", [P, NW])
        pm = ps("pm", [P, NW])
        pv = ps("pv", [P, D])
        ppt = pp[:, :, :, :].rearrange("p a b (c t) -> p a (b c) t", t=T)
        ppf = pp[:, :, :, :].rearrange("p a b n -> p (a b n)")
        pxt = px[:, :].rearrange("p (a b) -> p a b", b=P)

        s_const = sem("s_const")
        s_hload = sem("s_hload")
        w_in_sem = [Signal(sem("s_w_even"), 16 * (EVEN + 2), 16 * EVEN), Signal(sem("s_w_odd"), 16 * (ODD + 2), 16 * ODD)]
        small = Signal(sem("s_small"), SMALL)
        gains = Signal(sem("s_gain"), 16 * 3, early=16 * 2)
        keys_in = Signal(sem("s_keys"), 16)
        p_in = Signal(sem("s_p"), 16, early=0)
        sumsq = Signal(sem("s_sumsq"), 3, early=2)
        meansq = Signal(sem("s_meansq"), 3, early=2)
        rstds = Signal(sem("s_rstd"), 3, early=2)
        xns = Signal(sem("s_xn"), 6, early=4)
        tr_done = Signal(sem("s_transposed"), 6, early=4)
        xnT_done = Signal(sem("s_xnT"), 6, early=4)
        par_T = Signal(sem("s_params_transposed"), 1)
        par_done = Signal(sem("s_params"), 1)
        proj = Signal(sem("s_proj"), UNITS, early=UNITS - 4, head=1)
        hc_done = Signal(sem("s_hc"), 2)
        out_used = Signal(sem("s_out_used"), 4)
        expa_done = Signal(sem("s_expa"), 1)
        gc_in = Signal(sem("s_gc"), 2)
        z_exp = Signal(sem("s_z_exp"), 2)
        z_done = Signal(sem("s_z_done"), 2)
        xbc_cp = Signal(sem("s_xbc_copied"), XT // TPU)
        conv_done = Signal(sem("s_xbc_conv"), XT // TPU)
        silu_exp = Signal(sem("s_silu_exp"), XT // TPU)
        silu_done = Signal(sem("s_silu_done"), XT // TPU)
        yc_done = Signal(sem("s_yc"), 2)
        sq_done = Signal(sem("s_square"), 4)
        sq_used = Signal(sem("s_square_used"), 4)
        y_scaled = Signal(sem("s_y_scaled"), 2)
        dt_proj = Signal(sem("s_dt_proj"), 1)
        dt_raw = Signal(sem("s_dt_raw"), 1)
        dt_exp = Signal(sem("s_dt_exp"), 1)
        dt_ln = Signal(sem("s_dt_ln"), 1)
        dt_u = Signal(sem("s_dt_u"), 1)
        a_done = Signal(sem("s_a"), 1)
        acum_mm = Signal(sem("s_acum_mm"), 1)
        acum_cp = Signal(sem("s_acum"), 1)
        d_raw = Signal(sem("s_decay_raw"), 1)
        d_exp = Signal(sem("s_decay_exp"), 1)
        g_mm = Signal(sem("s_ssd_inputs"), 4)
        g_cbm = Signal(sem("s_cb_masked"), 4)
        g_x = Signal(sem("s_xdt"), 4)
        g_cdec = Signal(sem("s_decay_out"), 4)
        g_dif = Signal(sem("s_decay_diff"), 4)
        g_act = Signal(sem("s_decay_mats"), 4)
        g_mats = Signal(sem("s_ssd_mats"), 4)
        g_y = Signal(sem("s_ssd_y"), 4)
        g_used = Signal(sem("s_ssd_used"), 4)
        ys_done = Signal(sem("s_ys"), 2)
        ss2_ms = Signal(sem("s_ss2_ms"), 1)
        rstd2s = Signal(sem("s_rstd2"), 1)
        keysT_tr = Signal(sem("s_keysT_tr"), 4)
        keysT_cp = Signal(sem("s_keysT"), 4)
        qT_cp = Signal(sem("s_qT"), 4)
        score_mm = Signal(sem("s_scores_mm"), 4)
        score_cp = Signal(sem("s_scores"), 4)
        tv_sub = Signal(sem("s_gate_raw"), 2)
        tv_exp = Signal(sem("s_gate_exp"), 2)
        row_in = [Signal(sem(f"s_row{r}"), 16 * len(range(r, sum(n_rows.values()), RING))) for r in range(RING)]
        handed = Signal(sem("s_handed"), 2)
        used = {"u": Signal(sem("s_u_used"), n_rows["u"], head=n_rows["u"]),
                "vector": Signal(sem("s_v_added"), n_rows["vector"], head=n_rows["vector"]),
                "tensor": Signal(sem("s_v_multiplied"), n_rows["tensor"], head=n_rows["tensor"])}
        gelu_raw = Signal(sem("s_gelu_raw"), 2)
        gelu_exp = Signal(sem("s_gelu_exp"), 2)
        w_done = Signal(sem("s_weights"), 2)
        diag_done = Signal(sem("s_diag"), len(diag_groups))
        added = Signal(sem("s_block_added"), 2)
        held = sem("s_held")
        pT_tr = Signal(sem("s_pT_tr"), 1, early=0)
        pT_cp = Signal(sem("s_pT"), 1, early=0)
        pg_exp = Signal(sem("s_ple_exp"), 2, early=0)
        pg_used = Signal(sem("s_ple_exp_used"), 2, early=0)
        turn_end = sem("s_turn_end")
        s_vec = sem("s_vector_step")
        s_sca = sem("s_scalar_step")
        s_final_gain = sem("s_final_gain")
        last_w = [sem("s_last_gate_left"), sem("s_last_gate_right"), sem("s_last_w_ple")]
        last_p = sem("s_last_p")
        last_pT_tr, last_pT = sem("s_last_pT_tr"), sem("s_last_pT")
        last_sq, last_ms, last_ln = sem("s_last_sumsq"), sem("s_last_meansq"), sem("s_last_ln")
        last_rstd, last_xn = sem("s_last_rstd"), sem("s_last_xn")
        last_tr, last_xnT = sem("s_last_transposed"), sem("s_last_xnT")
        last_gate, last_exp = sem("s_last_gate"), sem("s_last_exp")
        last_ple, last_used = sem("s_last_ple"), sem("s_last_used")
        s_fin = sem("s_final")
        s_finsq = sem("s_final_sumsq")
        s_out = sem("s_out")

        def turn_barrier(eng, turn):
            eng.drain()
            eng.sem_inc(turn_end, 1)
            eng.wait_ge(turn_end, (turn + 1) * 4)
            eng.sem_inc(held, 1)

        x_v = x.rearrange("o (b p) d -> p (o b) d", p=P)
        out_v = out.rearrange("o (b p) d -> p (o b) d", p=P)
        p_v = p.rearrange("l o (b p) k -> p (l o b) k", p=P)
        win_v = w_in.rearrange("l (k p) n -> p (l k) n", p=P)
        wout_v = w_out.rearrange("l (k p) n -> p (l k) n", p=P)
        wq_v = peer_wq.rearrange("l (k p) n -> p (l k) n", p=P)
        wg_v = w_ple_gate.rearrange("l (k p) n -> p (l k) n", p=P)
        wp_v = w_ple.rearrange("l (k p) n -> p (l k) n", p=P)
        keys_v = peer_keys.rearrange("l h s (a q) d -> (l h s a) (q d)", q=J)
        rows = [(R_CONV, CONV_K * KT, conv_w.rearrange("l j (c p) -> (l j c) p", p=P)),
                (R_MCONV, MCONV_K * XT, mconv_w.rearrange("l j (c p) -> (l j c) p", p=P)),
                (R_MB, XT, mconv_b.rearrange("l (c p) -> (l c) p", p=P)),
                (R_CN, KT, conv_norm_w.rearrange("l (c p) -> (l c) p", p=P)),
                (R_SN, KT, ssd_norm_w.rearrange("l (c p) -> (l c) p", p=P))]
        u_rows = peer_u.rearrange("l e d -> (l e) d")
        v_rows = peer_v.rearrange("l e d -> (l e) d")

        block = c.enter_context(nc.Block())

        @block.sync
        def _(sp):
            def stream(src, par, turn, pos):
                if pos >= 2:
                    sp.wait_ge(proj.sem, proj.at(turn, pos - 1))
                    sp.sem_inc(held, 1)
                sp.dma_start(wbuf[:, par, 0:src.shape[1], :], src).then_inc(w_in_sem[par].sem, 16)

            def load_gain(row):
                sp.dma_start(gain[:, :], row.to_broadcast([P, D])).then_inc(gains.sem, 16)

            def embed(turn, half, layer, pos0):
                load_gain(norm_ple_w[layer:layer + 1, :])
                sp.dma_start(ptok[:, :, :], p_v[:, bass.ds(half * HB + layer * NBLK, HB), :]).then_inc(p_in.sem, 16)
                for i in range(4):
                    n, g = divmod(i, 2)
                    view, kt = ((wg_v, KT), (wp_v, PT))[g]
                    stream(view[:, layer * kt:(layer + 1) * kt, n * NW:(n + 1) * NW], i % 2, turn, pos0 + i)

            def mix(turn, half, layer, early):
                pos0 = 0 if early else 4
                norms = 0 if early else 1

                def load_unit(u):
                    if u < U_OUT:
                        src = win_v[:, layer * KT:(layer + 1) * KT, IN_COLS[u]:IN_COLS[u] + NW]
                    elif u < U_Q:
                        n, g = divmod(u - U_OUT, 2)
                        src = wout_v[:, (2 * layer + g) * KT:(2 * layer + g + 1) * KT, n * NW:(n + 1) * NW]
                    else:
                        n = u - U_Q
                        src = wq_v[:, layer * KT:(layer + 1) * KT, n * NW:(n + 1) * NW]
                    stream(src, u % 2, turn, pos0 + u)

                if not early:
                    sp.wait_ge(xns.sem, xns.at(turn, 2))
                    sp.sem_inc(held, 1)
                load_gain(norm_mix_w[layer:layer + 1, :])
                load_unit(0)
                for r0, n, view in rows:
                    sp.dma_start(params[r0:r0 + n, :], view[layer * n:(layer + 1) * n, :]).then_inc(small.sem, 16)
                sp.dma_start(wdt[:, :, :], win_v[:, layer * KT:(layer + 1) * KT, D_IN - HEADS:D_IN]).then_inc(small.sem, 16)
                sp.dma_start(dtb[:, :], dt_bias[layer:layer + 1, :].to_broadcast([P, HEADS])).then_inc(small.sem, 16)
                sp.dma_start(alog[:, :], a_log[layer:layer + 1, :].to_broadcast([P, HEADS])).then_inc(small.sem, 16)
                sp.dma_start(dall[:, :], d_skip[layer:layer + 1, :].to_broadcast([P, HEADS])).then_inc(small.sem, 16)
                for u in range(1, U_OUT):
                    load_unit(u)
                sp.wait_ge(xns.sem, xns.at(turn, norms * HB + 2))
                sp.sem_inc(held, 1)
                load_gain(norm_ffn_w[layer:layer + 1, :])
                for u in range(U_OUT, U_Q):
                    load_unit(u)
                load_unit(U_Q)
                sp.wait_ge(out_used.sem, out_used.at(turn, 4))
                sp.sem_inc(held, 1)
                sp.dma_start(keys.rearrange("p q d -> p (q d)"), keys_v[layer * P:(layer + 1) * P, :]).then_inc(keys_in.sem, 16)
                for u in range(U_Q + 1, U_PLE):
                    load_unit(u)

            sp.dma_start(h[:, :, :], x_v).then_inc(s_hload, 16)
            for turn in range(HALVES):
                mix(turn, turn, 0, True)
                turn_barrier(sp, turn)
            with sp.Fori(0, HALVES) as half:
                turn = half + HALVES
                embed(turn, half, 0, 0)
                mix(turn, half, 1, False)
                turn_barrier(sp, turn)
            sp.dma_start(ptok_all, p_v[:, NBLK:2 * NBLK, :]).then_inc(last_p, 16)
            load_gain(norm_ple_w[1:2, :])
            sp.dma_start(w_ple_all, wp_v[:, PT:2 * PT, :]).then_inc(last_w[2], 16)
            for n in range(2):
                sp.dma_start(wbuf[:, n, :, :], wg_v[:, KT:2 * KT, n * NW:(n + 1) * NW]).then_inc(last_w[n], 16)
            sp.dma_start(final_gain, final_norm_w.rearrange("(o d) -> o d", o=1).to_broadcast([P, D])).then_inc(s_final_gain, 16)
            for b in range(NBLK):
                sp.wait_ge(s_fin, b + 1)
                sp.dma_start(out_v[:, b, :], out_rows[:, b, :]).then_inc(s_out, 16)
            sp.wait_ge(s_out, 16 * NBLK)

        @block.gpsimd
        def _(g):
            g.memset(ident[:, :], 0.0).then_inc(s_const, 1)
            g.memset(ones[:, :], 1.0).then_inc(s_const, 1)
            g.iota(iota_i[:, :], pattern=[[1, TOPK]], base=0, channel_multiplier=0).then_inc(s_const, 1)
            g.wait_ge(s_const, 3)
            g.affine_select(out=ident[:, :], in_=ident[:, :], compare_op=ALU.not_equal, fill=1.0, base=0,
                            pattern=[[-1, P]], channel_multiplier=1).then_inc(s_const, 1)
            g.affine_select(out=causalT[:, :], in_=ones[:, :], compare_op=ALU.is_ge, fill=0.0, base=0,
                            pattern=[[1, P]], channel_multiplier=-1).then_inc(s_const, 1)

            g.wait_ge(s_const, 5)
            g.sem_inc(used["u"].sem, n_rows["u"])
            g.sem_inc(used["vector"].sem, n_rows["vector"])
            g.sem_inc(used["tensor"].sem, n_rows["tensor"])
            rows_of = [e for e in entries if e[0] in used]
            before_turn = {slot % RING: (who, nth) for who, _, _, slot, nth in rows_of}
            with g.Fori(0, 2 * HALVES) as bgt:
                g.wait_ge(handed.sem, handed.at(bgt, 1))
                g.sem_inc(held, 1)
                for i, (who, b, k, slot, nth) in enumerate(rows_of):
                    if who == "u" and b == 1 and k == 0:
                        g.wait_ge(handed.sem, handed.at(bgt, 2))
                        g.sem_inc(held, 1)
                    if who == "tensor" and group_of[b, k][1] == 0:
                        q = group_of[b, k][0]
                        _, k0, st, n = diag_groups[q]
                        if k == 0:
                            g.wait_ge(w_done.sem, w_done.at(bgt, b + 1))
                        if q >= 2:
                            g.wait_ge(used["tensor"].sem, used["tensor"].at(bgt, group_end[q - 2]))
                        g.sem_inc(held, 1)
                        g.tensor_tensor(diag[:, q % 2, 0:n, :], over(ident[:, :], 1, n),
                                        over(gl[:, b, k0:k0 + st * (n - 1) + 1:st], 2, P), ALU.mult).then_inc(diag_done.sem, 1)
                    if slot >= RING:
                        last, _, _, _, count = rows_of[i - RING]
                        g.wait_ge(used[last].sem, used[last].at(bgt, count))
                    else:
                        last, count = before_turn[slot]
                        g.wait_ge(used[last].sem, used[last].at(bgt, count - n_rows[last]))
                    g.sem_inc(held, 1)
                    g.indirect_dma_start(
                        out=ring[:, slot % RING, :], out_offset=None, in_=u_rows if who == "u" else v_rows,
                        in_offset=bass.IndirectOffsetOnAxis(ap=idx_c[:, b, k:k + 1], axis=0),
                    ).then_inc(row_in[slot % RING].sem, 16)

        @block.scalar
        def _(s):
            own = Steps(SCA_PER_ROUND)

            def idle(stage):
                pass

            def follow(kind, bgt):
                done = [UPTO[kind]["start"]]

                def background(stage):
                    for who, b, k, slot, nth in entries[done[0]:UPTO[kind][stage]]:
                        if who == "w1":
                            s.wait_ge(gelu_raw.sem, gelu_raw.at(bgt, b + 1))
                            s.activation(gl[:, b, :], gl[:, b, :], ACT.Exp, scale=-2.0 * GELU_C).then_inc(gelu_exp.sem, 1)
                    done[0] = UPTO[kind][stage]

                return background

            def norm(turn, half, n, name, background, between=None):
                for b in range(HB):
                    hb = h[:, bass.ds(half * HB + b, 1), :].rearrange("p o d -> p (o d)")
                    m = s.activation(etmp[:, 0:4, :].rearrange("p a b -> p (a b)"), hb, ACT.Square,
                                     accum_out=ss[:, b:b + 1])
                    if b == HB - 1:
                        m.then_inc(sumsq.sem, 1)
                    else:
                        m.then_inc(s_sca, own.one())
                        s.wait_ge(s_sca, own.so_far(turn))
                        s.sem_inc(held, 1)
                background(name + ".b")
                s.wait_ge(meansq.sem, meansq.at(turn, n + 1))
                s.activation(rstd[:, :], ss[:, :], ACT.Ln).then_inc(s_sca, own.one())
                s.wait_ge(s_sca, own.so_far(turn))
                s.activation(rstd[:, :], rstd[:, :], ACT.Exp, scale=-0.5).then_inc(rstds.sem, 1)
                if between is not None:
                    between()
                background(name + ".c")
                for b in range(HB):
                    s.wait_ge(tr_done.sem, tr_done.at(turn, n * HB + b + 1))
                    s.copy(xnT[:, :, b * P:(b + 1) * P],
                           ppf[:, b * D:(b + 1) * D].rearrange("p (a b) -> p a b", b=P)).then_inc(xnT_done.sem, 1)

            def embed(turn, half, n0, pos0, background):
                background("e_norm.a")
                if n0:
                    s.wait_ge(pg_used.sem, pg_used.at(turn, 2 * n0))
                    s.sem_inc(held, 1)
                norm(turn, half, n0, "e_norm", background)
                s.wait_ge(pT_tr.sem, pT_tr.at(turn, n0 + 1))
                s.copy(pT, pxt).then_inc(pT_cp.sem, 1)
                for n in range(2):
                    background(f"e{2 * n}.1")
                    s.wait_ge(proj.sem, proj.at(turn, pos0 + 2 * n + 1))
                    if n:
                        s.wait_ge(pg_used.sem, pg_used.at(turn, 2 * n0 + n))
                    else:
                        s.wait_ge(xnT_done.sem, xnT_done.at(turn, 2 * n0 + 2))
                    s.activation(etmp[:, :, :].rearrange("p a b -> p (a b)"), pp[:, 0].rearrange("p a b -> p (a b)"),
                                 ACT.Exp, scale=-1.0).then_inc(pg_exp.sem, 1)

            def mix(turn, half, early, background):
                pos0 = 0 if early else 4
                n0 = 0 if early else 1
                background("norm0.a")
                if not early:
                    s.wait_ge(pg_used.sem, pg_used.at(turn, 2))
                    s.sem_inc(held, 1)
                norm(turn, half, n0, "norm0", background)
                background("dt")
                s.wait_ge(par_T.sem, par_T.at(turn, 1))
                s.copy(paramsT[:, 0:ROWS], px[:, 0:ROWS]).then_inc(par_done.sem, 1)
                s.wait_ge(par_done.sem, par_done.at(turn, 1))
                s.wait_ge(small.sem, small.at(turn, SMALL))
                s.activation(expa[:, :], alog[:, :], ACT.Exp).then_inc(expa_done.sem, 1)
                s.wait_ge(dt_raw.sem, dt_raw.at(turn, 1))
                s.activation(dts[:, 2], dts[:, 1], ACT.Exp, scale=-1.0).then_inc(dt_exp.sem, 1)
                s.wait_ge(dt_u.sem, dt_u.at(turn, 1))
                s.activation(dts[:, 4], dts[:, 3], ACT.Ln).then_inc(dt_ln.sem, 1)
                for i in range(XT // TPU):
                    background(f"in{U_XBC + i}.3")
                    s.wait_ge(proj.sem, proj.at(turn, pos0 + U_XBC + i + 1))
                    s.copy(xbc_in[:, i * TPU:(i + 1) * TPU, MCONV_K - 1:], ppt[:, (U_XBC + i) % 2]).then_inc(xbc_cp.sem, 1)
                    if i:
                        s.wait_ge(silu_done.sem, silu_done.at(turn, i))
                    s.wait_ge(conv_done.sem, conv_done.at(turn, i + 1))
                    s.activation(etmp[:, :, :], xc[:, i * TPU:(i + 1) * TPU, :], ACT.Exp, scale=-1.0).then_inc(silu_exp.sem, 1)
                for i in range(2):
                    background(f"in{U_GC + i}.3")
                    s.wait_ge(proj.sem, proj.at(turn, pos0 + U_GC + i + 1))
                    s.copy(conv_in[:, i * TPU:(i + 1) * TPU, CONV_K - 1:], ppt[:, (U_GC + i) % 2]).then_inc(gc_in.sem, 1)
                for i in range(2):
                    background(f"in{U_Z + i}.3")
                    s.wait_ge(proj.sem, proj.at(turn, pos0 + U_Z + i + 1))
                    s.activation(zs[:, i * TPU:(i + 1) * TPU, :], ppt[:, (U_Z + i) % 2], ACT.Exp, scale=-1.0).then_inc(z_exp.sem, 1)
                background("cum0")
                s.wait_ge(d_raw.sem, d_raw.at(turn, 1))
                s.activation(d_in[:, :, :], d_in[:, :, :], ACT.Exp).then_inc(s_sca, own.one())
                s.activation(d_chunk[:, :, :], acum[:, :, 1, :], ACT.Exp).then_inc(d_exp.sem, 1)
                background(f"in{U_GB + 1}.3")
                s.wait_ge(silu_done.sem, silu_done.at(turn, XT // TPU))
                s.wait_ge(yc_done.sem, yc_done.at(turn, 1))
                s.activation(etmp[:, :, :], yc[:, 0:TPU, :], ACT.Square).then_inc(sq_done.sem, 1)
                for i in range(4):
                    background(f"ssd{i}a")
                    s.wait_ge(g_mm.sem, g_mm.at(turn, i + 1))
                    if i:
                        s.wait_ge(g_y.sem, g_y.at(turn, i))
                    s.activation(c_dec, ppf[:, 0:HG * P].rearrange("p (a b) -> p a b", b=P), ACT.Exp).then_inc(g_cdec.sem, 1)
                    background(f"ssd{i}b")
                    s.wait_ge(g_dif.sem, g_dif.at(turn, i + 1))
                    s.activation(decay, decay, ACT.Exp).then_inc(g_act.sem, 1)
                    if i == 0:
                        background("ssd0c")
                        s.wait_ge(yc_done.sem, yc_done.at(turn, 2))
                        s.wait_ge(sq_used.sem, sq_used.at(turn, 1))
                        s.activation(etmp[:, :, :], yc[:, TPU:, :], ACT.Square).then_inc(sq_done.sem, 1)
                background("ssd3c")
                s.wait_ge(sq_done.sem, sq_done.at(turn, 2))
                for t in range(KT):
                    m = s.activation(yc[:, t, :], yc[:, t, :], ACT.Copy, scale=paramsT[:, R_CN + t:R_CN + t + 1])
                m.then_inc(y_scaled.sem, 1)
                for b in range(HB):
                    background(f"post{b}")
                    s.wait_ge(ys_done.sem, ys_done.at(turn, b + 1))
                    s.wait_ge(sq_used.sem, sq_used.at(turn, 2 + b))
                    s.activation(etmp[:, :, :].rearrange("p a (b t) -> p (a b) t", t=P), ys[:, :, b * P:(b + 1) * P],
                                 ACT.Square).then_inc(sq_done.sem, 1)
                s.wait_ge(sq_done.sem, sq_done.at(turn, 4))
                for t in range(KT):
                    m = s.activation(ys[:, t, :], ys[:, t, :], ACT.Copy, scale=paramsT[:, R_SN + t:R_SN + t + 1])
                m.then_inc(y_scaled.sem, 1)
                s.wait_ge(ss2_ms.sem, ss2_ms.at(turn, 1))
                s.activation(rstd2[:, :, :], ss2[:, :, :], ACT.Ln).then_inc(s_sca, own.one())
                s.wait_ge(s_sca, own.so_far(turn))
                s.activation(rstd2[:, :, :], rstd2[:, :, :], ACT.Exp, scale=-0.5).then_inc(rstd2s.sem, 1)
                background("norm1.a")
                s.wait_ge(sq_used.sem, sq_used.at(turn, 4))
                s.wait_ge(out_used.sem, out_used.at(turn, 4))
                s.sem_inc(held, 1)

                def keys_in_columns():
                    background("keys")
                    for i in range(4):
                        s.wait_ge(keysT_tr.sem, keysT_tr.at(turn, i + 1))
                        s.copy(keysT.rearrange("d j n -> d (j n)").rearrange("d (r q) -> d q r", q=J)[:, i * 4:(i + 1) * 4, :],
                               (px, pm)[i % 2][:, :].rearrange("p (a b) -> p a b", b=P)).then_inc(keysT_cp.sem, 1)

                def scores(i):
                    s.wait_ge(score_mm.sem, score_mm.at(turn, i + 1))
                    for b in range(HB):
                        m = s.copy(sc[b][:, 4 * i:4 * i + 4, :], (px, pm)[b][:, :].rearrange("p (a b) -> p a b", b=P))
                    m.then_inc(score_cp.sem, 1)

                norm(turn, half, n0 + 1, "norm1", background, between=keys_in_columns)
                for i in range(4):
                    if i:
                        background(f"q{i}.2")
                        scores(i - 1)
                    background(f"q{i}.3")
                    s.wait_ge(proj.sem, proj.at(turn, pos0 + U_Q + i + 1))
                    s.copy(qT[:, i * TPU:(i + 1) * TPU, :], ppt[:, (U_Q + i) % 2]).then_inc(qT_cp.sem, 1)
                background("score")
                scores(3)
                for b in range(HB):
                    background(f"top{b}.6")
                    s.wait_ge(tv_sub.sem, tv_sub.at(turn, b + 1))
                    s.activation(gate[:, b, :], gate[:, b, :], ACT.Exp).then_inc(tv_exp.sem, 1)
                background("end")

            def last_block(b, background):
                background(f"last{b}.a")
                if b:
                    s.wait_ge(s_finsq, 4 * b)
                if b >= HB:
                    s.wait_ge(added.sem, added.at(2 * HALVES - 1, b - HB + 1))
                s.activation(final_squares, h[:, b, :], ACT.Square, accum_out=fin[:, 0, b:b + 1]).then_inc(last_sq, 1)
                background(f"last{b}.b")
                s.wait_ge(last_ms, b + 1)
                s.activation(fin[:, 1, b:b + 1], fin[:, 0, b:b + 1], ACT.Ln).then_inc(last_ln, 1)
                s.wait_ge(last_ln, b + 1)
                s.activation(fin[:, 1, b:b + 1], fin[:, 1, b:b + 1], ACT.Exp, scale=-0.5).then_inc(last_rstd, 1)
                background(f"last{b}.c")
                s.wait_ge(last_tr, b + 1)
                for i in range(2):
                    m = s.copy(xnT[:, i * 4:(i + 1) * 4, b % 2 * P:(b % 2 + 1) * P],
                               (px, pm)[i][:, :].rearrange("p (a b) -> p a b", b=P))
                m.then_inc(last_xnT, 1)
                for n in range(2):
                    background(f"last{b}." + "de"[n])
                    s.wait_ge(last_gate, 2 * b + n + 1)
                    if b:
                        s.wait_ge(last_used, 2 * b)
                    s.activation(etmp[:, 2 * n:2 * n + 2, :].rearrange("p a b -> p (a b)"), ppf[:, n * NW:(n + 1) * NW], ACT.Exp,
                                 scale=-1.0).then_inc(last_exp, 1)
                background(f"last{b}.f")
                s.wait_ge(last_used, 2 * b + 2)
                s.activation(final_squares, h[:, b, :], ACT.Square, accum_out=fin[:, 2, b:b + 1]).then_inc(s_finsq, 1)
                s.wait_ge(s_finsq, 4 * b + 2)
                s.activation(fin[:, 3, b:b + 1], fin[:, 2, b:b + 1], ACT.Ln).then_inc(s_finsq, 1)
                s.wait_ge(s_finsq, 4 * b + 3)
                s.activation(fin[:, 3, b:b + 1], fin[:, 3, b:b + 1], ACT.Exp, scale=-0.5).then_inc(s_finsq, 1)

            s.wait_ge(s_const, 5)
            s.wait_ge(s_hload, 16)
            mix(0, 0, True, follow("lead", 0))
            turn_barrier(s, 0)
            s.wait_ge(handed.sem, handed.at(0, 2))
            mix(1, 1, True, follow("mix", 0))
            turn_barrier(s, 1)
            before = own.n
            with s.Fori(0, HALVES) as half:
                turn = half + HALVES
                s.wait_ge(handed.sem, handed.at(turn - 1, 2))
                s.sem_inc(held, 1)
                background = follow("both", turn - 1)
                embed(turn, half, 0, 0, background)
                mix(turn, half, False, background)
                turn_barrier(s, turn)
            assert own.n - before == SCA_PER_ROUND, f"sca_turn={own.n - before}"
            own.n += SCA_PER_ROUND
            background = follow("last", 2 * HALVES - 1)
            s.wait_ge(last_pT_tr, 1)
            s.copy(pT_all, ppf[:, 0:NBLK * PLE].rearrange("p (a b) -> p a b", b=P)).then_inc(last_pT, 1)
            for b in range(NBLK - 1):
                last_block(b, background)
            background("end")
            last_block(NBLK - 1, idle)

        @block.vector
        def _(v):
            own = Steps(VEC_PER_ROUND)

            def h_of(half, b):
                return h[:, bass.ds(half * HB + b, 1), :].rearrange("p o d -> p (o d)")

            def h_cols(half, b, c0, n):
                return h[:, bass.ds(half * HB + b, 1), c0:c0 + n].rearrange("p o d -> p (o d)")

            def idle(stage):
                pass

            def follow(kind, bgt, bg_half, turn):
                done = [UPTO[kind]["start"]]

                def background(stage):
                    for who, b, k, slot, nth in entries[done[0]:UPTO[kind][stage]]:
                        if who == "u":
                            v.wait_ge(row_in[slot % RING].sem, row_in[slot % RING].at(bgt, 16 * (slot // RING + 1)))
                            v.scalar_tensor_tensor(out=ring[:, slot % RING, :], in0=ring[:, slot % RING, :], scalar=1.0,
                                                   in1=xf[:, b, :], op0=ALU.mult, op1=ALU.mult,
                                                   accum_out=act[:, b, k:k + 1]).then_inc(used["u"].sem, 1)
                        elif who == "vector":
                            v.wait_ge(row_in[slot % RING].sem, row_in[slot % RING].at(bgt, 16 * (slot // RING + 1)))
                            if nth > 1:
                                v.wait_ge(used["vector"].sem, used["vector"].at(bgt, nth - 1))
                            v.sem_inc(held, 1)
                            v.scalar_tensor_tensor(out=h_of(bg_half, b), in0=ring[:, slot % RING, :],
                                                   scalar=gl[:, b, k:k + 1], in1=h_of(bg_half, b), op0=ALU.mult,
                                                   op1=ALU.add).then_inc(used["vector"].sem, 1)
                        elif who == "w1":
                            v.wait_ge(used["u"].sem, used["u"].at(bgt, (b + 1) * P))
                            v.tensor_tensor(gl[:, b, :], act[:, b, :], act[:, b, :], ALU.mult).then_inc(s_vec, own.one())
                            v.wait_ge(s_vec, own.so_far(turn))
                            v.tensor_scalar(gl[:, b, :], gl[:, b, :], GELU_A, 1.0, ALU.mult, ALU.add).then_inc(s_vec, own.one())
                            v.wait_ge(s_vec, own.so_far(turn))
                            v.tensor_tensor(gl[:, b, :], gl[:, b, :], act[:, b, :], ALU.mult).then_inc(gelu_raw.sem, 1)
                        elif who == "w2":
                            v.wait_ge(gelu_exp.sem, gelu_exp.at(bgt, b + 1))
                            v.tensor_scalar_add(gl[:, b, :], gl[:, b, :], 1.0).then_inc(s_vec, own.one())
                            v.wait_ge(s_vec, own.so_far(turn))
                            v.reciprocal(gl[:, b, :], gl[:, b, :]).then_inc(s_vec, own.one())
                            v.wait_ge(s_vec, own.so_far(turn))
                            v.tensor_tensor(gl[:, b, :], gl[:, b, :], act[:, b, :], ALU.mult).then_inc(s_vec, own.one())
                            v.wait_ge(s_vec, own.so_far(turn))
                            v.tensor_tensor(gl[:, b, :], gl[:, b, :], gate_c[:, b, :], ALU.mult).then_inc(w_done.sem, 1)
                            v.wait_ge(w_done.sem, w_done.at(bgt, b + 1))
                        elif who == "add":
                            v.wait_ge(used["tensor"].sem, used["tensor"].at(bgt, tensor_rows[b]))
                            v.wait_ge(used["vector"].sem, used["vector"].at(bgt, vector_rows[b]))
                            v.sem_inc(held, 1)
                            v.tensor_tensor(h_of(bg_half, b), h_of(bg_half, b), pv[:, :], ALU.add).then_inc(added.sem, 1)
                    done[0] = UPTO[kind][stage]

                return background

            def hand_over(bgt, b):
                v.tensor_copy(xf[:, b, :], xfn[:, b, :])
                v.tensor_copy(gate_c[:, b, :], gate[:, b, :])
                v.tensor_copy(idx_c[:, b, :], idx_u[:, b, :]).then_inc(handed.sem, 1)
                v.wait_ge(handed.sem, handed.at(bgt, b + 1))
                v.sem_inc(held, 1)

            def norm(turn, half, n, out_rows, name, background):
                background(name + ".b")
                v.wait_ge(sumsq.sem, sumsq.at(turn, n + 1))
                v.tensor_scalar(ss[:, :], ss[:, :], 1.0 / D, EPS, ALU.mult, ALU.add).then_inc(meansq.sem, 1)
                v.wait_ge(gains.sem, gains.at(turn, 16 * (n + 1)))
                v.wait_ge(rstds.sem, rstds.at(turn, n + 1))
                for b in range(HB):
                    v.scalar_tensor_tensor(out=out_rows[:, b, :], in0=h_of(half, b), scalar=rstd[:, b:b + 1], in1=gain[:, :],
                                           op0=ALU.mult, op1=ALU.mult).then_inc(xns.sem, 1)

            def silu_tail(turn, out, e, arg, signal):
                v.tensor_scalar_add(e, e, 1.0).then_inc(s_vec, own.one())
                v.wait_ge(s_vec, own.so_far(turn))
                v.reciprocal(e, e).then_inc(s_vec, own.one())
                v.wait_ge(s_vec, own.so_far(turn))
                v.tensor_tensor(out, e, arg, ALU.mult).then_inc(signal.sem, 1)

            def embed(turn, half, n0, pos0, background):
                norm(turn, half, n0, xtmp, "e_norm", background)
                e2 = etmp[:, :, :].rearrange("p a b -> p (a b)")
                for n in range(2):
                    background(f"e{2 * n + 1}")
                    v.wait_ge(pg_exp.sem, pg_exp.at(turn, 2 * n0 + n + 1))
                    v.tensor_scalar_add(e2, e2, 1.0).then_inc(s_vec, own.one())
                    v.wait_ge(s_vec, own.so_far(turn))
                    v.reciprocal(e2, e2).then_inc(s_vec, own.one())
                    v.wait_ge(s_vec, own.so_far(turn))
                    v.wait_ge(proj.sem, proj.at(turn, pos0 + 2 * n + 2))
                    v.tensor_tensor(e2, e2, pp[:, 1].rearrange("p a b -> p (a b)"), ALU.mult).then_inc(s_vec, own.one())
                    v.wait_ge(s_vec, own.so_far(turn))
                    for b in range(HB):
                        hh = h_cols(half, b, n * NW, NW)
                        m = v.tensor_tensor(hh, hh, e2[:, b * NW:(b + 1) * NW], ALU.add)
                    m.then_inc(pg_used.sem, 1)

            def clear():
                v.memset(conv_past[:, :, :], 0.0)
                v.memset(xbc_past[:, :, :], 0.0)
                v.memset(state[:, :, :], 0.0).then_inc(s_vec, own.one())
                v.wait_ge(s_vec, own.n)

            def mix(turn, half, early, background):
                pos0 = 0 if early else 4
                n0 = 0 if early else 1
                v.tensor_copy(conv_in[:, :, 0:CONV_K - 1], conv_past[:, :, :]).then_inc(s_vec, own.one())
                v.tensor_copy(xbc_in[:, :, 0:MCONV_K - 1], xbc_past[:, :, :]).then_inc(s_vec, own.one())
                norm(turn, half, n0, xtmp, "norm0", background)
                background("dt")
                v.wait_ge(small.sem, small.at(turn, SMALL))
                for s_ in range(2):
                    v.tensor_copy(dskip[s_ * HD:(s_ + 1) * HD, :],
                                          dall[s_ * HD:(s_ + 1) * HD, :].rearrange("p (c s) -> p s c", s=2)[:, s_, :]).then_inc(s_vec, own.one())
                v.wait_ge(dt_proj.sem, dt_proj.at(turn, 1))
                v.tensor_tensor(dts[:, 0], pm[:, 0:HB * HEADS].rearrange("p (a b) -> p a b", b=HEADS),
                                         over(dtb[:, :], 1, HB), ALU.add).then_inc(s_vec, own.one())
                v.wait_ge(s_vec, own.so_far(turn))
                v.scalar_tensor_tensor(out=dts[:, 1], in0=dts[:, 0], scalar=-1.0, in1=dts[:, 0], op0=ALU.mult, op1=ALU.max).then_inc(dt_raw.sem, 1)
                v.tensor_scalar_max(dts[:, 0], dts[:, 0], 0.0).then_inc(s_vec, own.one())
                v.wait_ge(dt_exp.sem, dt_exp.at(turn, 1))
                v.tensor_scalar_add(dts[:, 3], dts[:, 2], 1.0).then_inc(dt_u.sem, 1)
                v.wait_ge(dt_u.sem, dt_u.at(turn, 1))
                v.reciprocal(dts[:, 5], dts[:, 3]).then_inc(s_vec, own.one())
                v.tensor_scalar_add(dt[:, :, :], dts[:, 3], -1.0).then_inc(s_vec, own.one())
                v.wait_ge(s_vec, own.so_far(turn))
                v.tensor_tensor(dts[:, 2], dts[:, 2], dt[:, :, :], ALU.subtract).then_inc(s_vec, own.one())
                v.wait_ge(s_vec, own.so_far(turn))
                v.tensor_tensor(dts[:, 2], dts[:, 2], dts[:, 5], ALU.mult).then_inc(s_vec, own.one())
                v.wait_ge(s_vec, own.so_far(turn))
                v.tensor_tensor(dts[:, 2], dts[:, 2], dts[:, 0], ALU.add).then_inc(s_vec, own.one())
                v.wait_ge(s_vec, own.so_far(turn))
                v.wait_ge(dt_ln.sem, dt_ln.at(turn, 1))
                v.tensor_tensor(dt[:, :, :], dts[:, 2], dts[:, 4], ALU.add).then_inc(s_vec, own.one())
                v.wait_ge(s_vec, own.so_far(turn))
                v.wait_ge(par_done.sem, par_done.at(turn, 1))
                v.wait_ge(expa_done.sem, expa_done.at(turn, 1))
                v.scalar_tensor_tensor(out=a_[:, :, :], in0=dt[:, :, :], scalar=-1.0, in1=over(expa[:, :], 1, HB),
                                       op0=ALU.mult, op1=ALU.mult).then_inc(a_done.sem, 1)
                for i in range(XT // TPU):
                    background(f"in{U_XBC + i}.3")
                    v.wait_ge(xbc_cp.sem, xbc_cp.at(turn, i + 1))

                    def mtap(j, t):
                        return paramsT[:, R_MCONV + j * XT + t:R_MCONV + j * XT + t + 1]

                    for j in range(MCONV_K):
                        for t in range(i * TPU, (i + 1) * TPU):
                            if j == 0:
                                m = v.tensor_scalar(xc[:, t, :], xbc_in[:, t, 0:T], mtap(0, t),
                                                    paramsT[:, R_MB + t:R_MB + t + 1], ALU.mult, ALU.add)
                            else:
                                m = v.scalar_tensor_tensor(out=xc[:, t, :], in0=xbc_in[:, t, j:j + T], scalar=mtap(j, t),
                                                           in1=xc[:, t, :], op0=ALU.mult, op1=ALU.add)
                            if j == MCONV_K - 1 and t == (i + 1) * TPU - 1:
                                m.then_inc(conv_done.sem, 1)
                            else:
                                m.then_inc(s_vec, own.one())
                        if j < MCONV_K - 1:
                            v.wait_ge(s_vec, own.so_far(turn))
                    v.wait_ge(silu_exp.sem, silu_exp.at(turn, i + 1))
                    silu_tail(turn, xc[:, i * TPU:(i + 1) * TPU, :], etmp[:, :, :], xc[:, i * TPU:(i + 1) * TPU, :], silu_done)
                v.tensor_copy(xbc_past[:, :, :], xbc_in[:, :, T:T + MCONV_K - 1]).then_inc(s_vec, own.one())
                for i in range(2):
                    tiles = slice(i * TPU, (i + 1) * TPU)
                    background(f"in{U_HC + i}.3")
                    v.wait_ge(proj.sem, proj.at(turn, pos0 + U_HC + i + 1))
                    v.wait_ge(gc_in.sem, gc_in.at(turn, 2))
                    v.tensor_tensor(conv_in[:, tiles, CONV_K - 1:], conv_in[:, tiles, CONV_K - 1:], ppt[:, (U_HC + i) % 2],
                                    ALU.mult).then_inc(hc_done.sem, 1)
                    v.wait_ge(hc_done.sem, hc_done.at(turn, i + 1))

                    def tap(j, t):
                        return paramsT[:, R_CONV + j * KT + t:R_CONV + j * KT + t + 1]

                    for j in range(CONV_K):
                        for t in range(i * TPU, (i + 1) * TPU):
                            if j == 0:
                                m = v.tensor_scalar(yc[:, t, :], conv_in[:, t, 0:T], tap(0, t), None, ALU.mult)
                            else:
                                m = v.scalar_tensor_tensor(out=yc[:, t, :], in0=conv_in[:, t, j:j + T], scalar=tap(j, t),
                                                           in1=yc[:, t, :], op0=ALU.mult, op1=ALU.add)
                            m.then_inc(s_vec, own.one())
                        v.wait_ge(s_vec, own.so_far(turn))
                v.tensor_copy(conv_past[:, :, :], conv_in[:, :, T:T + CONV_K - 1]).then_inc(s_vec, own.one())
                for i in range(2):
                    background(f"in{U_Z + i}.3")
                    v.wait_ge(z_exp.sem, z_exp.at(turn, i + 1))
                    silu_tail(turn, zs[:, i * TPU:(i + 1) * TPU, :], zs[:, i * TPU:(i + 1) * TPU, :], ppt[:, (U_Z + i) % 2], z_done)
                background("cum0")
                v.wait_ge(acum_mm.sem, acum_mm.at(turn, 1))
                v.tensor_copy(acum[:, :, :, :].rearrange("p a b c -> p (a b c)"), pm[:, 0:4 * HEADS]).then_inc(acum_cp.sem, 1)
                v.wait_ge(acum_cp.sem, acum_cp.at(turn, 1))
                v.tensor_tensor(d_in[:, :, :], acum[:, :, 1, :], acum[:, :, 0, :], ALU.subtract).then_inc(d_raw.sem, 1)
                background("cum1")
                v.wait_ge(d_exp.sem, d_exp.at(turn, 1))
                v.wait_ge(silu_done.sem, silu_done.at(turn, XT // TPU))
                for i in range(2):
                    tiles = slice(i * TPU, (i + 1) * TPU)
                    background(f"in{U_GB + i}.3")
                    v.wait_ge(proj.sem, proj.at(turn, pos0 + U_GB + i + 1))
                    v.tensor_tensor(yc[:, tiles, :], yc[:, tiles, :], ppt[:, (U_GB + i) % 2], ALU.mult).then_inc(yc_done.sem, 1)
                for i in range(4):
                    b, g = divmod(i, 2)
                    heads = slice(g * HG, (g + 1) * HG)
                    background(f"ssd{i}a")
                    v.wait_ge(g_mm.sem, g_mm.at(turn, i + 1))
                    if i:
                        v.wait_ge(g_y.sem, g_y.at(turn, i))
                    v.tensor_tensor(cbm[:, :], pm[:, P:2 * P], causalT[:, :], ALU.mult)
                    v.tensor_copy(b_tok[:, :], pm[:, 2 * P:3 * P])
                    v.tensor_tensor(xdt, pxt.rearrange("p a (b c) -> p (a b) c", c=HD),
                                             over(dt[:, b, heads], 2, HD), ALU.mult).then_inc(s_vec, own.one())
                    v.wait_ge(s_vec, own.so_far(turn))
                    v.tensor_tensor(xdtd, xdt, over(d_in[:, b, heads], 2, HD), ALU.mult).then_inc(s_vec, own.one())
                    v.wait_ge(g_cdec.sem, g_cdec.at(turn, i + 1))
                    for k in range(HG):
                        m = v.tensor_scalar(decay[:, k, :], ppf[:, k * P:(k + 1) * P],
                                            acum[:, b, 0, g * HG + k:g * HG + k + 1], 0.0, ALU.subtract, ALU.min)
                    m.then_inc(g_dif.sem, 1)
                    background(f"ssd{i}b")
                    v.wait_ge(g_act.sem, g_act.at(turn, i + 1))
                    v.tensor_tensor(c_dec, c_dec, over(xc[:, 10 + g, b * P:(b + 1) * P], 1, HG), ALU.mult)
                    v.tensor_tensor(decay, decay, over(cbm[:, :], 1, HG), ALU.mult).then_inc(g_mats.sem, 1)
                    background(f"ssd{i}c")
                    v.wait_ge(g_y.sem, g_y.at(turn, i + 1))
                    v.tensor_tensor(state[:, heads, :], state[:, heads, :],
                                             over(d_chunk[:, b, heads], 2, HD), ALU.mult).then_inc(s_vec, own.one())
                    v.wait_ge(s_vec, own.so_far(turn))
                    v.tensor_tensor(state[:, heads, :], state[:, heads, :],
                                            ppf[:, 3 * NW:4 * NW].rearrange("p (a b) -> p a b", b=HD), ALU.add).then_inc(s_vec, own.one())
                    for t in range(4):
                        tt = g * 4 + t
                        m = v.scalar_tensor_tensor(out=ys[:, tt, b * P:(b + 1) * P], in0=xc[:, tt, b * P:(b + 1) * P],
                                                   scalar=dskip[:, tt:tt + 1],
                                                   in1=ppf[:, 2 * NW + t * P:2 * NW + (t + 1) * P],
                                                   op0=ALU.mult, op1=ALU.add)
                    m.then_inc(g_used.sem, 1)
                    if g == 1:
                        v.wait_ge(g_used.sem, g_used.at(turn, i + 1))
                        v.tensor_tensor(ys[:, :, b * P:(b + 1) * P], ys[:, :, b * P:(b + 1) * P],
                                        zs[:, :, b * P:(b + 1) * P], ALU.mult).then_inc(ys_done.sem, 1)
                background("post1")
                v.wait_ge(sq_used.sem, sq_used.at(turn, 4))
                v.tensor_copy(sums[:, :], pm[:, SUMS:SUMS + 6]).then_inc(s_vec, own.one())
                v.wait_ge(s_vec, own.so_far(turn))
                v.tensor_tensor(sums[:, 0:HB], sums[:, 0:HB], sums[:, HB:2 * HB], ALU.add).then_inc(s_vec, own.one())
                v.wait_ge(s_vec, own.so_far(turn))
                v.tensor_scalar(ss2[:, :, 0], sums[:, 0:HB], 1.0 / D, EPS, ALU.mult, ALU.add)
                v.tensor_scalar(ss2[:, :, 1], sums[:, 2 * HB:3 * HB], 1.0 / D, EPS, ALU.mult,
                                ALU.add).then_inc(ss2_ms.sem, 1)
                v.wait_ge(rstd2s.sem, rstd2s.at(turn, 1))
                for i in range(4):
                    n, g = divmod(i, 2)
                    background(f"out{i}.1")
                    v.wait_ge(proj.sem, proj.at(turn, pos0 + U_OUT + i + 1))
                    for b in range(HB):
                        hh = h_cols(half, b, n * NW, NW)
                        m = v.scalar_tensor_tensor(out=hh, in0=pp[:, (U_OUT + i) % 2, b, :], scalar=rstd2[:, b, g:g + 1],
                                                   in1=hh, op0=ALU.mult, op1=ALU.add)
                        if b == HB - 1:
                            m.then_inc(out_used.sem, 1)
                    v.wait_ge(out_used.sem, out_used.at(turn, i + 1))
                background("norm1.a")
                norm(turn, half, n0 + 1, xfn, "norm1", background)
                for i in range(4):
                    background(f"q{i + 1}.3" if i < 3 else "best")
                    v.wait_ge(score_cp.sem, score_cp.at(turn, i + 1))
                    v.sem_inc(held, 1)
                    four = [(b, j) for b in range(HB) for j in range(4 * i, 4 * i + 4)]
                    for b, j in four:
                        v.max(out=sv[:, b, j, 0:8], in_=sc[b][:, j, :]).then_inc(s_vec, own.one())
                    v.wait_ge(s_vec, own.so_far(turn))
                    v.sem_inc(held, 1)
                    for b, j in four:
                        v.max_index(out=si[:, b, j, 0:8], in_max=sv[:, b, j, 0:8], in_values=sc[b][:, j, :]).then_inc(s_vec, own.one())
                        v.match_replace(out=sc2[:, b * 4 + j % 4, :], in_to_replace=sv[:, b, j, 0:8], in_values=sc[b][:, j, :],
                                        imm_value=NEG).then_inc(s_vec, own.one())
                    v.wait_ge(s_vec, own.so_far(turn))
                    v.sem_inc(held, 1)
                    for b, j in four:
                        v.max(out=sv[:, b, j, 8:16], in_=sc2[:, b * 4 + j % 4, :]).then_inc(s_vec, own.one())
                    v.wait_ge(s_vec, own.so_far(turn))
                    v.sem_inc(held, 1)
                    for b, j in four:
                        v.max_index(out=si[:, b, j, 8:16], in_max=sv[:, b, j, 8:16],
                                    in_values=sc2[:, b * 4 + j % 4, :]).then_inc(s_vec, own.one())
                v.wait_ge(s_vec, own.so_far(turn))
                v.sem_inc(held, 1)
                for b in range(HB):
                    if b:
                        hand_over(turn, 0)
                    background(f"top{b}.0")
                    svp = sv[:, b, :, :].rearrange("p (h s) k -> p h s k", s=2)
                    v.tensor_copy(sif[:, :, :], si[:, b, :, :]).then_inc(s_vec, own.one())
                    v.tensor_tensor(cand[:, :, :, :], over(svp[:, :, 0, :], 3, TOPK), over(svp[:, :, 1, :], 2, TOPK),
                                             ALU.add).then_inc(s_vec, own.one())
                    background(f"top{b}.1")
                    v.wait_ge(s_vec, own.so_far(turn))
                    v.sem_inc(held, 1)
                    cf = cand[:, :, :, :].rearrange("p h a b -> p h (a b)")
                    for j in range(PH):
                        v.max(out=tv[:, j, 0:8], in_=cf[:, j, :]).then_inc(s_vec, own.one())
                    background(f"top{b}.2")
                    v.wait_ge(s_vec, own.so_far(turn))
                    v.sem_inc(held, 1)
                    for j in range(PH):
                        v.max_index(out=ti[:, j, 0:8], in_max=tv[:, j, 0:8], in_values=cf[:, j, :]).then_inc(s_vec, own.one())
                        v.match_replace(out=cand2[:, j, :], in_to_replace=tv[:, j, 0:8], in_values=cf[:, j, :],
                                                imm_value=NEG).then_inc(s_vec, own.one())
                    background(f"top{b}.3")
                    v.wait_ge(s_vec, own.so_far(turn))
                    v.sem_inc(held, 1)
                    for j in range(PH):
                        v.max(out=tv[:, j, 8:16], in_=cand2[:, j, :]).then_inc(s_vec, own.one())
                    background(f"top{b}.4")
                    v.wait_ge(s_vec, own.so_far(turn))
                    v.sem_inc(held, 1)
                    for j in range(PH):
                        v.max_index(out=ti[:, j, 8:16], in_max=tv[:, j, 8:16], in_values=cand2[:, j, :]).then_inc(s_vec, own.one())
                    background(f"top{b}.5")
                    v.wait_ge(s_vec, own.so_far(turn))
                    v.sem_inc(held, 1)
                    gb = gate[:, b, :].rearrange("p (h k) -> p h k", k=TOPK)
                    v.tensor_tensor(gb, tv[:, :, :], tv[:, :, 0:1].to_broadcast([P, PH, TOPK]),
                                    ALU.subtract).then_inc(tv_sub.sem, 1)
                    tif = ti[:, :, :].rearrange("p h k -> p (h k)")
                    v.tensor_single_scalar(tq[:, 0, :], tif, 4, ALU.logical_shift_right).then_inc(s_vec, own.one())
                    v.tensor_single_scalar(tq[:, 1, :], tif, 15, ALU.bitwise_and).then_inc(s_vec, own.one())
                    v.wait_ge(s_vec, own.so_far(turn))
                    v.tensor_copy(tqf[:, :, :], tq[:, :, :]).then_inc(s_vec, own.one())
                    v.wait_ge(s_vec, own.so_far(turn))
                    background(f"top{b}.6")
                    for s_ in range(2):
                        v.tensor_tensor(hot, over(tqf[:, s_, :], 2, TOPK), over(iota_f[:, :], 1, SLOTS), ALU.is_equal).then_inc(s_vec, own.one())
                        v.wait_ge(s_vec, own.so_far(turn))
                        h4 = hot.rearrange("p (h k) j -> p h k j", k=TOPK)
                        sel = over(sif[:, :, :].rearrange("p (h s) k -> p h s k", s=2)[:, :, s_, :], 2, TOPK)
                        v.tensor_tensor(h4, h4, sel, ALU.mult).then_inc(s_vec, own.one())
                        v.wait_ge(s_vec, own.so_far(turn))
                        v.tensor_reduce(out=ei[:, s_, :], in_=hot, axis=AX.X, op=ALU.add).then_inc(s_vec, own.one())
                        v.wait_ge(s_vec, own.so_far(turn))
                    v.scalar_tensor_tensor(out=eidx, in0=ei[:, 0, :], scalar=float(KEYS), in1=ei[:, 1, :],
                                                    op0=ALU.mult, op1=ALU.add).then_inc(s_vec, own.one())
                    v.wait_ge(s_vec, own.so_far(turn))
                    if not early:
                        v.tensor_scalar_add(eidx, eidx, float(EXPERTS)).then_inc(s_vec, own.one())
                        v.wait_ge(s_vec, own.so_far(turn))
                    v.tensor_copy(idx_u[:, b, :], eidx).then_inc(s_vec, own.one())
                    background(f"top{b}.7")
                    v.wait_ge(tv_exp.sem, tv_exp.at(turn, b + 1))
                    v.tensor_reduce(out=gsum[:, :], in_=gb, axis=AX.X, op=ALU.add).then_inc(s_vec, own.one())
                    v.wait_ge(s_vec, own.so_far(turn))
                    v.reciprocal(gsum[:, :], gsum[:, :]).then_inc(s_vec, own.one())
                    v.wait_ge(s_vec, own.so_far(turn))
                    v.tensor_tensor(gb, gb, over(gsum[:, :], 2, TOPK), ALU.mult).then_inc(s_vec, own.one())
                    v.wait_ge(s_vec, own.so_far(turn))
                background("end")

            def last_block(b, background):
                background(f"last{b}.b")
                v.wait_ge(last_sq, b + 1)
                v.tensor_scalar(fin[:, 0, b:b + 1], fin[:, 0, b:b + 1], 1.0 / D, EPS, ALU.mult, ALU.add).then_inc(last_ms, 1)
                v.wait_ge(gains.sem, gains.at(2 * HALVES, 16))
                v.wait_ge(last_rstd, b + 1)
                v.scalar_tensor_tensor(out=xtmp[:, b % 2, :], in0=h[:, b, :], scalar=fin[:, 1, b:b + 1], in1=gain[:, :],
                                       op0=ALU.mult, op1=ALU.mult).then_inc(last_xn, 1)
                background(f"last{b}.e")
                for n in range(2):
                    e2 = etmp[:, 2 * n:2 * n + 2, :].rearrange("p a b -> p (a b)")
                    hh = h[:, b, n * NW:(n + 1) * NW]
                    v.wait_ge(last_exp, 2 * b + n + 1)
                    v.tensor_scalar_add(e2, e2, 1.0).then_inc(s_vec, own.one())
                    v.wait_ge(s_vec, own.n)
                    v.reciprocal(e2, e2).then_inc(s_vec, own.one())
                    v.wait_ge(s_vec, own.n)
                    v.wait_ge(last_ple, b + 1)
                    v.tensor_tensor(e2, e2, ppf[:, D + n * NW:D + (n + 1) * NW], ALU.mult).then_inc(s_vec, own.one())
                    v.wait_ge(s_vec, own.n)
                    v.tensor_tensor(hh, hh, e2, ALU.add).then_inc(last_used, 1)
                background(f"last{b}.f")
                v.wait_ge(s_finsq, 4 * b + 1)
                v.tensor_scalar(fin[:, 2, b:b + 1], fin[:, 2, b:b + 1], 1.0 / D, EPS, ALU.mult, ALU.add).then_inc(s_finsq, 1)
                v.wait_ge(s_final_gain, 16)
                v.wait_ge(s_finsq, 4 * b + 4)
                v.scalar_tensor_tensor(out=out_rows[:, b, :], in0=h[:, b, :], scalar=fin[:, 3, b:b + 1], in1=final_gain,
                                       op0=ALU.mult, op1=ALU.mult).then_inc(s_fin, 1)

            v.wait_ge(s_const, 5)
            v.tensor_copy(iota_f[:, :], iota_i[:, :]).then_inc(s_vec, own.one())
            clear()
            v.wait_ge(s_hload, 16)
            mix(0, 0, True, follow("lead", 0, 0, 0))
            turn_barrier(v, 0)
            hand_over(0, 1)
            mix(1, 1, True, follow("mix", 0, 0, 1))
            clear()
            turn_barrier(v, 1)
            before = own.n
            with v.Fori(0, HALVES) as half:
                turn = half + HALVES
                hand_over(turn - 1, 1)
                background = follow("both", turn - 1, 1 - half, turn)
                embed(turn, half, 0, 0, background)
                mix(turn, half, False, background)
                turn_barrier(v, turn)
            assert own.n - before == VEC_PER_ROUND, f"vec_turn={own.n - before}"
            own.n += VEC_PER_ROUND
            turn = 2 * HALVES
            hand_over(turn - 1, 1)
            background = follow("last", turn - 1, 1, turn)
            for b in range(NBLK - 1):
                last_block(b, background)
            background("end")
            last_block(NBLK - 1, idle)

        @block.tensor
        def _(t):
            etf = etmp[:, :, :].rearrange("p a b -> p (a b)")

            def idle(stage):
                pass

            def follow(kind, bgt):
                done = [UPTO[kind]["start"]]

                def background(stage):
                    for who, b, k, slot, nth in entries[done[0]:UPTO[kind][stage]]:
                        if who != "tensor":
                            continue
                        q, j = group_of[b, k]
                        first = k == 0
                        last = nth == tensor_rows[b]
                        if j == 0:
                            t.wait_ge(diag_done.sem, diag_done.at(bgt, q + 1))
                        if first and b:
                            t.wait_ge(added.sem, added.at(bgt, b))
                        t.wait_ge(row_in[slot % RING].sem, row_in[slot % RING].at(bgt, 16 * (slot // RING + 1)))
                        for n in range(D // NW):
                            mm = t.matmul(pv[:, n * NW:(n + 1) * NW], diag[:, q % 2, j, :],
                                          ring[:, slot % RING, n * NW:(n + 1) * NW], start=first, stop=last)
                        mm.then_inc(used["tensor"].sem, 1)
                    done[0] = UPTO[kind][stage]

                return background

            def block_of(tile, k, b):
                return tile[:, k, b * P:(b + 1) * P]

            def norm_T(turn, n, rows_in, name, background):
                background(name + ".c")
                for b in range(HB):
                    t.wait_ge(xns.sem, xns.at(turn, n * HB + b + 1))
                    for k in range(KT):
                        mm = t.transpose(ppf[:, b * D + k * P:b * D + (k + 1) * P], rows_in[:, b, k * P:(k + 1) * P],
                                         ident[:, :])
                    mm.then_inc(tr_done.sem, 1)

            def embed(turn, n0, pos0, background):
                background("e_norm.a")
                t.wait_ge(p_in.sem, p_in.at(turn, 16 * (n0 + 1)))
                for b in range(HB):
                    for k in range(PT):
                        m_ = b * PT + k
                        mm = t.transpose(px[:, m_ * P:(m_ + 1) * P], ptok[:, b, k * P:(k + 1) * P], ident[:, :])
                mm.then_inc(pT_tr.sem, 1)
                norm_T(turn, n0, xtmp, "e_norm", background)
                for i in range(4):
                    n, g = divmod(i, 2)
                    if g == 0:
                        background(f"e{i}.0")
                        if i == 0:
                            t.wait_ge(xnT_done.sem, xnT_done.at(turn, n0 * HB + HB))
                        else:
                            t.wait_ge(pg_exp.sem, pg_exp.at(turn, 2 * n0 + n))
                    else:
                        background(f"e{i}")
                        if i == 1:
                            t.wait_ge(pT_cp.sem, pT_cp.at(turn, n0 + 1))
                        else:
                            t.wait_ge(pg_used.sem, pg_used.at(turn, 2 * n0 + n))
                    t.wait_ge(w_in_sem[g].sem, w_in_sem[g].at(turn, 16 * (2 * n0 + n + 1)))
                    nk = (KT, PT)[g]
                    for b in range(HB):
                        if g == 0 and b:
                            background(f"e{i}.1")
                        for k in range(nk):
                            lhs = pT[:, b * PT + k, :] if g else block_of(xnT, k, b)
                            mm = t.matmul(pp[:, g, b, :], lhs, wbuf[:, g, k, :], start=(k == 0), stop=(k == nk - 1))
                    mm.then_inc(proj.sem, 1)

            def mix(turn, early, background):
                n0 = 0 if early else 1

                def weights(u):
                    t.wait_ge(w_in_sem[u % 2].sem, w_in_sem[u % 2].at(turn, 16 * (u // 2 + 1 + 2 * n0)))

                def tiles_unit(u, name):
                    weights(u)
                    for m in range(TPU):
                        if m:
                            background(f"{name}.{m}")
                        for k in range(KT):
                            mm = t.matmul(ppt[:, u % 2, m, :], wbuf[:, u % 2, k, m * P:(m + 1) * P], xnT[:, k, :],
                                          start=(k == 0), stop=(k == KT - 1))
                    mm.then_inc(proj.sem, 1)

                norm_T(turn, n0, xtmp, "norm0", background)
                background("dt")
                t.wait_ge(xnT_done.sem, xnT_done.at(turn, n0 * HB + HB))
                t.wait_ge(small.sem, small.at(turn, SMALL))
                t.transpose(px[:, 0:ROWS], params[0:ROWS, :], ident[0:ROWS, 0:ROWS]).then_inc(par_T.sem, 1)
                for b in range(HB):
                    for k in range(KT):
                        mm = t.matmul(pm[:, b * HEADS:(b + 1) * HEADS], block_of(xnT, k, b), wdt[:, k, :],
                                      start=(k == 0), stop=(k == KT - 1))
                mm.then_inc(dt_proj.sem, 1)
                readers = [(U_XBC, xbc_cp), (U_GC, gc_in), (U_HC, hc_done), (U_Z, z_done), (U_GB, yc_done)]
                for u in range(U_OUT):
                    if u == U_GB:
                        background("cum0")
                        t.wait_ge(a_done.sem, a_done.at(turn, 1))
                        for b in range(HB):
                            t.matmul(pm[:, b * 2 * HEADS:(b * 2 + 1) * HEADS], causalT[:, :], a_[:, b, :], start=True, stop=True)
                            mm = t.matmul(pm[:, (b * 2 + 1) * HEADS:(b * 2 + 2) * HEADS], ones[:, :], a_[:, b, :], start=True, stop=True)
                        mm.then_inc(acum_mm.sem, 1)
                    background(f"in{u}.0")
                    if u >= 2:
                        first, reader = [w for w in readers if w[0] <= u - 2][-1]
                        t.wait_ge(reader.sem, reader.at(turn, u - 2 - first + 1))
                    tiles_unit(u, f"in{u}")

                def inputs(i):
                    b, g = divmod(i, 2)
                    t.matmul(pm[:, P:2 * P], block_of(xc, KT + g, b), block_of(xc, KT + 2 + g, b), start=True, stop=True)
                    t.transpose(pm[:, 2 * P:3 * P], block_of(xc, KT + g, b), ident[:, :])
                    for m in range(TPU):
                        t.transpose(px[:, m * P:(m + 1) * P], block_of(xc, g * TPU + m, b), ident[:, :])
                    for k in range(HG):
                        col = a_[:, b, g * HG + k:g * HG + k + 1].to_broadcast([P, P])
                        mm = t.matmul(ppf[:, k * P:(k + 1) * P], col, causalT[:, :], start=True, stop=True)
                    mm.then_inc(g_mm.sem, 1)

                background("ssd0a")
                t.wait_ge(acum_cp.sem, acum_cp.at(turn, 1))
                t.wait_ge(silu_done.sem, silu_done.at(turn, XT // TPU))
                t.wait_ge(yc_done.sem, yc_done.at(turn, 2))
                inputs(0)
                for i in range(4):
                    b, g = divmod(i, 2)
                    background(f"ssd{i}c")
                    t.wait_ge(g_act.sem, g_act.at(turn, i + 1))
                    if i < 2:
                        t.wait_ge(sq_done.sem, sq_done.at(turn, i + 1))
                        for b_ in range(HB):
                            for m in range(TPU):
                                mm = t.matmul(pm[:, SUMS + i * HB + b_:SUMS + i * HB + b_ + 1], block_of(etmp, m, b_),
                                              ones[:, 0:1], start=(m == 0), stop=(m == TPU - 1))
                        mm.then_inc(sq_used.sem, 1)
                    if i < 3:
                        inputs(i + 1)
                    t.wait_ge(g_mats.sem, g_mats.at(turn, i + 1))
                    if i:
                        t.wait_ge(g_used.sem, g_used.at(turn, i))
                    for k in range(HG):
                        y = ppf[(k % 2) * HD:(k % 2 + 1) * HD, 2 * NW + (k // 2) * P:2 * NW + (k // 2 + 1) * P]
                        t.matmul(y, xdt[:, k, :], decay[:, k, :], start=True, stop=False)
                        t.matmul(y, state[:, g * HG + k, :], c_dec[:, k, :], start=False, stop=True)
                    t.matmul(ppf[:, 3 * NW:4 * NW], b_tok[:, :], xdtd.rearrange("p a b -> p (a b)"), start=True,
                             stop=True).then_inc(g_y.sem, 1)
                for b in range(HB):
                    background(f"post{b}")
                    t.wait_ge(sq_done.sem, sq_done.at(turn, 2 + b + 1))
                    for m in range(KT):
                        mm = t.matmul(pm[:, SUMS + 2 * HB + b:SUMS + 2 * HB + b + 1], etf[:, m * P:(m + 1) * P],
                                      ones[:, 0:1], start=(m == 0), stop=(m == KT - 1))
                    mm.then_inc(sq_used.sem, 1)
                for i in range(4):
                    n, g = divmod(i, 2)
                    for b in range(HB):
                        background(f"out{i}.{b}")
                        if b == 0:
                            if i == 0:
                                t.wait_ge(y_scaled.sem, y_scaled.at(turn, 2))
                            if i >= 2:
                                t.wait_ge(out_used.sem, out_used.at(turn, i - 1))
                            weights(U_OUT + i)
                        for k in range(KT):
                            mm = t.matmul(pp[:, (U_OUT + i) % 2, b, :], block_of((yc, ys)[g], k, b),
                                          wbuf[:, (U_OUT + i) % 2, k, :], start=(k == 0), stop=(k == KT - 1))
                    mm.then_inc(proj.sem, 1)
                background("keys")
                t.wait_ge(keys_in.sem, keys_in.at(turn, 16))
                for i in range(J // 4):
                    if i >= 2:
                        t.wait_ge(keysT_cp.sem, keysT_cp.at(turn, i - 1))
                    for m in range(4):
                        mm = t.transpose((px, pm)[i % 2][:, m * P:(m + 1) * P], keys[:, i * 4 + m, :], ident[:, :])
                    mm.then_inc(keysT_tr.sem, 1)

                def scores(i):
                    t.wait_ge(qT_cp.sem, qT_cp.at(turn, i + 1))
                    if i:
                        t.wait_ge(score_cp.sem, score_cp.at(turn, i))
                    else:
                        t.wait_ge(keysT_cp.sem, keysT_cp.at(turn, 4))
                    for b in range(HB):
                        for j in range(4):
                            mm = t.matmul((px, pm)[b][:, j * KEYS:(j + 1) * KEYS], block_of(qT, 4 * i + j, b),
                                          keysT[:, 4 * i + j, :], start=True, stop=True)
                    mm.then_inc(score_mm.sem, 1)

                norm_T(turn, n0 + 1, xfn, "norm1", background)
                for i in range(4):
                    background(f"q{i}.0")
                    if i == 0:
                        t.wait_ge(xnT_done.sem, xnT_done.at(turn, (n0 + 1) * HB + HB))
                    if i >= 2:
                        t.wait_ge(qT_cp.sem, qT_cp.at(turn, i - 1))
                    weights(U_Q + i)
                    for m in range(TPU):
                        if m:
                            background(f"q{i}.{m}")
                        if m == 1 and i:
                            scores(i - 1)
                        for k in range(KT):
                            mm = t.matmul(ppt[:, (U_Q + i) % 2, m, :], wbuf[:, (U_Q + i) % 2, k, m * P:(m + 1) * P],
                                          xnT[:, k, :], start=(k == 0), stop=(k == KT - 1))
                    mm.then_inc(proj.sem, 1)
                background("score")
                scores(3)
                background("end")

            def last_block(b, background):
                background(f"last{b}.c")
                if b:
                    t.wait_ge(last_used, 2 * b)
                else:
                    t.wait_ge(last_pT, 1)
                    t.wait_ge(last_w[2], 16)
                for n in range(2):
                    for k in range(PT):
                        mm = t.matmul(ppf[:, D + n * NW:D + (n + 1) * NW], pT_all[:, b * PT + k, :],
                                      w_ple_all[:, k, n * NW:(n + 1) * NW], start=(k == 0), stop=(k == PT - 1))
                mm.then_inc(last_ple, 1)
                t.wait_ge(last_xn, b + 1)
                for k in range(KT):
                    mm = t.transpose((px, pm)[k // 4][:, k % 4 * P:(k % 4 + 1) * P], xtmp[:, b % 2, k * P:(k + 1) * P],
                                     ident[:, :])
                mm.then_inc(last_tr, 1)
                for n in range(2):
                    background(f"last{b}." + "de"[n])
                    if n == 0:
                        t.wait_ge(last_xnT, b + 1)
                    if b == 0:
                        t.wait_ge(last_w[n], 16)
                    for k in range(KT):
                        mm = t.matmul(ppf[:, n * NW:(n + 1) * NW], xnT[:, k, b % 2 * P:(b % 2 + 1) * P], wbuf[:, n, k, :],
                                      start=(k == 0), stop=(k == KT - 1))
                    mm.then_inc(last_gate, 1)

            t.wait_ge(s_const, 5)
            t.sem_inc(proj.sem, 1)
            mix(0, True, follow("lead", 0))
            turn_barrier(t, 0)
            mix(1, True, follow("mix", 0))
            turn_barrier(t, 1)
            with t.Fori(0, HALVES) as half:
                turn = half + HALVES
                background = follow("both", turn - 1)
                embed(turn, 0, 0, background)
                mix(turn, False, background)
                turn_barrier(t, turn)
            background = follow("last", 2 * HALVES - 1)
            t.wait_ge(last_p, 16)
            for b in range(NBLK):
                for k in range(PT):
                    m_ = b * PT + k
                    mm = t.transpose(ppf[:, m_ * P:(m_ + 1) * P], ptok_all[:, b, k * P:(k + 1) * P], ident[:, :])
            mm.then_inc(last_pT_tr, 1)
            for b in range(NBLK - 1):
                last_block(b, background)
            background("end")
            last_block(NBLK - 1, idle)


_INS = ['x', 'p', 'norm_mix_w', 'w_in', 'conv_w', 'mconv_w', 'mconv_b', 'dt_bias', 'a_log', 'd_skip', 'conv_norm_w',
        'ssd_norm_w', 'w_out', 'norm_ffn_w', 'peer_wq', 'peer_keys', 'peer_u', 'peer_v', 'norm_ple_w', 'w_ple_gate',
        'w_ple', 'final_norm_w']


def kernel(**inputs):
    import numpy as _np
    import concourse.bacc as _bacc
    from concourse import mybir as _mybir
    from concourse.bass_utils import run_bass_kernel_spmd as _run

    nc = _bacc.Bacc("TRN2", target_bir_lowering=False, num_devices=1)
    arrays, args = {}, []
    for name in _INS:
        a = _np.ascontiguousarray(inputs[name])
        arrays[f"in_{name}_dram"] = a
        args.append(nc.dram_tensor(f"in_{name}_dram", a.shape, _mybir.dt.from_np(a.dtype), kind="ExternalInput").ap())
    shape = inputs["x"].shape
    args.append(nc.dram_tensor("out_0_dram", shape, _mybir.dt.float32, kind="ExternalOutput").ap())
    trunk(nc, *args)
    r = _run(nc, [arrays], core_ids=[0])
    return r.results[0]["out_0_dram"]
```
